# Optimizing a Trainium2 kernel written in Bass

```python
import jax, jax.numpy as jnp
from jax import lax
import numpy as np
import math
import jax
import jax.numpy as jnp

D_MODEL = 1024
BATCH = 1
SEQ = 512
DEPTH = 1

N_META = 16
BLOCK = 128
LEAD_PAD = BLOCK - N_META
SB_HEAD_DIM = 64
SB_WIDTH = D_MODEL // 2
SB_HEADS = SB_WIDTH // SB_HEAD_DIM
HG_HEAD_DIM = 128
HG_WIDTH = D_MODEL - SB_WIDTH
HG_HEADS = HG_WIDTH // HG_HEAD_DIM
MIX_WIDTH = SB_WIDTH + HG_WIDTH
IN_SPLITS = [SB_WIDTH, SB_WIDTH, SB_WIDTH, HG_WIDTH, HG_WIDTH, HG_WIDTH, HG_WIDTH]
IN_PROJ_WIDTH = sum(IN_SPLITS)
N_GROUPS = 4
EXPERTS_PER_GROUP = 8
N_EXPERTS = N_GROUPS * EXPERTS_PER_GROUP
TOP_K_IN_GROUP = 2
EXPERT_FF = D_MODEL // 2
MOE_BLOCK = 128
EPS = 1e-6


def rmsnorm(x, gain):
    xf = x.astype(jnp.float32)
    y = xf * lax.rsqrt(jnp.mean(xf * xf, axis=-1, keepdims=True) + EPS)
    return (y * gain.astype(jnp.float32)).astype(x.dtype)

def split_heads(t, n_heads, head_dim):
    b, l, _ = t.shape
    return t.reshape(b, l, n_heads, head_dim).transpose(0, 2, 1, 3)

def merge_heads_norm(o, gain):
    b, h, l, d = o.shape
    o = rmsnorm(o.transpose(0, 2, 1, 3), gain.reshape(h, d))
    return o.reshape(b, l, h * d)

def stick_breaking_attention(q, k, v):
    L = q.shape[2]
    scale = SB_HEAD_DIM ** -0.5
    outs = []
    for blk in range(L // BLOCK):
        t0 = blk * BLOCK
        t1 = t0 + BLOCK
        z = jnp.einsum('bhtd,bhsd->bhts', q[:, :, t0:t1], k[:, :, :t1]).astype(jnp.float32) * scale
        t_pos = jnp.arange(t0, t1)[:, None]
        s_pos = jnp.arange(t1)[None, :]
        valid = (s_pos < t_pos) & (s_pos >= LEAD_PAD)
        log_beta = jax.nn.log_sigmoid(z)
        log_keep = jnp.where(valid, jax.nn.log_sigmoid(-z), 0.0)
        log_tail = lax.cumsum(log_keep, axis=3, reverse=True) - log_keep
        w = jnp.where(valid, jnp.exp(log_beta + log_tail), 0.0)
        outs.append(jnp.einsum('bhts,bhsd->bhtd', w.astype(v.dtype), v[:, :, :t1]))
    return jnp.concatenate(outs, axis=2)

def hgrn2_chunked(q, k, v, log_f):
    b, h, L, dk = q.shape
    dv = v.shape[-1]
    nc = L // BLOCK

    def to_chunks(t):
        return jnp.moveaxis(t.reshape(b, h, nc, BLOCK, t.shape[-1]), 2, 0)

    causal = jnp.tril(jnp.ones((BLOCK, BLOCK), bool))[:, :, None]

    def step(state, inp):
        qc, kc, vc, gc = inp
        bc = jnp.cumsum(gc, axis=2)
        diff = bc[:, :, :, None, :] - bc[:, :, None, :, :]
        decay = jnp.exp(jnp.where(causal, diff, -jnp.inf))
        scores = jnp.einsum('bhtd,bhsd,bhtsd->bhts', qc, kc, decay)
        o = jnp.einsum('bhts,bhsv->bhtv', scores, vc) + jnp.einsum('bhtd,bhdv->bhtv', qc * jnp.exp(bc), state)
        b_last = bc[:, :, -1, :]
        state = jnp.exp(b_last)[..., None] * state + jnp.einsum(
            'bhsd,bhsv->bhdv', kc * jnp.exp(b_last[:, :, None, :] - bc), vc)
        return state, o

    s0 = jnp.zeros((b, h, dk, dv), jnp.float32)
    _, o = lax.scan(step, s0, (to_chunks(q), to_chunks(k), to_chunks(v), to_chunks(log_f)))
    return jnp.moveaxis(o, 0, 2).reshape(b, h, L, dv)

def hierarchical_moe(x2, w_rg, b_rg, w_re, b_re, w_gate, w_up, w_down):
    n_tok = x2.shape[0]
    grp_probs = jax.nn.softmax(jnp.dot(x2, w_rg).astype(jnp.float32) + b_rg.astype(jnp.float32), axis=-1)
    grp = jnp.argmax(grp_probs, axis=-1)
    p_grp = jnp.max(grp_probs, axis=-1)
    exp_logits = (jnp.dot(x2, w_re).astype(jnp.float32) + b_re.astype(jnp.float32)).reshape(
        n_tok, N_GROUPS, EXPERTS_PER_GROUP)
    in_grp = exp_logits[jnp.arange(n_tok), grp]
    top_val, top_idx = lax.top_k(in_grp, TOP_K_IN_GROUP)
    gate = jax.nn.softmax(top_val, axis=-1) * p_grp[:, None]
    expert_id = (grp[:, None] * EXPERTS_PER_GROUP + top_idx).reshape(-1).astype(jnp.int32)
    gate_flat = gate.reshape(-1)
    token_id = jnp.repeat(jnp.arange(n_tok, dtype=jnp.int32), TOP_K_IN_GROUP)
    n_assign = n_tok * TOP_K_IN_GROUP
    n_slots = -(-n_assign // MOE_BLOCK) * MOE_BLOCK + N_EXPERTS * MOE_BLOCK
    n_blocks = n_slots // MOE_BLOCK
    counts = jnp.zeros((N_EXPERTS,), jnp.int32).at[expert_id].add(1)
    padded = (counts + MOE_BLOCK - 1) // MOE_BLOCK * MOE_BLOCK
    padded_end = jnp.cumsum(padded)
    padded_start = padded_end - padded
    start = jnp.cumsum(counts) - counts
    order = jnp.argsort(expert_id)
    sorted_e = expert_id[order]
    dest = padded_start[sorted_e] + jnp.arange(n_assign, dtype=jnp.int32) - start[sorted_e]
    slot_tok = jnp.zeros((n_slots,), jnp.int32).at[dest].set(token_id[order])
    slot_gate = jnp.zeros((n_slots,), jnp.float32).at[dest].set(gate_flat[order])
    block_e = jnp.clip(jnp.searchsorted(padded_end, jnp.arange(n_blocks, dtype=jnp.int32) * MOE_BLOCK,
                                        side='right'), 0, N_EXPERTS - 1)

    def run_block(args):
        tok, g, e = args
        xb = x2[tok]
        hb = jax.nn.silu(xb @ w_gate[e]) * (xb @ w_up[e])
        return (hb @ w_down[e]) * g[:, None].astype(x2.dtype)

    y_blocks = lax.map(run_block, (slot_tok.reshape(n_blocks, MOE_BLOCK),
                                   slot_gate.reshape(n_blocks, MOE_BLOCK), block_e))
    return jnp.zeros_like(x2).at[slot_tok].add(y_blocks.reshape(n_slots, -1))

def first_inputs(seed: int = 0) -> dict:
    key = jax.random.key(seed)
    ks = jax.random.split(key, 18)
    f32 = jnp.float32

    def nrm(k, shape, scale):
        return jax.random.normal(k, shape, f32) * scale

    return {
        'x': nrm(ks[0], (BATCH, SEQ, D_MODEL), 1.0),
        'meta_tokens': nrm(ks[1], (N_META, D_MODEL), 1.0),
        'lb_logits': nrm(ks[2], (DEPTH + 1, HG_WIDTH), 0.1).at[-1].add(2.0),
        'g_mix': 1.0 + nrm(ks[3], (DEPTH, D_MODEL), 0.02),
        'w_in': nrm(ks[4], (DEPTH, D_MODEL, IN_PROJ_WIDTH), D_MODEL ** -0.5),
        'sb_gain': 1.0 + nrm(ks[5], (DEPTH, SB_WIDTH), 0.02),
        'hg_gain': 1.0 + nrm(ks[6], (DEPTH, HG_WIDTH), 0.02),
        'w_out': nrm(ks[7], (DEPTH, MIX_WIDTH, D_MODEL), MIX_WIDTH ** -0.5),
        'g_ffn': 1.0 + nrm(ks[8], (DEPTH, D_MODEL), 0.02),
        'w_router_group': nrm(ks[9], (DEPTH, D_MODEL, N_GROUPS), D_MODEL ** -0.5),
        'b_router_group': nrm(ks[10], (DEPTH, N_GROUPS), 0.01),
        'w_router_expert': nrm(ks[11], (DEPTH, D_MODEL, N_EXPERTS), D_MODEL ** -0.5),
        'b_router_expert': nrm(ks[12], (DEPTH, N_EXPERTS), 0.01),
        'w_expert_gate': nrm(ks[13], (DEPTH, N_EXPERTS, D_MODEL, EXPERT_FF), D_MODEL ** -0.5),
        'w_expert_up': nrm(ks[14], (DEPTH, N_EXPERTS, D_MODEL, EXPERT_FF), D_MODEL ** -0.5),
        'w_expert_down': nrm(ks[15], (DEPTH, N_EXPERTS, EXPERT_FF, D_MODEL), EXPERT_FF ** -0.5),
        'g_final': 1.0 + nrm(ks[16], (D_MODEL,), 0.02),
    }

def first_block(x, meta_tokens, lb_logits, g_mix, w_in, sb_gain, hg_gain, w_out, g_ffn,
              w_router_group, b_router_group, w_router_expert, b_router_expert,
              w_expert_gate, w_expert_up, w_expert_down, g_final):
    b = x.shape[0]
    lead = jnp.zeros((b, LEAD_PAD, D_MODEL), x.dtype)
    meta = jnp.broadcast_to(meta_tokens.astype(x.dtype)[None], (b, N_META, D_MODEL))
    h = jnp.concatenate([lead, meta, x], axis=1)
    L = h.shape[1]
    real = (jnp.arange(L) >= LEAD_PAD)[None, :, None]
    lower_bounds = jnp.cumsum(jax.nn.softmax(lb_logits.astype(jnp.float32), axis=0), axis=0)
    split_idx = np.cumsum(IN_SPLITS)[:-1].tolist()

    for layer in range(DEPTH):
        a = rmsnorm(h, g_mix[layer])
        proj = jnp.einsum('bld,de->ble', a, w_in[layer])
        sb_q, sb_k, sb_v, hg_q, hg_f, hg_i, hg_g = jnp.split(proj, split_idx, axis=-1)

        o_sb = stick_breaking_attention(split_heads(sb_q, SB_HEADS, SB_HEAD_DIM),
                                        split_heads(sb_k, SB_HEADS, SB_HEAD_DIM),
                                        split_heads(sb_v, SB_HEADS, SB_HEAD_DIM))
        o_sb = merge_heads_norm(o_sb, sb_gain[layer]).astype(proj.dtype)

        lb = lower_bounds[layer]
        f_pre = hg_f.astype(jnp.float32)
        log_f = jnp.log(lb + (1.0 - lb) * jax.nn.sigmoid(f_pre))
        k_in = jnp.where(real, (1.0 - lb) * jax.nn.sigmoid(-f_pre), 0.0)
        q_in = jax.nn.silu(hg_q.astype(jnp.float32))
        o_hg = hgrn2_chunked(split_heads(q_in, HG_HEADS, HG_HEAD_DIM),
                             split_heads(k_in, HG_HEADS, HG_HEAD_DIM),
                             split_heads(hg_i.astype(jnp.float32), HG_HEADS, HG_HEAD_DIM),
                             split_heads(log_f, HG_HEADS, HG_HEAD_DIM))
        o_hg = (merge_heads_norm(o_hg, hg_gain[layer]) * jax.nn.silu(hg_g.astype(jnp.float32))).astype(proj.dtype)

        mixed = jnp.concatenate([o_sb, o_hg], axis=-1)
        h = h + jnp.einsum('ble,ed->bld', mixed, w_out[layer])

        m = rmsnorm(h[:, LEAD_PAD:], g_ffn[layer])
        n_pos = m.shape[1]
        y = hierarchical_moe(m.reshape(b * n_pos, D_MODEL), w_router_group[layer], b_router_group[layer],
                             w_router_expert[layer], b_router_expert[layer], w_expert_gate[layer],
                             w_expert_up[layer], w_expert_down[layer])
        h = h + jnp.pad(y.reshape(b, n_pos, D_MODEL), ((0, 0), (LEAD_PAD, 0), (0, 0)))

    out = rmsnorm(h[:, BLOCK:], g_final)
    return out


CHUNK = 64
CONV_CH = D_MODEL
CONV_K = 31
D_INNER = 2 * D_MODEL
HEAD_DIM = 64
N_HEADS = D_INNER // HEAD_DIM
N_GROUPS_2 = 8
HEADS_PER_GROUP = N_HEADS // N_GROUPS_2
D_STATE = 128
SSM_CONV_K = 4
XBC_CH = D_INNER + 2 * N_GROUPS_2 * D_STATE
FFN_HIDDEN = ((8 * D_MODEL // 3 + 255) // 256) * 256
RMS_EPS = 1e-6
LN_EPS = 1e-5

OFF_Z = 2 * CONV_CH
OFF_XBC = OFF_Z + D_INNER
OFF_DT = OFF_XBC + XBC_CH
OFF_GATE = OFF_DT + N_HEADS
IN_COLS = OFF_GATE + 2 * D_MODEL


def rms_norm(x, g):
    xf = x.astype(jnp.float32)
    y = xf * lax.rsqrt(jnp.mean(xf * xf, axis=-1, keepdims=True) + RMS_EPS)
    return (y * g.astype(jnp.float32)).astype(x.dtype)

def layer_norm(x, g, b):
    xf = x.astype(jnp.float32)
    mu = jnp.mean(xf, axis=-1, keepdims=True)
    xc = xf - mu
    y = xc * lax.rsqrt(jnp.mean(xc * xc, axis=-1, keepdims=True) + LN_EPS)
    return (y * g.astype(jnp.float32) + b.astype(jnp.float32)).astype(x.dtype)

def causal_depthwise_conv(u, w, b):
    k, ch = w.shape
    y = lax.conv_general_dilated(
        u, w[:, None, :], window_strides=(1,), padding=[(k - 1, 0)],
        dimension_numbers=("NWC", "WIO", "NWC"), feature_group_count=ch)
    return y + b

def conformer_conv_branch(u_glu, glu_b, dw_w, dw_b, ln_g, ln_b, pw_w, pw_b):
    u = u_glu + glu_b
    val, gt = jnp.split(u, 2, axis=-1)
    v = val * jax.nn.sigmoid(gt)
    v = causal_depthwise_conv(v, dw_w, dw_b)
    v = jax.nn.silu(layer_norm(v, ln_g, ln_b))
    return v @ pw_w + pw_b

def ssd_chunked(x, dt, a, b_mat, c_mat, d_skip):
    bsz, seqlen = x.shape[0], x.shape[1]
    nc = seqlen // CHUNK
    G, R = N_GROUPS_2, HEADS_PER_GROUP
    x = x.reshape(bsz, nc, CHUNK, G, R, HEAD_DIM)
    dt = dt.reshape(bsz, nc, CHUNK, G, R)
    b_mat = b_mat.reshape(bsz, nc, CHUNK, G, D_STATE)
    c_mat = c_mat.reshape(bsz, nc, CHUNK, G, D_STATE)
    a_dt = jnp.transpose(dt * a.reshape(G, R), (0, 3, 4, 1, 2))
    a_cs = jnp.cumsum(a_dt, axis=-1)
    xdt = x * dt[..., None]
    causal = jnp.tril(jnp.ones((CHUNK, CHUNK), dtype=bool))
    seg = a_cs[..., :, None] - a_cs[..., None, :]
    decay_in = jnp.exp(jnp.where(causal, seg, -jnp.inf))
    cb = jnp.einsum("bclgn,bcsgn->bgcls", c_mat, b_mat)
    y_diag = jnp.einsum("bgcls,bgrcls,bcsgrp->bclgrp", cb, decay_in, xdt)
    decay_to_end = jnp.exp(a_cs[..., -1:] - a_cs)
    chunk_states = jnp.einsum("bclgn,bgrcl,bclgrp->bcgrpn", b_mat, decay_to_end, xdt)
    chunk_decay = jnp.exp(a_cs[..., -1])

    def step(carry, inp):
        s_c, dec_c = inp
        return carry * dec_c[..., None, None] + s_c, carry

    init = jnp.zeros((bsz, G, R, HEAD_DIM, D_STATE), jnp.float32)
    _, prev = lax.scan(step, init, (jnp.moveaxis(chunk_states, 1, 0),
                                    jnp.moveaxis(chunk_decay, -1, 0)))
    prev = jnp.moveaxis(prev, 0, 1)
    y_off = jnp.einsum("bclgn,bcgrpn,bgrcl->bclgrp", c_mat, prev, jnp.exp(a_cs))
    y = y_diag + y_off + x * d_skip.reshape(G, R)[..., None]
    return y.reshape(bsz, seqlen, N_HEADS * HEAD_DIM)

def ssd_branch(z, xbc, dt_raw, conv_w, conv_b, dt_bias, a_log, d_skip, norm_g, out_w):
    f32 = jnp.float32
    bsz, seqlen = z.shape[0], z.shape[1]
    xbc = jax.nn.silu(causal_depthwise_conv(xbc, conv_w, conv_b))
    gn = N_GROUPS_2 * D_STATE
    xs = xbc[..., :D_INNER]
    bm = xbc[..., D_INNER:D_INNER + gn]
    cm = xbc[..., D_INNER + gn:]
    dt = jax.nn.softplus(dt_raw.astype(f32) + dt_bias.astype(f32))
    a = -jnp.exp(a_log.astype(f32))
    y = ssd_chunked(xs.astype(f32).reshape(bsz, seqlen, N_HEADS, HEAD_DIM), dt, a,
                    bm.astype(f32).reshape(bsz, seqlen, N_GROUPS_2, D_STATE),
                    cm.astype(f32).reshape(bsz, seqlen, N_GROUPS_2, D_STATE),
                    d_skip.astype(f32))
    y = y * jax.nn.silu(z.astype(f32))
    yg = y.reshape(bsz, seqlen, N_GROUPS_2, D_INNER // N_GROUPS_2)
    yg = yg * lax.rsqrt(jnp.mean(yg * yg, axis=-1, keepdims=True) + RMS_EPS)
    y = (yg.reshape(bsz, seqlen, D_INNER) * norm_g.astype(f32)).astype(z.dtype)
    return y @ out_w

def second_inputs(seed: int = 0) -> dict:
    key = jax.random.key(seed)
    ks = jax.random.split(key, 24)
    f32 = jnp.float32

    def nrm(k, shape, scale):
        return jax.random.normal(k, shape, f32) * scale

    def gain(k, n):
        return 1.0 + 0.05 * jax.random.normal(k, (DEPTH, n), f32)

    u = jax.random.uniform(ks[13], (DEPTH, N_HEADS), f32)
    dt0 = jnp.exp(u * (math.log(0.1) - math.log(1e-3)) + math.log(1e-3))
    dt_bias = dt0 + jnp.log(-jnp.expm1(-dt0))
    a_log = jnp.log(jax.random.uniform(ks[14], (DEPTH, N_HEADS), f32, 1.0, 16.0))
    return {
        "x": nrm(ks[0], (BATCH, SEQ, D_MODEL), 1.0),
        "mix_pre_g": gain(ks[1], D_MODEL),
        "w_in": nrm(ks[2], (DEPTH, D_MODEL, IN_COLS), D_MODEL ** -0.5),
        "gate_b": nrm(ks[3], (DEPTH, 2 * D_MODEL), 0.02),
        "glu_b": nrm(ks[4], (DEPTH, 2 * CONV_CH), 0.02),
        "conv_dw_w": nrm(ks[5], (DEPTH, CONV_K, CONV_CH), CONV_K ** -0.5),
        "conv_dw_b": nrm(ks[6], (DEPTH, CONV_CH), 0.02),
        "conv_ln_g": gain(ks[7], CONV_CH),
        "conv_ln_b": nrm(ks[8], (DEPTH, CONV_CH), 0.02),
        "conv_pw_w": nrm(ks[9], (DEPTH, CONV_CH, D_MODEL), CONV_CH ** -0.5),
        "conv_pw_b": nrm(ks[10], (DEPTH, D_MODEL), 0.02),
        "ssm_conv_w": nrm(ks[11], (DEPTH, SSM_CONV_K, XBC_CH), SSM_CONV_K ** -0.5),
        "ssm_conv_b": nrm(ks[12], (DEPTH, XBC_CH), 0.02),
        "dt_bias": dt_bias,
        "a_log": a_log,
        "d_skip": 1.0 + 0.1 * jax.random.normal(ks[15], (DEPTH, N_HEADS), f32),
        "ssm_norm_g": gain(ks[16], D_INNER),
        "ssm_out_w": nrm(ks[17], (DEPTH, D_INNER, D_MODEL), D_INNER ** -0.5),
        "w_out": nrm(ks[18], (DEPTH, D_MODEL, D_MODEL), D_MODEL ** -0.5),
        "mix_post_g": gain(ks[19], D_MODEL),
        "ffn_pre_g": gain(ks[20], D_MODEL),
        "w_gate_up": nrm(ks[21], (DEPTH, D_MODEL, 2 * FFN_HIDDEN), D_MODEL ** -0.5),
        "w_down": nrm(ks[22], (DEPTH, FFN_HIDDEN, D_MODEL), FFN_HIDDEN ** -0.5),
        "ffn_post_g": gain(ks[23], D_MODEL),
    }

def second_block(x, mix_pre_g, w_in, gate_b, glu_b, conv_dw_w, conv_dw_b, conv_ln_g,
              conv_ln_b, conv_pw_w, conv_pw_b, ssm_conv_w, ssm_conv_b, dt_bias, a_log,
              d_skip, ssm_norm_g, ssm_out_w, w_out, mix_post_g, ffn_pre_g, w_gate_up,
              w_down, ffn_post_g):
    for i in range(DEPTH):
        h = rms_norm(x, mix_pre_g[i])
        proj = h @ w_in[i]
        u_glu = proj[..., :OFF_Z]
        z = proj[..., OFF_Z:OFF_XBC]
        xbc = proj[..., OFF_XBC:OFF_DT]
        dt_raw = proj[..., OFF_DT:OFF_GATE]
        gates = jax.nn.sigmoid(proj[..., OFF_GATE:] + gate_b[i])
        g_conv, g_ssm = jnp.split(gates, 2, axis=-1)
        conv_out = conformer_conv_branch(u_glu, glu_b[i], conv_dw_w[i], conv_dw_b[i],
                                         conv_ln_g[i], conv_ln_b[i], conv_pw_w[i],
                                         conv_pw_b[i])
        ssm_out = ssd_branch(z, xbc, dt_raw, ssm_conv_w[i], ssm_conv_b[i], dt_bias[i],
                             a_log[i], d_skip[i], ssm_norm_g[i], ssm_out_w[i])
        mixed = (g_conv * conv_out + g_ssm * ssm_out) @ w_out[i]
        x = x + rms_norm(mixed, mix_post_g[i])
        h = rms_norm(x, ffn_pre_g[i])
        gt, up = jnp.split(h @ w_gate_up[i], 2, axis=-1)
        f = (jax.nn.silu(gt) * up) @ w_down[i]
        x = x + rms_norm(f, ffn_post_g[i])
    return x


def setup_inputs(seed=0):
    out = dict(first_inputs(seed))
    for name, value in second_inputs(seed + 1).items():
        if name != "x":
            out[name + "_2"] = value
    return out


def reference(
    x, meta_tokens, lb_logits, g_mix, w_in, sb_gain, hg_gain, w_out, g_ffn, w_router_group,
    b_router_group, w_router_expert, b_router_expert, w_expert_gate, w_expert_up, w_expert_down,
    g_final, mix_pre_g_2, w_in_2, gate_b_2, glu_b_2, conv_dw_w_2, conv_dw_b_2, conv_ln_g_2,
    conv_ln_b_2, conv_pw_w_2, conv_pw_b_2, ssm_conv_w_2, ssm_conv_b_2, dt_bias_2, a_log_2,
    d_skip_2, ssm_norm_g_2, ssm_out_w_2, w_out_2, mix_post_g_2, ffn_pre_g_2, w_gate_up_2,
    w_down_2, ffn_post_g_2,
):
    x = first_block(
        x, meta_tokens, lb_logits, g_mix, w_in, sb_gain, hg_gain, w_out, g_ffn, w_router_group,
        b_router_group, w_router_expert, b_router_expert, w_expert_gate, w_expert_up,
        w_expert_down, g_final,
    )
    return second_block(
        x, mix_pre_g_2, w_in_2, gate_b_2, glu_b_2, conv_dw_w_2, conv_dw_b_2, conv_ln_g_2,
        conv_ln_b_2, conv_pw_w_2, conv_pw_b_2, ssm_conv_w_2, ssm_conv_b_2, dt_bias_2, a_log_2,
        d_skip_2, ssm_norm_g_2, ssm_out_w_2, w_out_2, mix_post_g_2, ffn_pre_g_2, w_gate_up_2,
        w_down_2, ffn_post_g_2,
    )


_drawn_inputs = setup_inputs


def setup_inputs(seed=0):
    import zlib

    import numpy as np

    out = dict(_drawn_inputs(seed))
    spreads = {}
    factors = {'b_router_group': 2.891,
     'b_router_expert': 4.405,
     'gate_b_2': 8.0,
     'glu_b_2': 5.987,
     'conv_dw_b_2': 3.212,
     'conv_ln_b_2': 6.348,
     'conv_pw_b_2': 3.91,
     'ssm_conv_b_2': 2.851}
    for name, (base, spread) in spreads.items():
        noise = np.random.default_rng([zlib.crc32(name.encode()), seed]).standard_normal(out[name].shape)
        drawn = base * np.exp(spread * noise) if base else spread * noise
        out[name] = jnp.asarray(drawn.astype(out[name].dtype))
    for name, factor in factors.items():
        out[name] = (out[name] * factor).astype(out[name].dtype)
    return out
```

```python
from contextlib import ExitStack

import concourse.bass as bass
from concourse import mybir

ALU = mybir.AluOpType
ACT = mybir.ActivationFunctionType
AX = mybir.AxisListType
F32 = mybir.dt.float32
F32R = mybir.dt.float32r
I32 = mybir.dt.int32
U32 = mybir.dt.uint32

P = 128
T = 512
NT = T // P
D = 1024
KD = D // P
META = 16
TM = T + META
BANK = 512
UNIT = 2048
EPS = 1e-6
SB_HEADS, SB_DIM = 8, 64
HG_HEADS, HG_DIM = 4, 128
N_GROUPS, PER_GROUP, N_EXPERTS, FF = 4, 8, 32, 512
SLOTS = 128
OVER = (2 * T - 1) // SLOTS
NB = N_EXPERTS + OVER
CONV_K = 31
SSM_K = 4
SSM_GROUPS, SSM_STATE, SSM_HD, SSM_RANK = 8, 128, 64, 4
SSM_HEADS = SSM_GROUPS * SSM_RANK
D_INNER = 2 * D
OFF_Z = 2 * D
OFF_XBC = OFF_Z + D_INNER
OFF_B = OFF_XBC + D_INNER
OFF_C = OFF_B + SSM_GROUPS * SSM_STATE
OFF_DT = OFF_C + SSM_GROUPS * SSM_STATE
OFF_GATE = OFF_DT + SSM_HEADS
HIDDEN = 2816


def split_mm(nc, out, w_hi, w_lo, m_hi, m_lo, start, stop):
    nc.tensor.matmul(out, w_lo, m_hi, start=start, stop=False)
    nc.tensor.matmul(out, w_hi, m_lo, start=False, stop=False)
    return nc.tensor.matmul(out, w_hi, m_hi, start=False, stop=stop)


VEC_TILES = [
    [("lb", 8), ("sb_gain", 4), ("hg_gain", 4), ("gate_b", 16), ("glu_b", 16), ("dw_b", 8), ("ln_g", 8), ("ln_b", 8),
     ("pw_b", 8), ("ssm_b", 32), ("norm_g", 16)],
    [("dw_w_a", 128)],
    [("dw_w_b", CONV_K * 8 - 128)],
    [("ssm_w", 128)],
]
VEC_AT, VEC_ROWS = {}, []
_at = 0
for _tile in VEC_TILES:
    VEC_ROWS.append(sum(n for _, n in _tile))
    for _name, _n in _tile:
        VEC_AT[_name] = _at
        _at += _n
VEC_COLS = _at


def stage_a(nc, dram, g, sem, banks):
    h, cols, ident, ones, eps = g["h"], g["cols"], g["ident"], g["ones"], g["eps"]
    x_t = dram["x"][0].rearrange("(i p) d -> p i d", p=P)
    w_in = dram["w_in"][0].rearrange("(k p) c -> p k c", p=P)

    with ExitStack() as keep:
        def sb(name, shape, dt=F32, ctx=None):
            return (ctx or keep).enter_context(nc.sbuf_tensor(name, shape, dt))

        qT = sb("qT", [P, 4, T])
        kT = sb("kT", [P, 4, TM])
        v_nat = sb("v_nat", [P, NT + 1, 512])
        hqT = sb("hqT", [P, HG_HEADS, T])
        hfT = sb("hfT", [P, HG_HEADS, TM])
        hv_nat = sb("hv_nat", [P, NT + 1, 512])
        hg_nat = sb("hg_nat", [P, NT, 512])
        lb = sb("lb", [P, HG_HEADS])
        omlb = sb("omlb", [P, HG_HEADS])
        masks = sb("masks", [P, 8, P], I32)

        s = {n: sem("a_" + n) for n in (
            "x meta vec gbc ident ones eps hm0 ssq rt rs xn tr hi lo vtr cols lbd lb whi wlo wused out evac "
            "it xor xf up ge mask".split())}
        s_x = [sem(f"a_x{i}") for i in range(NT)]
        s_raw = [sem(f"a_raw{i}") for i in range(3)]
        with ExitStack() as tmp:
            hm = sb("hm", [P, D], ctx=tmp)
            gbc = sb("gbc", [P, D], ctx=tmp)
            sq = sb("sq_a", [P, D], ctx=tmp)
            xn = [sb(f"xn_a{i}", [P, D], ctx=tmp) for i in range(2)]
            ssq, rt, rs = (sb(n, [P, NT + 1], ctx=tmp) for n in ("ssq_a", "rt_a", "rs_a"))
            aT_hi = sb("aT_hi", [P, KD, T + P], F32R, ctx=tmp)
            aT_lo = sb("aT_lo", [P, KD, T + P], F32R, ctx=tmp)
            raw = [g["mixed"][:, 2 * i:2 * i + 2, :].rearrange("p a d -> p (a d)") for i in range(2)]
            raw.append(sb("raw_a", [P, UNIT], ctx=tmp)[:, :])
            whi = [sb(f"whi_a{i}", [P, UNIT], F32R, ctx=tmp) for i in range(2)]
            wlo = [sb(f"wlo_a{i}", [P, UNIT], F32R, ctx=tmp) for i in range(2)]
            vrow = sb("vrow", [P, len(VEC_TILES), P], ctx=tmp)
            s_i = sb("s_i", [P, P], I32, ctx=tmp)
            t_i = sb("t_i", [P, P], I32, ctx=tmp)
            x_i = sb("x_i", [P, P], I32, ctx=tmp)
            x_f = sb("x_f", [P, P], ctx=tmp)
            up_f = g["up"]
            ge_f = sq[:, :].rearrange("p (b t) -> p b t", b=8)
            lbd = sb("lbd", [P, HG_HEADS], ctx=tmp)

            groups = [("q", True), ("k", True), ("v", False), ("hq", True), ("hf", True), ("hi", False), ("hg", False)]
            units = []
            for n, (what, turned) in enumerate(groups):
                for half in range(2):
                    units.append((n, what, turned, half))
            outs, finished = [], []
            RING = 6

            def tiles_of(what):
                return [0, 1, 2, 3] if what == "hg" else [0, 1, 2, 3, 4]

            singles = 0
            for u, (n, what, turned, half) in enumerate(units):
                made = [2 * half, 2 * half + 1] if turned else tiles_of(what) if half else []
                for e in made:
                    singles += e != made[-1]
                    finished.append(("out", singles) if e != made[-1] else ("wused", u + 1))
                    outs.append((what, e))

            def is_meta_turned(what):
                return what in ("k", "hf")

            block = tmp.enter_context(nc.Block())

            @block.sync
            def _(sp):
                for i in range(NT):
                    sp.dma_start(h[:, i, :], x_t[:, i, :]).then_inc(s_x[i], 16)
                for u, (n, what, turned, half) in enumerate(units):
                    if u >= 3:
                        sp.wait_ge(s["wlo"], u - 2)
                    c = n * 512
                    if turned:
                        src = w_in[:, :, c + half * 256:c + half * 256 + 256]
                        dst = raw[u % 3].rearrange("p (k c) -> p k c", k=KD)
                    else:
                        src = w_in[:, half * 4:half * 4 + 4, c:c + 512]
                        dst = raw[u % 3].rearrange("p (k c) -> p k c", k=4)
                    sp.dma_start(dst, src).then_inc(s_raw[u % 3], 16)

            @block.gpsimd
            def _(pool):
                nc.gpsimd.memset(ident[:, :], 0.0).then_inc(s["ident"], 1)
                nc.gpsimd.memset(ones[:, :], 1.0).then_inc(s["ones"], 1)
                nc.gpsimd.memset(eps[:, 0:1], EPS)
                nc.gpsimd.memset(eps[:, 1:2], 1e-5).then_inc(s["eps"], 1)
                pool.wait_ge(s["ident"], 1)
                nc.gpsimd.affine_select(out=ident[:, :], in_=ident[:, :], compare_op=ALU.not_equal, fill=1.0, base=0,
                                        pattern=[[-1, P]], channel_multiplier=1).then_inc(s["ident"], 1)
                nc.gpsimd.iota(s_i[:, :], [[0, P]], 0, 1).then_inc(s["it"], 1)
                nc.gpsimd.iota(t_i[:, :], [[1, P]], 0, 0).then_inc(s["it"], 1)
                pool.wait_ge(s["ones"], 1)
                nc.gpsimd.affine_select(out=up_f[:, :], in_=ones[:, :], compare_op=ALU.is_gt, fill=0.0, base=0,
                                        pattern=[[1, P]], channel_multiplier=-1).then_inc(s["up"], 1)
                nc.gpsimd.affine_select(out=g["tri"][:, :], in_=ones[:, :], compare_op=ALU.is_ge, fill=0.0, base=0,
                                        pattern=[[1, P]], channel_multiplier=-1)

            @block.scalar
            def _(act):
                act.wait_ge(s["hm0"], 1)
                act.dma_start(hm[0:META, :], dram["meta_tokens"]).then_inc(s["meta"], 16)
                act.dma_start(gbc[:, :], dram["g_mix"][0].partition_broadcast(P)).then_inc(s["gbc"], 16)
                srcs = {
                    "lb": dram["lb_logits"].rearrange("l (c p) -> (l c) p", p=P),
                    "sb_gain": dram["sb_gain"].rearrange("l (c p) -> (l c) p", p=P),
                    "hg_gain": dram["hg_gain"].rearrange("l (c p) -> (l c) p", p=P),
                    "gate_b": dram["gate_b_2"].rearrange("l (c p) -> (l c) p", p=P),
                    "glu_b": dram["glu_b_2"].rearrange("l (c p) -> (l c) p", p=P),
                    "dw_b": dram["conv_dw_b_2"].rearrange("l (c p) -> (l c) p", p=P),
                    "ln_g": dram["conv_ln_g_2"].rearrange("l (c p) -> (l c) p", p=P),
                    "ln_b": dram["conv_ln_b_2"].rearrange("l (c p) -> (l c) p", p=P),
                    "pw_b": dram["conv_pw_b_2"].rearrange("l (c p) -> (l c) p", p=P),
                    "ssm_b": dram["ssm_conv_b_2"].rearrange("l (c p) -> (l c) p", p=P),
                    "norm_g": dram["ssm_norm_g_2"].rearrange("l (c p) -> (l c) p", p=P),
                    "dw_w_a": dram["conv_dw_w_2"][0].rearrange("k (c p) -> (k c) p", p=P)[0:128],
                    "dw_w_b": dram["conv_dw_w_2"][0].rearrange("k (c p) -> (k c) p", p=P)[128:CONV_K * 8],
                    "ssm_w": dram["ssm_conv_w_2"][0].rearrange("k (c p) -> (k c) p", p=P),
                }
                for t, tile in enumerate(VEC_TILES):
                    at = 0
                    for name, n in tile:
                        act.dma_start(vrow[at:at + n, t, :], srcs[name]).then_inc(s["vec"], 16)
                        at += n
                act.wait_ge(s["eps"], 1)
                for j, i in enumerate([NT, 0, 1, 2, 3]):
                    if i == NT:
                        act.wait_ge(s["meta"], 16)
                    else:
                        act.wait_ge(s_x[i], 16)
                    nc.scalar.activation(sq[:, :], hm[:, :] if i == NT else h[:, i, :], ACT.Square,
                                         accum_out=ssq[:, i:i + 1]).then_inc(s["ssq"], 1)
                    act.wait_ge(s["ssq"], j + 1)
                    nc.scalar.activation(rt[:, i:i + 1], ssq[:, i:i + 1], ACT.Sqrt, bias=eps[:, 0:1],
                                         scale=1.0 / D).then_inc(s["rt"], 1)
                for j, i in enumerate([NT, 0, 1, 2, 3]):
                    for half in range(2):
                        act.wait_ge(s["tr"], 2 * j + half + 1)
                        nc.scalar.copy(aT_hi[:, 4 * half:4 * half + 4, i * P:i * P + P],
                                       banks[6 + half][:, :].rearrange("p (k t) -> p k t", k=4)).then_inc(s["hi"], 1)
                act.wait_ge(s["lbd"], 1)
                nc.scalar.activation(lb[:, :], lbd[:, :], ACT.Sigmoid).then_inc(s["lb"], 1)
                nc.scalar.activation(omlb[:, :], lbd[:, :], ACT.Sigmoid, scale=-1.0).then_inc(s["lb"], 1)

                def make_hi(u):
                    act.wait_ge(s_raw[u % 3], 16 * (u // 3 + 1))
                    if u >= 2:
                        act.wait_ge(s["wused"], u - 1)
                    nc.scalar.copy(whi[u % 2][:, :], raw[u % 3]).then_inc(s["whi"], 1)

                def evacuate(o):
                    what, e = outs[o]
                    name, value = finished[o]
                    act.wait_ge(s[name], value)
                    b = banks[o % RING]
                    if what == "q":
                        last = nc.scalar.activation(qT[:, e, :], b[:, :], ACT.Copy, scale=SB_DIM ** -0.5)
                    elif what in ("k", "hf"):
                        dst = kT if what == "k" else hfT
                        nc.scalar.copy(dst[:, e, META:TM], b[:, :])
                        last = nc.scalar.copy(dst[:, e, 0:META], banks[6 + e % 2][:, 0:META])
                    elif what == "v":
                        last = nc.scalar.copy(v_nat[:, e, :], b[:, :])
                    elif what == "hq":
                        last = nc.scalar.activation(hqT[:, e, :], b[:, :], ACT.Silu)
                    elif what == "hi":
                        last = nc.scalar.copy(hv_nat[:, e, :], b[:, :])
                    else:
                        last = nc.scalar.activation(hg_nat[:, e, :], b[:, :], ACT.Silu)
                    last.then_inc(s["evac"], 1)

                make_hi(0)
                make_hi(1)
                o = 0
                for u, (n, what, turned, half) in enumerate(units):
                    made = 2 if turned else (len(tiles_of(what)) if half else 0)
                    for _ in range(made):
                        evacuate(o)
                        o += 1
                    if u + 2 < len(units):
                        make_hi(u + 2)

            @block.vector
            def _(dve):
                nc.vector.memset(hm[:, :], 0.0).then_inc(s["hm0"], 1)

                def make_lo(u):
                    dve.wait_ge(s["whi"], u + 1)
                    if u >= 2:
                        dve.wait_ge(s["wused"], u - 1)
                    nc.vector.tensor_tensor(wlo[u % 2][:, :], raw[u % 3], whi[u % 2][:, :].bitcast(F32),
                                            ALU.subtract).then_inc(s["wlo"], 1)

                def lower(j, i):
                    for half in range(2):
                        dve.wait_ge(s["hi"], 2 * j + half + 1)
                        nc.vector.tensor_tensor(aT_lo[:, 4 * half:4 * half + 4, i * P:i * P + P],
                                                banks[6 + half][:, :].rearrange("p (k t) -> p k t", k=4),
                                                aT_hi[:, 4 * half:4 * half + 4, i * P:i * P + P].bitcast(F32),
                                                ALU.subtract).then_inc(s["lo"], 1)

                order = [NT, 0, 1, 2, 3]
                dve.wait_ge(s["gbc"], 16)
                for j, i in enumerate(order):
                    dve.wait_ge(s["rt"], j + 1)
                    nc.vector.reciprocal(rs[:, i:i + 1], rt[:, i:i + 1]).then_inc(s["rs"], 1)
                    dve.wait_ge(s["rs"], j + 1)
                    if j >= 2:
                        dve.wait_ge(s["tr"], 2 * (j - 1))
                    nc.vector.scalar_tensor_tensor(xn[j % 2][:, :], hm[:, :] if i == NT else h[:, i, :], rs[:, i:i + 1],
                                                   gbc[:, :], ALU.mult, ALU.mult).then_inc(s["xn"], 1)
                    if j >= 1:
                        lower(j - 1, order[j - 1])
                lower(4, order[4])
                dve.wait_ge(s["vtr"], 1)
                first = sum(VEC_ROWS[:3])
                nc.vector.tensor_copy(cols[:, 0:first], banks[0][:, 0:first])
                nc.vector.tensor_copy(cols[:, first:VEC_COLS], banks[1][:, 0:VEC_ROWS[3]]).then_inc(s["cols"], 1)
                dve.wait_ge(s["cols"], 1)
                a = VEC_AT["lb"]
                nc.vector.tensor_tensor(lbd[:, :], cols[:, a:a + 4], cols[:, a + 4:a + 8],
                                        ALU.subtract).then_inc(s["lbd"], 1)
                make_lo(0)
                make_lo(1)
                dve.wait_ge(s["it"], 2)
                nc.vector.tensor_tensor(x_i[:, :], s_i[:, :], t_i[:, :], ALU.bitwise_xor).then_inc(s["xor"], 1)
                dve.wait_ge(s["xor"], 1)
                nc.vector.tensor_copy(x_f[:, :], x_i[:, :]).then_inc(s["xf"], 1)
                dve.wait_ge(s["xf"], 1)
                dve.wait_ge(s["up"], 1)
                for b in range(8):
                    nc.vector.scalar_tensor_tensor(ge_f[:, b, :], x_f[:, :], float(1 << b), up_f[:, :], ALU.is_ge,
                                                   ALU.mult).then_inc(s["ge"], 1)
                dve.wait_ge(s["ge"], 8)
                for b in range(7):
                    nc.vector.tensor_tensor(masks[:, b, :], ge_f[:, b, :], ge_f[:, b + 1, :], ALU.subtract)
                dve.wait_ge(s["ident"], 2)
                nc.vector.tensor_copy(masks[:, 7, :], ident[:, :]).then_inc(s["mask"], 1)
                for u in range(2, len(units)):
                    make_lo(u)

            @block.tensor
            def _(pe):
                pe.wait_ge(s["ident"], 2)
                for j, i in enumerate([NT, 0, 1, 2, 3]):
                    pe.wait_ge(s["xn"], j + 1)
                    for half in range(2):
                        if j >= 1:
                            pe.wait_ge(s["lo"], 2 * (j - 1) + half + 1)
                        for k in range(4):
                            last = nc.tensor.transpose(banks[6 + half][:, k * P:k * P + P],
                                                       xn[j % 2][:, (4 * half + k) * P:(4 * half + k + 1) * P], ident[:, :])
                        last.then_inc(s["tr"], 1)
                pe.wait_ge(s["vec"], 16 * sum(len(t) for t in VEC_TILES))
                at = 0
                for t, n in enumerate(VEC_ROWS):
                    dst = banks[0][:, at:at + n] if t < 3 else banks[1][:, 0:n]
                    last = nc.tensor.transpose(dst, vrow[0:n, t, :], ident[0:n, 0:n])
                    at += n
                last.then_inc(s["vtr"], 1)
                pe.wait_ge(s["cols"], 1)
                pe.wait_ge(s["lo"], 10)
                o = 0
                for u, (n, what, turned, half) in enumerate(units):
                    pe.wait_ge(s["wlo"], u + 1)
                    wh, wl = whi[u % 2], wlo[u % 2]
                    if turned:
                        wh = wh[:, :].rearrange("p (k c) -> p k c", k=KD)
                        wl = wl[:, :].rearrange("p (k c) -> p k c", k=KD)
                        for e in range(2):
                            if o >= RING:
                                pe.wait_ge(s["evac"], o - RING + 1)
                            if is_meta_turned(what):
                                if o >= 2:
                                    pe.wait_ge(s["evac"], o - 1)
                            b, bm = banks[o % RING], banks[6 + e]
                            for k in range(KD):
                                a_hi, a_lo = aT_hi[:, k, 0:T], aT_lo[:, k, 0:T]
                                m_hi, m_lo = aT_hi[:, k, T:T + META], aT_lo[:, k, T:T + META]
                                w_h, w_l = wh[:, k, e * P:e * P + P], wl[:, k, e * P:e * P + P]
                                st, sp_ = k == 0, k == KD - 1
                                nc.tensor.matmul(b[:, :], w_l, a_hi, start=st, stop=False)
                                if is_meta_turned(what):
                                    nc.tensor.matmul(bm[:, 0:META], w_l, m_hi, start=st, stop=False)
                                    nc.tensor.matmul(bm[:, 0:META], w_h, m_lo, start=False, stop=False)
                                    nc.tensor.matmul(bm[:, 0:META], w_h, m_hi, start=False, stop=sp_)
                                nc.tensor.matmul(b[:, :], w_h, a_lo, start=False, stop=False)
                                last = nc.tensor.matmul(b[:, :], w_h, a_hi, start=False, stop=sp_)
                            last.then_inc(s["out" if e == 0 else "wused"], 1)
                            o += 1
                    else:
                        wh = wh[:, :].rearrange("p (k c) -> p k c", k=4)
                        wl = wl[:, :].rearrange("p (k c) -> p k c", k=4)
                        for j in tiles_of(what):
                            if half == 0 and o + j >= RING:
                                pe.wait_ge(s["evac"], o + j - RING + 1)
                            for k in range(4):
                                kk = 4 * half + k
                                last = split_mm(nc, banks[(o + j) % RING][:, :], aT_hi[:, kk, j * P:j * P + P],
                                                aT_lo[:, kk, j * P:j * P + P], wh[:, k, :], wl[:, k, :],
                                                kk == 0, kk == KD - 1)
                            if j == tiles_of(what)[-1]:
                                last.then_inc(s["wused"], 1)
                            elif half:
                                last.then_inc(s["out"], 1)
                        if half:
                            o += len(tiles_of(what))

        g["clear"](s, s_x, s_raw)

        mixed = g["mixed"]
        steps = [(i, hd) for i in range(NT) for hd in range(SB_HEADS)]
        NSTEP = len(steps)
        pall = g["pall"]
        s = {n: sem("b_" + n) for n in (
            "z ab u sp_l sp spm scan lw w wm tr ev evm o oev osq ossq ort ors on ones".split())}
        with ExitStack() as tmp:
            ab, uu, ll, sp_, cc, lw, ww = ([sb(f"{n}{i}", [P, TM], ctx=tmp) for i in range(2)]
                                           for n in ("ab", "uu", "ll", "sp", "cc", "lw", "ww"))
            wT = [sb(f"wT{i}", [P, NT, P], ctx=tmp) for i in range(2)]
            wTm = [sb(f"wTm{i}", [META, P], ctx=tmp) for i in range(2)]
            one_row = sb("one_row", [P, TM], ctx=tmp)
            o_sb = sb("o_sb", [P, NT, 512], ctx=tmp)
            osq = sb("osq", [P, 512], ctx=tmp)
            ossq, ort, ors = (sb(n, [P, NT, SB_HEADS], ctx=tmp) for n in ("ossq", "ort", "ors"))

            def width(n):
                return META + P * (steps[n][0] + 1)

            def z_of(n):
                b = 2 * (n % 2)
                return pall[:, b:b + 2, :].rearrange("p b n -> p (b n)")[:, 0:width(n)]

            def o_of(n):
                return pall[:, 6 + n % 2, 0:SB_DIM]

            block = tmp.enter_context(nc.Block())

            @block.tensor
            def _(pe):
                def scores(n):
                    i, hd = steps[n]
                    if n >= 2:
                        pe.wait_ge(s["lw"], n - 1)
                    q = qT[64 * (hd % 2):64 * (hd % 2) + 64, hd // 2, i * P:i * P + P]
                    k = kT[64 * (hd % 2):64 * (hd % 2) + 64, hd // 2, :]
                    w = width(n)
                    b = 2 * (n % 2)
                    last = nc.tensor.matmul(pall[:, b, 0:min(w, BANK)], q, k[:, 0:min(w, BANK)], start=True, stop=True)
                    if w > BANK:
                        last = nc.tensor.matmul(pall[:, b + 1, 0:w - BANK], q, k[:, BANK:w], start=True, stop=True)
                    last.then_inc(s["z"], 1)

                def turn(n):
                    i, hd = steps[n]
                    pe.wait_ge(s["wm"], n + 1)
                    if n >= 1:
                        pe.wait_ge(s["ev"], n)
                        pe.wait_ge(s["evm"], n)
                    w = ww[n % 2]
                    nc.tensor.transpose(pall[0:META, 5, 0:P], w[:, 0:META], ident[:, :])
                    for c in range(i + 1):
                        last = nc.tensor.transpose(pall[:, 4, c * P:c * P + P], w[:, META + c * P:META + c * P + P], ident[:, :])
                    last.then_inc(s["tr"], 1)

                def values(n):
                    i, hd = steps[n]
                    pe.wait_ge(s["ev"], n + 1)
                    pe.wait_ge(s["evm"], n + 1)
                    if n >= 2:
                        pe.wait_ge(s["oev"], n - 1)
                    vc = slice(hd * SB_DIM, hd * SB_DIM + SB_DIM)
                    nc.tensor.matmul(o_of(n), wTm[n % 2][:, :], v_nat[0:META, NT, vc], start=True, stop=False)
                    for c in range(i + 1):
                        last = nc.tensor.matmul(o_of(n), wT[n % 2][:, c, :], v_nat[:, c, vc], start=False, stop=c == i)
                    last.then_inc(s["o"], 1)

                for n in range(NSTEP + 3):
                    if n < NSTEP:
                        scores(n)
                    if 2 <= n < NSTEP + 2:
                        turn(n - 2)
                    if n >= 3:
                        values(n - 3)

            @block.scalar
            def _(act):
                def front(n):
                    w = width(n)
                    act.wait_ge(s["z"], n + 1)
                    nc.scalar.activation(ab[n % 2][:, 0:w], z_of(n), ACT.Abs).then_inc(s["ab"], 1)
                    act.wait_ge(s["ab"], n + 1)
                    nc.scalar.activation(uu[n % 2][:, 0:w], ab[n % 2][:, 0:w], ACT.Exp, scale=-1.0).then_inc(s["u"], 1)
                    act.wait_ge(s["u"], n + 1)
                    if n >= 2:
                        act.wait_ge(s["sp"], n - 1)
                    nc.scalar.activation(ll[n % 2][:, 0:w], uu[n % 2][:, 0:w], ACT.Ln, bias=1.0).then_inc(s["sp_l"], 1)

                def weights(n):
                    w = width(n)
                    act.wait_ge(s["lw"], n + 1)
                    if n >= 2:
                        act.wait_ge(s["tr"], n - 1)
                    nc.scalar.activation(ww[n % 2][:, 0:w], lw[n % 2][:, 0:w], ACT.Exp).then_inc(s["w"], 1)

                def evacuate(n):
                    i, hd = steps[n]
                    act.wait_ge(s["tr"], n + 1)
                    if n >= 2:
                        act.wait_ge(s["o"], n - 1)
                    nc.scalar.copy(wT[n % 2][:, 0:i + 1, :],
                                   pall[:, 4, 0:(i + 1) * P].rearrange("p (c t) -> p c t", c=i + 1)).then_inc(s["ev"], 1)

                nc.scalar.preload_act_table_set("natural_log_exp_and_others")
                for n in range(NSTEP + 2):
                    if n < NSTEP:
                        front(n)
                    if 1 <= n < NSTEP + 1:
                        weights(n - 1)
                    if n >= 2:
                        evacuate(n - 2)
                for i in range(NT):
                    act.wait_ge(s["ossq"], i + 1)
                    nc.scalar.activation(ort[:, i, :], ossq[:, i, :], ACT.Sqrt, bias=eps[:, 0:1],
                                         scale=1.0 / SB_DIM).then_inc(s["ort"], 1)

            @block.gpsimd
            def _(pool):
                def mask_keep(n):
                    w = width(n)
                    pool.wait_ge(s["sp"], n + 1)
                    d = sp_[n % 2][:, w - P:w]
                    nc.gpsimd.affine_select(out=d, in_=d, compare_op=ALU.is_gt, fill=0.0, base=0, pattern=[[-1, P]],
                                            channel_multiplier=1).then_inc(s["spm"], 1)

                def mask_weights(n):
                    w = width(n)
                    pool.wait_ge(s["w"], n + 1)
                    d = ww[n % 2][:, w - P:w]
                    nc.gpsimd.affine_select(out=d, in_=d, compare_op=ALU.is_gt, fill=0.0, base=0, pattern=[[-1, P]],
                                            channel_multiplier=1).then_inc(s["wm"], 1)

                for n in range(NSTEP + 1):
                    if n < NSTEP:
                        mask_keep(n)
                    if n >= 1:
                        mask_weights(n - 1)

            @block.vector
            def _(dve):
                nc.vector.memset(one_row[:, :], 1.0).then_inc(s["ones"], 1)
                dve.wait_ge(s["ones"], 1)

                def softplus(n):
                    w = width(n)
                    dve.wait_ge(s["sp_l"], n + 1)
                    if n >= 2:
                        dve.wait_ge(s["scan"], n - 1)
                    nc.vector.scalar_tensor_tensor(sp_[n % 2][:, 0:w], z_of(n), 0.0, ll[n % 2][:, 0:w], ALU.max,
                                                   ALU.add).then_inc(s["sp"], 1)

                def log_weights(n):
                    w = width(n)
                    dve.wait_ge(s["spm"], n + 1)
                    nc.vector.tensor_tensor_scan(cc[n % 2][:, 0:w][:, ::-1], one_row[:, 0:w], sp_[n % 2][:, 0:w][:, ::-1],
                                                 0.0, ALU.mult, ALU.add).then_inc(s["scan"], 1)
                    dve.wait_ge(s["scan"], n + 1)
                    if n >= 2:
                        dve.wait_ge(s["w"], n - 1)
                    nc.vector.tensor_tensor(lw[n % 2][:, 0:w], z_of(n), cc[n % 2][:, 0:w],
                                            ALU.subtract).then_inc(s["lw"], 1)

                def meta_evacuate(n):
                    dve.wait_ge(s["tr"], n + 1)
                    if n >= 2:
                        dve.wait_ge(s["o"], n - 1)
                    nc.vector.tensor_copy(wTm[n % 2][:, :], pall[0:META, 5, 0:P]).then_inc(s["evm"], 1)

                def out_evacuate(n):
                    i, hd = steps[n]
                    dve.wait_ge(s["o"], n + 1)
                    nc.vector.tensor_copy(o_sb[:, i, hd * SB_DIM:hd * SB_DIM + SB_DIM], o_of(n)).then_inc(s["oev"], 1)

                def square(i):
                    dve.wait_ge(s["oev"], SB_HEADS * (i + 1))
                    nc.vector.tensor_tensor(osq[:, :], o_sb[:, i, :], o_sb[:, i, :], ALU.mult).then_inc(s["osq"], 1)
                    dve.wait_ge(s["osq"], i + 1)
                    nc.vector.tensor_reduce(ossq[:, i, :], osq[:, :].rearrange("p (h d) -> p h d", h=SB_HEADS), AX.X,
                                            ALU.add).then_inc(s["ossq"], 1)

                for n in range(NSTEP + 4):
                    if n < NSTEP:
                        softplus(n)
                    if 1 <= n < NSTEP + 1:
                        log_weights(n - 1)
                    if 2 <= n < NSTEP + 2:
                        meta_evacuate(n - 2)
                    if 4 <= n:
                        out_evacuate(n - 4)
                        if (n - 4) % SB_HEADS == SB_HEADS - 1:
                            square((n - 4) // SB_HEADS)
                for i in range(NT):
                    dve.wait_ge(s["ort"], i + 1)
                    nc.vector.reciprocal(ors[:, i, :], ort[:, i, :]).then_inc(s["ors"], 1)
                    dve.wait_ge(s["ors"], i + 1)
                    nc.vector.tensor_tensor(mixed[:, i, 0:512].rearrange("p (h d) -> p h d", h=SB_HEADS),
                                            o_sb[:, i, :].rearrange("p (h d) -> p h d", h=SB_HEADS),
                                            ors[:, i, :].unsqueeze(2).to_broadcast([P, SB_HEADS, SB_DIM]),
                                            ALU.mult).then_inc(s["on"], 1)

        g["clear"](s)

        s = {n: sem("c_" + n) for n in (
            "sig rst lf k bx q0 d e qz kz sc s0 s_ acc be qe kd kdt kdn st stp os ssq rt rs on og".split())}
        HC = HG_HEADS * T
        with ExitStack() as tmp:
            sgm = kT
            sgn = sb("sgn", [P, HG_HEADS, TM], ctx=tmp)
            lf = hfT
            kx = qT
            km = sb("km", [P, HG_HEADS, META], ctx=tmp)
            bx = sb("bx", [P, HC], ctx=tmp)
            bm = sb("bm", [P, HG_HEADS, META], ctx=tmp)
            rst = sb("rst", [P, T], ctx=tmp)
            dd = [sb(f"dd{i}", [P, HC], ctx=tmp) for i in range(2)]
            ee = [sb(f"ee{i}", [P, HC], ctx=tmp) for i in range(2)]
            qz = [sb(f"qz{i}", [P, HC], ctx=tmp) for i in range(2)]
            kz = [sb(f"kz{i}", [P, HC], ctx=tmp) for i in range(2)]
            acc = v_nat[:, 0:NT, :]
            dm = sb("dm", [P, HG_HEADS, META], ctx=tmp)
            em = sb("em", [P, HG_HEADS, META], ctx=tmp)
            kdm = sb("kdm", [P, HG_HEADS, META], ctx=tmp)
            kdn = sb("kdn", [P, 3, HG_HEADS, P], ctx=tmp)
            kdnm = sb("kdnm", [META, HG_HEADS, P], ctx=tmp)
            st = sb("st", [P, NT, HG_HEADS, P], ctx=tmp)
            elast = sb("elast", [P, HG_HEADS * NT], ctx=tmp)
            sqo = sb("sqo", [P, 512], ctx=tmp)
            on = sb("on", [P, 512], ctx=tmp)
            ssq, rt, rs = (sb(n, [P, NT, HG_HEADS], ctx=tmp) for n in ("ssq_c", "rt_c", "rs_c"))
            q_in = hqT[:, :, :].rearrange("p e t -> p (e t)")
            k_in = kx[:, :, :].rearrange("p e t -> p (e t)")
            LEVELS = 7

            def halves(t, lv):
                return t.rearrange("p (n two w) -> p n two w", two=2, w=64 >> lv)

            block = tmp.enter_context(nc.Block())

            @block.scalar
            def _(act):
                nc.scalar.activation(sgm[:, :, :], hfT[:, :, :], ACT.Sigmoid).then_inc(s["sig"], 1)
                nc.scalar.activation(sgn[:, :, :], hfT[:, :, :], ACT.Sigmoid, scale=-1.0).then_inc(s["sig"], 1)
                act.wait_ge(s["sig"], 2)
                for e in range(HG_HEADS):
                    nc.scalar.activation(lf[:, e, :], sgm[:, e, :], ACT.Ln, bias=lb[:, e:e + 1],
                                         scale=omlb[:, e:e + 1]).then_inc(s["lf"], 1)
                for lv in range(LEVELS):
                    act.wait_ge(s["d"], lv + 1)
                    if lv >= 2:
                        act.wait_ge(s["kz"], lv - 1)
                        act.wait_ge(s["qz"], lv - 1)
                    nc.scalar.activation(ee[lv % 2][:, :], dd[lv % 2][:, :], ACT.Exp).then_inc(s["e"], 1)
                act.wait_ge(s["kz"], LEVELS)
                act.wait_ge(s["qz"], LEVELS)
                nc.scalar.activation(ee[1][:, :], bx[:, :], ACT.Exp).then_inc(s["be"], 1)
                act.wait_ge(s["d"], LEVELS + 1)
                nc.scalar.activation(ee[0][:, :], dd[1][:, :], ACT.Exp).then_inc(s["be"], 1)
                nc.scalar.activation(em[:, :, :], dm[:, :, :], ACT.Exp).then_inc(s["be"], 1)
                nc.scalar.activation(elast[:, :], bx[:, :].rearrange("p (n w) -> p n w", w=P)[:, :, P - 1],
                                     ACT.Exp).then_inc(s["be"], 1)
                act.wait_ge(s["kdt"], 1)
                nc.scalar.copy(kdnm[:, :, :], pall[0:META, 0, :].rearrange("p (e d) -> p e d", e=HG_HEADS)).then_inc(s["kdn"], 1)
                for c in range(3):
                    act.wait_ge(s["kdt"], c + 2)
                    nc.scalar.copy(kdn[:, c, :, :], pall[:, 1 + c, :].rearrange("p (e d) -> p e d", e=HG_HEADS)).then_inc(s["kdn"], 1)
                for c in range(NT):
                    act.wait_ge(s["ssq"], c + 1)
                    nc.scalar.activation(rt[:, c, :], ssq[:, c, :], ACT.Sqrt, bias=eps[:, 0:1],
                                         scale=1.0 / HG_DIM).then_inc(s["rt"], 1)

            @block.vector
            def _(dve):
                nc.vector.memset(rst[:, :], 1.0).then_inc(s["rst"], 1)
                dve.wait_ge(s["rst"], 1)
                nc.vector.memset(rst[:, 0:T:P], 0.0).then_inc(s["rst"], 1)
                nc.vector.memset(acc, 0.0).then_inc(s["s_"], 1)
                for i in range(2):
                    nc.vector.memset(qz[i][:, :], 0.0).then_inc(s["s_"], 1)
                    nc.vector.memset(kz[i][:, :], 0.0).then_inc(s["s_"], 1)
                dve.wait_ge(s["sig"], 2)
                for e in range(HG_HEADS):
                    nc.vector.tensor_scalar(km[:, e, :], sgn[:, e, 0:META], omlb[:, e:e + 1], None, ALU.mult)
                    nc.vector.tensor_scalar(kx[:, e, :], sgn[:, e, META:TM], omlb[:, e:e + 1], None,
                                            ALU.mult).then_inc(s["k"], 1)
                dve.wait_ge(s["rst"], 2)
                for e in range(HG_HEADS):
                    dve.wait_ge(s["lf"], e + 1)
                    nc.vector.tensor_tensor_scan(bm[:, e, :], ones[:, 0:META], lf[:, e, 0:META], 0.0, ALU.mult, ALU.add)
                    nc.vector.tensor_tensor_scan(bx[:, e * T:e * T + T], rst[:, :], lf[:, e, META:TM], 0.0, ALU.mult,
                                                 ALU.add).then_inc(s["bx"], 1)
                dve.wait_ge(s["bx"], HG_HEADS)
                dve.wait_ge(s["k"], HG_HEADS)
                dve.wait_ge(s["s_"], 5)

                def exponents(lv):
                    if lv >= 2:
                        dve.wait_ge(s["e"], lv - 1)
                    w = 64 >> lv
                    b, d = halves(bx[:, :], lv), halves(dd[lv % 2][:, :], lv)
                    ref = b[:, :, 0, w - 1:w].to_broadcast([P, HC // (2 * w), w])
                    nc.vector.tensor_tensor(d[:, :, 0, :], ref, b[:, :, 0, :], ALU.subtract)
                    nc.vector.tensor_tensor(d[:, :, 1, :], b[:, :, 1, :], ref, ALU.subtract).then_inc(s["d"], 1)

                def query_factors(lv):
                    dve.wait_ge(s["e"], lv + 1)
                    if lv >= 2:
                        dve.wait_ge(s["sc"], HG_HEADS * (lv - 1))
                    nc.vector.tensor_tensor(halves(qz[lv % 2][:, :], lv)[:, :, 1, :], halves(q_in, lv)[:, :, 1, :],
                                            halves(ee[lv % 2][:, :], lv)[:, :, 1, :], ALU.mult).then_inc(s["qz"], 1)

                def select(n):
                    lv, e = divmod(n, HG_HEADS)
                    dve.wait_ge(s["sc"], n + 1)
                    if n >= HG_HEADS:
                        dve.wait_ge(s["acc"], n - HG_HEADS + 1)
                    nc.vector.copy_predicated(acc[:, e, :].rearrange("p (c t) -> p c t", c=NT),
                                              masks[:, (6 - lv) if lv < 7 else 7, :].unsqueeze(1).to_broadcast([P, NT, P]),
                                              pall[:, n % 8, :].rearrange("p (c t) -> p c t", c=NT)).then_inc(s["acc"], 1)

                exponents(0)
                exponents(1)
                for lv in range(LEVELS):
                    query_factors(lv)
                    if lv + 2 < LEVELS:
                        exponents(lv + 2)
                    if lv >= 1:
                        for e in range(HG_HEADS):
                            select(HG_HEADS * (lv - 1) + e)
                dve.wait_ge(s["e"], LEVELS)
                bc = bx[:, :].rearrange("p (n w) -> p n w", w=P)
                nc.vector.tensor_tensor(dm[:, :, :], bm[:, :, META - 1:META].to_broadcast([P, HG_HEADS, META]), bm[:, :, :],
                                        ALU.subtract)
                nc.vector.tensor_tensor(dd[1][:, :].rearrange("p (n w) -> p n w", w=P),
                                        bc[:, :, P - 1:P].to_broadcast([P, HC // P, P]), bc,
                                        ALU.subtract).then_inc(s["d"], 1)
                for n in range(HG_HEADS * 6, HG_HEADS * 8):
                    select(n)
                dve.wait_ge(s["be"], 4)
                nc.vector.tensor_tensor(qz[0][:, :], q_in, ee[1][:, :], ALU.mult).then_inc(s["qe"], 1)
                nc.vector.tensor_tensor(kdm[:, :, :], km[:, :, :], em[:, :, :], ALU.mult).then_inc(s["kd"], 1)
                nc.vector.tensor_tensor(kz[0][:, :], k_in, ee[0][:, :], ALU.mult).then_inc(s["kd"], 1)
                for c in range(NT):
                    dve.wait_ge(s["stp"], c + 1)
                    b = pall[:, 4 + c % 2, :].rearrange("p (e d) -> p e d", e=HG_HEADS)
                    if c == 0:
                        nc.vector.tensor_copy(st[:, 0, :, :], b).then_inc(s["st"], 1)
                    else:
                        dve.wait_ge(s["st"], c)
                        for e in range(HG_HEADS):
                            last = nc.vector.scalar_tensor_tensor(
                                st[:, c, e, :], st[:, c - 1, e, :], elast[:, e * NT + c - 1:e * NT + c], b[:, e, :], ALU.mult, ALU.add)
                        last.then_inc(s["st"], 1)
                for c in range(NT):
                    dve.wait_ge(s["os"], c + 1)
                    o = pall[:, 6 + c % 2, :]
                    if c >= 1:
                        dve.wait_ge(s["og"], c)
                    nc.vector.tensor_copy(on[:, :], o).then_inc(s["on"], 1)
                    dve.wait_ge(s["on"], 2 * c + 1)
                    nc.vector.tensor_tensor(sqo[:, :], on[:, :], on[:, :], ALU.mult).then_inc(s["s0"], 1)
                    dve.wait_ge(s["s0"], c + 1)
                    nc.vector.tensor_reduce(ssq[:, c, :], sqo[:, :].rearrange("p (e d) -> p e d", e=HG_HEADS), AX.X,
                                            ALU.add).then_inc(s["ssq"], 1)
                    dve.wait_ge(s["rt"], c + 1)
                    nc.vector.reciprocal(rs[:, c, :], rt[:, c, :]).then_inc(s["rs"], 1)
                    dve.wait_ge(s["rs"], c + 1)
                    nc.vector.tensor_tensor(on[:, :].rearrange("p (e d) -> p e d", e=HG_HEADS),
                                            on[:, :].rearrange("p (e d) -> p e d", e=HG_HEADS),
                                            rs[:, c, :].unsqueeze(2).to_broadcast([P, HG_HEADS, P]), ALU.mult).then_inc(s["on"], 1)
                    dve.wait_ge(s["on"], 2 * c + 2)
                    nc.vector.tensor_tensor(mixed[:, c, 512:D], on[:, :], hg_nat[:, c, :], ALU.mult).then_inc(s["og"], 1)

            @block.gpsimd
            def _(pool):
                pool.wait_ge(s["k"], HG_HEADS)
                pool.wait_ge(s["s_"], 5)
                for lv in range(LEVELS):
                    pool.wait_ge(s["e"], lv + 1)
                    if lv >= 2:
                        pool.wait_ge(s["sc"], HG_HEADS * (lv - 1))
                    nc.gpsimd.tensor_tensor(halves(kz[lv % 2][:, :], lv)[:, :, 0, :], halves(k_in, lv)[:, :, 0, :],
                                            halves(ee[lv % 2][:, :], lv)[:, :, 0, :], ALU.mult).then_inc(s["kz"], 1)

            @block.tensor
            def _(pe):
                def products(n):
                    lv, e = divmod(n, HG_HEADS)
                    if lv < LEVELS:
                        pe.wait_ge(s["qz"], lv + 1)
                        pe.wait_ge(s["kz"], lv + 1)
                    ks, qs = (kz[lv % 2][:, :], qz[lv % 2][:, :]) if lv < LEVELS else (k_in, q_in)
                    if n >= 8:
                        pe.wait_ge(s["acc"], n - 7)
                    for c in range(NT):
                        a = e * T + c * P
                        last = nc.tensor.matmul(pall[:, n % 8, c * P:c * P + P], ks[:, a:a + P], qs[:, a:a + P],
                                                start=True, stop=True)
                    last.then_inc(s["sc"], 1)

                pe.wait_ge(s["k"], HG_HEADS)
                for n in range(HG_HEADS * (LEVELS + 1)):
                    products(n)
                pe.wait_ge(s["acc"], HG_HEADS * (LEVELS + 1))
                pe.wait_ge(s["kd"], 1)
                for e in range(HG_HEADS):
                    last = nc.tensor.transpose(pall[0:META, 0, e * P:e * P + P], kdm[:, e, :], ident[:, :])
                last.then_inc(s["kdt"], 1)
                pe.wait_ge(s["kd"], 2)
                for c in range(3):
                    for e in range(HG_HEADS):
                        last = nc.tensor.transpose(pall[:, 1 + c, e * P:e * P + P], kz[0][:, e * T + c * P:e * T + c * P + P],
                                                   ident[:, :])
                    last.then_inc(s["kdt"], 1)
                for c in range(NT):
                    pe.wait_ge(s["kdn"], c + 1)
                    if c >= 2:
                        pe.wait_ge(s["st"], c - 1)
                    for e in range(HG_HEADS):
                        lhs = kdnm[:, e, :] if c == 0 else kdn[:, c - 1, e, :]
                        rhs = hv_nat[0:META, NT, e * P:e * P + P] if c == 0 else hv_nat[:, c - 1, e * P:e * P + P]
                        last = nc.tensor.matmul(pall[:, 4 + c % 2, e * P:e * P + P], lhs, rhs, start=True, stop=True)
                    last.then_inc(s["stp"], 1)
                pe.wait_ge(s["qe"], 1)
                for c in range(NT):
                    pe.wait_ge(s["st"], c + 1)
                    if c >= 2:
                        pe.wait_ge(s["on"], 2 * (c - 2) + 1)
                    for e in range(HG_HEADS):
                        o = pall[:, 6 + c % 2, e * P:e * P + P]
                        a = e * T + c * P
                        nc.tensor.matmul(o, acc[:, e, c * P:c * P + P], hv_nat[:, c, e * P:e * P + P], start=True, stop=False)
                        last = nc.tensor.matmul(o, qz[0][:, a:a + P], st[:, c, e, :], start=False, stop=True)
                    last.then_inc(s["os"], 1)
        g["clear"](s)


BIG = 60000.0


def stage_b(nc, dram, g, sem, banks):
    h, cols, ident, ones, eps, mixed, pall = (g[k] for k in "h cols ident ones eps mixed pall".split())
    w_out = dram["w_out"][0].rearrange("(k p) c -> p k c", p=P)
    m_rows, y_rows = g["m_rows"], g["y_rows"]
    NR = N_GROUPS + N_EXPERTS

    s = {n: sem("d_" + n) for n in (
        "gbc wr rb wrh wrl tr hi lo whi wlo wused out res ssq rt rs xn mtr mhi mlo log io lg mx mi pe gs v "
        "tab pfx tabf iod".split())}
    s_raw = [sem(f"d_raw{i}") for i in range(3)]
    s_mrow = [sem(f"d_mrow{i}") for i in range(2)]
    with ExitStack() as tmp:
        def sb(name, shape, dt=F32):
            return tmp.enter_context(nc.sbuf_tensor(name, shape, dt))

        gbc = sb("gbc_d", [P, D])
        mixT_hi, mixT_lo = sb("mixT_hi", [P, KD, T], F32R), sb("mixT_lo", [P, KD, T], F32R)
        raw = [sb(f"raw_d{i}", [P, UNIT]) for i in range(3)]
        whi = [sb(f"whi_d{i}", [P, UNIT], F32R) for i in range(2)]
        wlo = [sb(f"wlo_d{i}", [P, UNIT], F32R) for i in range(2)]
        wr = sb("wr", [P, KD, NR])
        wr_hi, wr_lo = sb("wr_hi", [P, KD, NR], F32R), sb("wr_lo", [P, KD, NR], F32R)
        rb = sb("rb", [P, NR])
        sq = sb("sq_d", [P, D])
        xn = [sb(f"xn_d{i}", [P, D]) for i in range(2)]
        ssq, rt, rs = (sb(n, [P, NT]) for n in ("ssq_d", "rt_d", "rs_d"))
        mT_hi = [sb(f"mT_hi{i}", [P, KD, P], F32R) for i in range(2)]
        mT_lo = [sb(f"mT_lo{i}", [P, KD, P], F32R) for i in range(2)]
        lg = sb("lg", [P, NT, NR])
        gpad = sb("gpad", [P, NT, 8])
        gm, tv = sb("gm", [P, NT, 8]), sb("tv", [P, NT, 8])
        gi, ti = sb("gi", [P, NT, 8], U32), sb("ti", [P, NT, 8], U32)
        ngm, gsum, pg = sb("ngm", [P, NT]), sb("gsum", [P, NT]), sb("pg", [P, NT])
        gex = sb("gex", [P, NT, N_GROUPS])
        gidx = sb("gidx", [P, NT])
        oh4 = sb("oh4", [P, NT, N_GROUPS])
        pick = sb("pick", [P, NT, N_GROUPS, PER_GROUP])
        ing = sb("ing", [P, NT, PER_GROUP])
        td, te, tden, trec = (sb(n, [P, NT]) for n in ("td", "te", "tden", "trec"))
        tif = sb("tif", [P, NT, 2])
        eid = [sb(f"eid{k}", [P, NT]) for k in range(2)]
        oh = [sb(f"oh{k}", [P, NT, N_EXPERTS]) for k in range(2)]
        oha = sb("oha", [P, NT, N_EXPERTS])
        iota = sb("iota_f", [P, P])
        arow = [sb(f"arow{k}", [P, NT]) for k in range(2)]
        ohp = sb("ohp", [P, NT, N_EXPERTS])
        rank, over, rin, isov, ovb, blk, blo = ([sb(f"{n}{k}", [P, NT]) for k in range(2)]
                                                for n in ("rank", "over", "rin", "isov", "ovb", "blk", "blo"))
        nov, ovi, ove = (sb(n, [P, N_EXPERTS]) for n in ("nov", "ovi", "ove"))
        cmp = sb("cmp", [P, OVER, N_EXPERTS])
        oexp = sb("oexp", [P, OVER])
        ohr = [sb(f"ohr{i}", [P, P]) for i in range(2 * NT)]
        ohb = [sb(f"ohb{i}", [P, NB]) for i in range(2 * NT)]
        tab, tmiss, trow, txs = (sb(n, [P, NB]) for n in ("tab", "tmiss", "trow", "txs"))

        block = tmp.enter_context(nc.Block())

        @block.sync
        def _(sp):
            for u in range(4):
                if u >= 3:
                    sp.wait_ge(s["wlo"], u - 2)
                n, half = divmod(u, 2)
                sp.dma_start(raw[u % 3][:, :].rearrange("p (k c) -> p k c", k=4),
                             w_out[:, 4 * half:4 * half + 4, n * 512:n * 512 + 512]).then_inc(s_raw[u % 3], 16)
            for i in range(NT):
                sp.wait_ge(s["xn"], i + 1)
                sp.dma_start(m_rows[i * P:i * P + P, :], xn[i % 2][:, :]).then_inc(s_mrow[i % 2], 16)
            for x in s_mrow:
                sp.wait_ge(x, 16 * NT // 2)

        @block.gpsimd
        def _(pool):
            nc.gpsimd.iota(iota[:, :], [[1, P]], 0, 0, allow_small_or_imprecise_dtypes=True).then_inc(s["io"], 1)
            for k in range(2):
                nc.gpsimd.iota(arow[k][:, :], [[P, NT]], 1 + k * T, 1, allow_small_or_imprecise_dtypes=True).then_inc(s["io"], 1)
            nc.gpsimd.memset(gpad[:, :, :], -3.0e38).then_inc(s["io"], 1)

        @block.scalar
        def _(act):
            act.dma_start(gbc[:, :], dram["g_ffn"][0].partition_broadcast(P)).then_inc(s["gbc"], 16)
            act.dma_start(wr[:, :, 0:N_GROUPS], dram["w_router_group"][0].rearrange("(k p) c -> p k c", p=P)).then_inc(s["wr"], 16)
            act.dma_start(wr[:, :, N_GROUPS:NR], dram["w_router_expert"][0].rearrange("(k p) c -> p k c", p=P)).then_inc(s["wr"], 16)
            act.dma_start(rb[:, 0:N_GROUPS], dram["b_router_group"][0].partition_broadcast(P)).then_inc(s["rb"], 16)
            act.dma_start(rb[:, N_GROUPS:NR], dram["b_router_expert"][0].partition_broadcast(P)).then_inc(s["rb"], 16)

            def make_hi(u):
                act.wait_ge(s_raw[u % 3], 16 * (u // 3 + 1))
                if u >= 2:
                    act.wait_ge(s["wused"], u - 1)
                nc.scalar.copy(whi[u % 2][:, :], raw[u % 3][:, :]).then_inc(s["whi"], 1)

            make_hi(0)
            make_hi(1)
            for k in range(KD):
                act.wait_ge(s["tr"], k + 1)
                a = VEC_AT["sb_gain"] + k if k < 4 else VEC_AT["hg_gain"] + k - 4
                nc.scalar.activation(mixT_hi[:, k, :], banks[6 + k % 2], ACT.Copy, scale=cols[:, a:a + 1]).then_inc(s["hi"], 1)
            act.wait_ge(s["wr"], 32)
            nc.scalar.copy(wr_hi[:, :, :], wr[:, :, :]).then_inc(s["wrh"], 1)
            make_hi(2)
            make_hi(3)
            for i in range(NT):
                act.wait_ge(s["res"], NT + i + 1)
                nc.scalar.activation(sq[:, :], h[:, i, :], ACT.Square, accum_out=ssq[:, i:i + 1]).then_inc(s["ssq"], 1)
                act.wait_ge(s["ssq"], i + 1)
                nc.scalar.activation(rt[:, i:i + 1], ssq[:, i:i + 1], ACT.Sqrt, bias=eps[:, 0:1],
                                     scale=1.0 / D).then_inc(s["rt"], 1)
            for i in range(NT):
                for half in range(2):
                    act.wait_ge(s["mtr"], 2 * i + half + 1)
                    if i >= 2:
                        act.wait_ge(s["log"], i - 1)
                    nc.scalar.copy(mT_hi[i % 2][:, 4 * half:4 * half + 4, :],
                                   banks[6 + half].rearrange("p (k t) -> p k t", k=4)).then_inc(s["mhi"], 1)
            act.wait_ge(s["mx"], 2)
            for i in range(NT):
                nc.scalar.activation(gex[:, i, :], lg[:, i, 0:N_GROUPS], ACT.Exp, bias=ngm[:, i:i + 1],
                                     accum_out=gsum[:, i:i + 1]).then_inc(s["gs"], 1)
            act.wait_ge(s["v"], 1)
            nc.scalar.activation(te[:, :], td[:, :], ACT.Exp).then_inc(s["pe"], 1)

        @block.vector
        def _(dve):
            def make_lo(u):
                dve.wait_ge(s["whi"], u + 1)
                if u >= 2:
                    dve.wait_ge(s["wused"], u - 1)
                nc.vector.tensor_tensor(wlo[u % 2][:, :], raw[u % 3][:, :], whi[u % 2][:, :].bitcast(F32),
                                        ALU.subtract).then_inc(s["wlo"], 1)

            make_lo(0)
            make_lo(1)
            for k in range(KD):
                dve.wait_ge(s["hi"], k + 1)
                a = VEC_AT["sb_gain"] + k if k < 4 else VEC_AT["hg_gain"] + k - 4
                nc.vector.scalar_tensor_tensor(mixT_lo[:, k, :], banks[6 + k % 2], cols[:, a:a + 1],
                                               mixT_hi[:, k, :].bitcast(F32), ALU.mult, ALU.subtract).then_inc(s["lo"], 1)
            dve.wait_ge(s["wrh"], 1)
            nc.vector.tensor_tensor(wr_lo[:, :, :], wr[:, :, :], wr_hi[:, :, :].bitcast(F32), ALU.subtract).then_inc(s["wrl"], 1)

            def residual(o):
                n, i = divmod(o, NT)
                dve.wait_ge(s["out"] if i < NT - 1 else s["wused"], (NT - 1) * n + i + 1 if i < NT - 1 else 2 * n + 2)
                hh = h[:, i, n * 512:n * 512 + 512]
                nc.vector.tensor_tensor(hh, hh, banks[o % 6], ALU.add).then_inc(s["res"], 1)

            make_lo(2)
            for i in range(NT):
                residual(i)
            make_lo(3)
            for i in range(NT):
                residual(NT + i)
            dve.wait_ge(s["gbc"], 16)

            def lower(i):
                for half in range(2):
                    dve.wait_ge(s["mhi"], 2 * i + half + 1)
                    nc.vector.tensor_tensor(mT_lo[i % 2][:, 4 * half:4 * half + 4, :],
                                            banks[6 + half].rearrange("p (k t) -> p k t", k=4),
                                            mT_hi[i % 2][:, 4 * half:4 * half + 4, :].bitcast(F32),
                                            ALU.subtract).then_inc(s["mlo"], 1)

            for i in range(NT):
                dve.wait_ge(s["rt"], i + 1)
                nc.vector.reciprocal(rs[:, i:i + 1], rt[:, i:i + 1]).then_inc(s["rs"], 1)
                dve.wait_ge(s["rs"], i + 1)
                if i >= 2:
                    dve.wait_ge(s["mtr"], 2 * (i - 1))
                    dve.wait_ge(s_mrow[i % 2], 16 * (i // 2))
                nc.vector.scalar_tensor_tensor(xn[i % 2][:, :], h[:, i, :], rs[:, i:i + 1], gbc[:, :], ALU.mult,
                                               ALU.mult).then_inc(s["xn"], 1)
                if i >= 1:
                    lower(i - 1)
            lower(NT - 1)

            chain = [0]

            def step(ins):
                chain[0] += 1
                ins.then_inc(s["lg"], 1)
                dve.wait_ge(s["lg"], chain[0])

            V = nc.vector
            dve.wait_ge(s["log"], NT)
            dve.wait_ge(s["rb"], 32)
            step(V.tensor_tensor(lg[:, :, :], banks[0][:, 0:NT * NR].rearrange("p (i n) -> p i n", i=NT),
                                 rb[:, :].unsqueeze(1).to_broadcast([P, NT, NR]), ALU.add))
            dve.wait_ge(s["io"], 4)
            step(V.tensor_copy(gpad[:, :, 0:N_GROUPS], lg[:, :, 0:N_GROUPS]))
            for i in range(NT):
                step(V.max(gm[:, i, :], gpad[:, i, :]))
                step(V.max_index(gi[:, i, :], gm[:, i, :], gpad[:, i, :]))
            V.tensor_copy(gidx[:, :], gi[:, :, 0]).then_inc(s["mx"], 1)
            V.tensor_scalar(ngm[:, :], gm[:, :, 0], -1.0, None, ALU.mult).then_inc(s["mx"], 1)
            dve.wait_ge(s["mx"], 1)
            step(V.tensor_tensor(oh4[:, :, :], iota[:, 0:N_GROUPS].unsqueeze(1).to_broadcast([P, NT, N_GROUPS]),
                                 gidx[:, :].unsqueeze(2).to_broadcast([P, NT, N_GROUPS]), ALU.is_equal))
            for i in range(NT):
                last = V.tensor_tensor(pick[:, i, :, :], lg[:, i, N_GROUPS:NR].rearrange("p (g j) -> p g j", g=N_GROUPS),
                                       oh4[:, i, :].unsqueeze(2).to_broadcast([P, N_GROUPS, PER_GROUP]), ALU.mult)
            step(last)
            step(V.tensor_reduce(ing[:, :, :], pick[:, :, :, :].rearrange("p i g j -> p i j g"), AX.X, ALU.add))
            for i in range(NT):
                step(V.max(tv[:, i, :], ing[:, i, :]))
                step(V.max_index(ti[:, i, :], tv[:, i, :], ing[:, i, :]))
            V.tensor_tensor(td[:, :], tv[:, :, 1], tv[:, :, 0], ALU.subtract).then_inc(s["v"], 1)
            step(V.tensor_copy(tif[:, :, :], ti[:, :, 0:2]))
            dve.wait_ge(s["gs"], NT)
            step(V.reciprocal(pg[:, :], gsum[:, :]))
            dve.wait_ge(s["pe"], 1)
            step(V.tensor_scalar(tden[:, :], te[:, :], 1.0, None, ALU.add))
            step(V.reciprocal(trec[:, :], tden[:, :]))
            step(V.tensor_tensor(g["gate"][0][:, :], trec[:, :], pg[:, :], ALU.mult))
            step(V.tensor_tensor(g["gate"][1][:, :], g["gate"][0][:, :], te[:, :], ALU.mult))
            for k in range(2):
                step(V.scalar_tensor_tensor(eid[k][:, :], gidx[:, :], float(PER_GROUP), tif[:, :, k], ALU.mult, ALU.add))
                step(V.tensor_tensor(oh[k][:, :, :], iota[:, 0:N_EXPERTS].unsqueeze(1).to_broadcast([P, NT, N_EXPERTS]),
                                     eid[k][:, :].unsqueeze(2).to_broadcast([P, NT, N_EXPERTS]), ALU.is_equal))
            V.tensor_tensor(oha[:, :, :], oh[0][:, :, :], oh[1][:, :, :], ALU.add).then_inc(s["v"], 1)
            dve.wait_ge(s["pfx"], 1)
            count = banks[1][:, NT * N_EXPERTS:(NT + 1) * N_EXPERTS]
            step(V.tensor_scalar(nov[:, :], count, float(SLOTS + 1), None, ALU.is_ge))
            for o in range(2, T // SLOTS):
                step(V.scalar_tensor_tensor(nov[:, :], count, float(o * SLOTS + 1), nov[:, :], ALU.is_ge, ALU.add))
            step(V.tensor_tensor_scan(ovi[:, :], ones[:, 0:N_EXPERTS], nov[:, :], 0.0, ALU.mult, ALU.add))
            step(V.tensor_tensor(ove[:, :], ovi[:, :], nov[:, :], ALU.subtract))
            step(V.tensor_tensor(cmp[:, :, :], ovi[:, :].unsqueeze(1).to_broadcast([P, OVER, N_EXPERTS]),
                                 iota[:, 0:OVER].unsqueeze(2).to_broadcast([P, OVER, N_EXPERTS]), ALU.is_le))
            step(V.tensor_reduce(oexp[:, :], cmp[:, :, :], AX.X, ALU.add))
            step(V.tensor_scalar(g["over_e"][:, 0:OVER], oexp[:, :], float(N_EXPERTS - 1), None, ALU.min))
            step(V.tensor_copy(g["over_e"][:, OVER:OVER + 1], ovi[:, N_EXPERTS - 1:N_EXPERTS]))
            pfx = banks[1][:, 0:NT * N_EXPERTS].rearrange("p (i e) -> p i e", i=NT)
            for k in range(2):
                step(V.tensor_tensor(ohp[:, :, :], oh[k][:, :, :], pfx, ALU.mult))
                step(V.tensor_reduce(rank[k][:, :], ohp[:, :, :], AX.X, ALU.add))
                step(V.tensor_tensor(ohp[:, :, :], oh[k][:, :, :], ove[:, :].unsqueeze(1).to_broadcast([P, NT, N_EXPERTS]),
                                     ALU.mult))
                step(V.tensor_reduce(ovb[k][:, :], ohp[:, :, :], AX.X, ALU.add))
                step(V.tensor_scalar(isov[k][:, :], rank[k][:, :], float(SLOTS), None, ALU.is_ge))
                step(V.tensor_copy(over[k][:, :], isov[k][:, :]))
                for o in range(2, T // SLOTS):
                    step(V.scalar_tensor_tensor(over[k][:, :], rank[k][:, :], float(o * SLOTS), over[k][:, :], ALU.is_ge, ALU.add))
                step(V.scalar_tensor_tensor(rin[k][:, :], over[k][:, :], -float(SLOTS), rank[k][:, :], ALU.mult, ALU.add))
                step(V.scalar_tensor_tensor(blo[k][:, :], over[k][:, :], float(N_EXPERTS - 1), ovb[k][:, :], ALU.add, ALU.add))
                step(V.tensor_tensor(blo[k][:, :], blo[k][:, :], eid[k][:, :], ALU.subtract))
                step(V.tensor_tensor(blo[k][:, :], blo[k][:, :], isov[k][:, :], ALU.mult))
                step(V.tensor_tensor(blk[k][:, :], blo[k][:, :], eid[k][:, :], ALU.add))
                for i in range(NT):
                    V.tensor_scalar(ohr[NT * k + i][:, :], iota[:, :], rin[k][:, i:i + 1], None, ALU.is_equal)
                    V.tensor_scalar(ohb[NT * k + i][:, :], iota[:, 0:NB], blk[k][:, i:i + 1], arow[k][:, i:i + 1], ALU.is_equal,
                                    ALU.mult).then_inc(s["tab"], 1)
            dve.wait_ge(s["tabf"], 1)
            step(V.tensor_copy(tab[:, :], banks[2][:, 0:NB]))
            step(V.tensor_scalar(tmiss[:, :], tab[:, :], 0.5, BIG, ALU.is_lt, ALU.mult))
            step(V.scalar_tensor_tensor(trow[:, :], tab[:, :], -1.0, tmiss[:, :], ALU.add, ALU.add))
            step(V.tensor_copy(g["row_y"][:, :], trow[:, :]))
            step(V.tensor_scalar(txs[:, :], trow[:, :], float(T), -float(T), ALU.is_ge, ALU.mult))
            step(V.tensor_tensor(txs[:, :], txs[:, :], trow[:, :], ALU.add))
            step(V.tensor_copy(g["row_x"][:, :], txs[:, :]))

        @block.tensor
        def _(pe):
            for k in range(KD):
                if k >= 2:
                    pe.wait_ge(s["lo"], k - 1)
                for i in range(NT):
                    last = nc.tensor.transpose(banks[6 + k % 2][:, i * P:i * P + P], mixed[:, i, k * P:k * P + P], ident[:, :])
                last.then_inc(s["tr"], 1)
            pe.wait_ge(s["lo"], KD)
            for u in range(4):
                n, half = divmod(u, 2)
                pe.wait_ge(s["wlo"], u + 1)
                wh = whi[u % 2][:, :].rearrange("p (k c) -> p k c", k=4)
                wl = wlo[u % 2][:, :].rearrange("p (k c) -> p k c", k=4)
                for i in range(NT):
                    o = NT * n + i
                    if half == 0 and o >= 6:
                        pe.wait_ge(s["res"], o - 5)
                    for k in range(4):
                        kk = 4 * half + k
                        last = split_mm(nc, banks[o % 6], mixT_hi[:, kk, i * P:i * P + P], mixT_lo[:, kk, i * P:i * P + P],
                                        wh[:, k, :], wl[:, k, :], kk == 0, kk == KD - 1)
                    if i == NT - 1:
                        last.then_inc(s["wused"], 1)
                    elif half:
                        last.then_inc(s["out"], 1)
            for i in range(NT + 1):
                if i < NT:
                    pe.wait_ge(s["xn"], i + 1)
                    for half in range(2):
                        if i >= 1:
                            pe.wait_ge(s["mlo"], 2 * (i - 1) + half + 1)
                        for k in range(4):
                            last = nc.tensor.transpose(banks[6 + half][:, k * P:k * P + P],
                                                       xn[i % 2][:, (4 * half + k) * P:(4 * half + k + 1) * P], ident[:, :])
                        last.then_inc(s["mtr"], 1)
                if i >= 1:
                    j = i - 1
                    pe.wait_ge(s["mlo"], 2 * j + 2)
                    if j == 0:
                        pe.wait_ge(s["wrl"], 1)
                        pe.wait_ge(s["res"], 2 * NT)
                    for k in range(KD):
                        last = split_mm(nc, banks[0][:, j * NR:j * NR + NR], mT_hi[j % 2][:, k, :], mT_lo[j % 2][:, k, :],
                                        wr_hi[:, k, :], wr_lo[:, k, :], k == 0, k == KD - 1)
                    last.then_inc(s["log"], 1)
            pe.wait_ge(s["v"], 2)
            E = N_EXPERTS
            for i in range(NT):
                for j in range(i):
                    nc.tensor.matmul(banks[1][:, i * E:i * E + E], ones[:, :], oha[:, j, :], start=j == 0, stop=False)
                nc.tensor.matmul(banks[1][:, i * E:i * E + E], g["up"][:, :], oha[:, i, :], start=i == 0, stop=True)
            for j in range(NT):
                last = nc.tensor.matmul(banks[1][:, NT * E:NT * E + E], ones[:, :], oha[:, j, :], start=j == 0, stop=j == NT - 1)
            last.then_inc(s["pfx"], 1)
            for n in range(2 * NT):
                pe.wait_ge(s["tab"], n + 1)
                last = nc.tensor.matmul(banks[2][:, 0:NB], ohr[n][:, :], ohb[n][:, :], start=n == 0, stop=n == 2 * NT - 1)
            last.then_inc(s["tabf"], 1)
    g["clear"](s, s_raw, s_mrow)

    U = 6
    w_gate = dram["w_expert_gate"][0].rearrange("e (k p) f -> p e k f", p=P)
    w_up = dram["w_expert_up"][0].rearrange("e (k p) f -> p e k f", p=P)
    w_down = dram["w_expert_down"][0].rearrange("e (k p) f -> p e k f", p=P)
    s = {n: sem("e_" + n) for n in "hi lo used xg0 xg xt xhi xlo sg hid ht hhi hlo ya yd ysc".split()}
    s_raw = [sem(f"e_raw{j}") for j in range(U)]
    g["gathers"] += [s["xg"], s["ysc"]]
    with ExitStack() as tmp:
        def sb(name, shape, dt=F32):
            return tmp.enter_context(nc.sbuf_tensor(name, shape, dt))

        raw = [sb(f"raw_e{j}", [P, UNIT]) for j in range(U)]
        whi = [sb(f"whi_e{j}", [P, UNIT], F32R) for j in range(U)]
        wlo = [sb(f"wlo_e{j}", [P, UNIT], F32R) for j in range(U)]
        xg = sb("xg", [P, D])
        xT_hi, xT_lo = sb("xT_hi", [P, KD, P], F32R), sb("xT_lo", [P, KD, P], F32R)
        sg, hid = sb("sg", [P, FF]), sb("hid", [P, FF])
        hT_hi, hT_lo = sb("hT_hi", [P, 4, P], F32R), sb("hT_lo", [P, 4, P], F32R)
        y = sb("y_e", [P, D])
        row_x, row_y = g["row_x"], g["row_y"]
        GATE, UP, XT, HT, Y = banks[0], banks[1], (banks[2], banks[3]), banks[4], (banks[5], banks[6])

        def k4(t):
            return t[:, :].rearrange("p (k c) -> p k c", k=4)

        def k2(t):
            return t[:, :].rearrange("p (k c) -> p k c", k=2)

        def unit_source(e, j):
            if j < 4:
                w = w_gate if j < 2 else w_up
                k = 4 * (j % 2)
                return w[:, bass.ds(e, 1), k:k + 4, :].rearrange("p o k f -> p (o k) f")
            k = 2 * (j - 4)
            return w_down[:, bass.ds(e, 1), k:k + 2, :].rearrange("p o k f -> p (o k) f")

        def unit_place(j):
            return k4(raw[j]) if j < 4 else k2(raw[j])

        block = tmp.enter_context(nc.Block())

        @block.sync
        def _(sp):
            def load(e, j, of):
                sp.dma_start(unit_place(j), unit_source(of, j)).then_inc(s_raw[j], 16)

            for j in range(4):
                load(0, j, 0)
            for j in range(4):
                sp.wait_ge(s["lo"], j + 1)
                load(1, j, 1)
            for j in range(4, U):
                load(1, j, 0)
            with sp.Fori(2, N_EXPERTS) as e:
                for j in range(U):
                    sp.wait_ge(s["lo"], e * U - U + j + 1)
                    load(e, j, e if j < 4 else e - 1)
            for j in range(4, U):
                sp.wait_ge(s["lo"], N_EXPERTS * U - U + j + 1)
                load(N_EXPERTS, j, N_EXPERTS - 1)

        @block.scalar
        def _(act):
            def hi(e, j):
                act.wait_ge(s_raw[j], e * 16 + 16 if j < 4 else e * 16)
                if not (isinstance(e, int) and (e == 0 or (e == 1 and j >= 4))):
                    act.wait_ge(s["used"], e * U - U + j + 1)
                ins = nc.scalar.copy(whi[j][:, :], raw[j][:, :])
                ins.then_inc(s["hi"], 3 if isinstance(e, int) and e == 0 and j == 3 else 1)

            def x_hi(e):
                for half in range(2):
                    act.wait_ge(s["xt"], e * 2 + half + 1)
                    nc.scalar.copy(xT_hi[:, 4 * half:4 * half + 4, :],
                                   XT[half].rearrange("p (k t) -> p k t", k=4)).then_inc(s["xhi"], 1)

            def silu(e):
                act.wait_ge(s["used"], e * U + 2)
                if not isinstance(e, int) or e >= 1:
                    act.wait_ge(s["hid"], e)
                nc.scalar.activation(sg[:, :], GATE, ACT.Silu).then_inc(s["sg"], 1)

            def h_hi(e):
                act.wait_ge(s["ht"], e + 1)
                if not isinstance(e, int) or e >= 1:
                    act.wait_ge(s["used"], e * U + U)
                nc.scalar.copy(hT_hi[:, :, :], HT.rearrange("p (k t) -> p k t", k=4)).then_inc(s["hhi"], 1)

            def y_out(e):
                act.wait_ge(s["used"], e * U + 2 * U)
                if not isinstance(e, int) or e >= 1:
                    act.wait_ge(s["ysc"], e * 16)
                nc.scalar.copy(y[:, 0:512], Y[0]).then_inc(s["ya"], 1)

            def turn(e, first=False, last=False):
                hi(e, 3)
                silu(e)
                if not first:
                    h_hi(e - 1)
                    hi(e, 4)
                x_hi(e + 1)
                if not first:
                    hi(e, 5)
                if not last:
                    hi(e + 1, 0)
                    hi(e + 1, 1)
                if not first:
                    y_out(e - 1)
                if not last:
                    hi(e + 1, 2)

            x_hi(0)
            for j in range(3):
                hi(0, j)
            turn(0, first=True)
            turn(1)
            with act.Fori(2, N_EXPERTS - 1) as e:
                turn(e)
            turn(N_EXPERTS - 1, last=True)
            h_hi(N_EXPERTS - 1)
            hi(N_EXPERTS, 4)
            hi(N_EXPERTS, 5)
            y_out(N_EXPERTS - 1)

        @block.vector
        def _(dve):
            nc.vector.memset(xg[:, :], 0.0).then_inc(s["xg0"], 1)

            def lo(e, j):
                dve.wait_ge(s["hi"], (j + 1 if j < 3 else 6) if isinstance(e, int) and e == 0 else
                            e * U + j + 1 if not (isinstance(e, int) and e == N_EXPERTS) else e * U + j - 3)
                ins = nc.vector.tensor_tensor(wlo[j][:, :], raw[j][:, :], whi[j][:, :].bitcast(F32), ALU.subtract)
                ins.then_inc(s["lo"], 3 if isinstance(e, int) and e == 0 and j == 3 else 1)

            def x_lo(e):
                for half in range(2):
                    dve.wait_ge(s["xhi"], e * 2 + half + 1)
                    nc.vector.tensor_tensor(xT_lo[:, 4 * half:4 * half + 4, :], XT[half].rearrange("p (k t) -> p k t", k=4),
                                            xT_hi[:, 4 * half:4 * half + 4, :].bitcast(F32), ALU.subtract).then_inc(s["xlo"], 1)

            def hidden(e):
                dve.wait_ge(s["sg"], e + 1)
                dve.wait_ge(s["used"], e * U + 4 if not (isinstance(e, int) and e == 0) else 4)
                if not isinstance(e, int) or e >= 1:
                    dve.wait_ge(s["ht"], e)
                nc.vector.tensor_tensor(hid[:, :], sg[:, :], UP, ALU.mult).then_inc(s["hid"], 1)

            def h_lo(e):
                dve.wait_ge(s["hhi"], e + 1)
                nc.vector.tensor_tensor(hT_lo[:, :, :], HT.rearrange("p (k t) -> p k t", k=4), hT_hi[:, :, :].bitcast(F32),
                                        ALU.subtract).then_inc(s["hlo"], 1)

            def y_out(e):
                dve.wait_ge(s["used"], e * U + 2 * U)
                if not isinstance(e, int) or e >= 1:
                    dve.wait_ge(s["ysc"], e * 16)
                nc.vector.tensor_copy(y[:, 512:D], Y[1]).then_inc(s["yd"], 1)

            def turn(e, first=False, last=False):
                lo(e, 3)
                if not first:
                    h_lo(e - 1)
                    lo(e, 4)
                hidden(e)
                x_lo(e + 1)
                if not first:
                    lo(e, 5)
                if not last:
                    lo(e + 1, 0)
                    lo(e + 1, 1)
                if not first:
                    y_out(e - 1)
                if not last:
                    lo(e + 1, 2)

            x_lo(0)
            for j in range(3):
                lo(0, j)
            turn(0, first=True)
            turn(1)
            with dve.Fori(2, N_EXPERTS - 1) as e:
                turn(e)
            turn(N_EXPERTS - 1, last=True)
            h_lo(N_EXPERTS - 1)
            lo(N_EXPERTS, 4)
            lo(N_EXPERTS, 5)
            y_out(N_EXPERTS - 1)

        @block.gpsimd
        def _(pool):
            def gather(b):
                pool.indirect_dma_start(xg[:, :], None, m_rows, bass.IndirectOffsetOnAxis(row_x[:, b:b + 1], 0),
                                        bounds_check=T - 1, oob_is_err=False).then_inc(s["xg"], 16)

            def scatter(b):
                pool.indirect_dma_start(y_rows, bass.IndirectOffsetOnAxis(row_y[:, b:b + 1], 0), y[:, :], None,
                                        bounds_check=2 * T - 1, oob_is_err=False).then_inc(s["ysc"], 16)

            pool.wait_ge(s["xg0"], 1)
            gather(0)
            for e in range(N_EXPERTS):
                pool.wait_ge(s["xt"], e * 2 + 2)
                gather(e + 1)
                if e >= 1:
                    pool.wait_ge(s["ya"], e)
                    pool.wait_ge(s["yd"], e)
                    scatter(e - 1)
            pool.wait_ge(s["ya"], N_EXPERTS)
            pool.wait_ge(s["yd"], N_EXPERTS)
            scatter(N_EXPERTS - 1)
            pool.wait_ge(s["ysc"], 16 * N_EXPERTS)

        @block.tensor
        def _(pe):
            def x_turn(e):
                pe.wait_ge(s["xg"], e * 16 + 16)
                if not isinstance(e, int) or e >= 1:
                    pe.wait_ge(s["xlo"], e * 2)
                for half in range(2):
                    for k in range(4):
                        last = nc.tensor.transpose(XT[half][:, k * P:k * P + P], xg[:, (4 * half + k) * P:(4 * half + k + 1) * P],
                                                   ident[:, :])
                    last.then_inc(s["xt"], 1)

            def project(e, out, j0):
                for j in (j0, j0 + 1):
                    pe.wait_ge(s["lo"], e * U + j + 1 if not (isinstance(e, int) and e == 0 and j == 3) else U)
                    for k in range(4):
                        kk = 4 * (j % 2) + k
                        last = split_mm(nc, out, xT_hi[:, kk, :], xT_lo[:, kk, :], k4(whi[j])[:, k, :], k4(wlo[j])[:, k, :],
                                        kk == 0, kk == KD - 1)
                    last.then_inc(s["used"], 3 if isinstance(e, int) and e == 0 and j == 3 else 1)

            def h_turn(e):
                pe.wait_ge(s["hid"], e + 1)
                for k in range(4):
                    last = nc.tensor.transpose(HT[:, k * P:k * P + P], hid[:, k * P:k * P + P], ident[:, :])
                last.then_inc(s["ht"], 1)

            def down(e, n):
                pe.wait_ge(s["hlo"], e + 1)
                if not isinstance(e, int) or e >= 1:
                    pe.wait_ge(s["ya"], e)
                    pe.wait_ge(s["yd"], e)
                for j in (4, 5):
                    pe.wait_ge(s["lo"], n * U + j + 1 if not (isinstance(e, int) and e == N_EXPERTS - 1) else n * U + j - 3)
                    for half in range(2):
                        for k in range(2):
                            kk = 2 * (j - 4) + k
                            c = slice(half * 512, half * 512 + 512)
                            last = split_mm(nc, Y[half], hT_hi[:, kk, :], hT_lo[:, kk, :], k2(whi[j])[:, k, c], k2(wlo[j])[:, k, c],
                                            kk == 0, kk == 3)
                    if isinstance(e, int) and e == N_EXPERTS - 1:
                        last.then_inc(s["used"], 1 if j == 4 else 5)
                    else:
                        last.then_inc(s["used"], 1)

            def turn(e, first=False):
                pe.wait_ge(s["xlo"], e * 2 + 2)
                if not isinstance(e, int) or e >= 1:
                    pe.wait_ge(s["sg"], e)
                project(e, GATE, 0)
                if not first:
                    h_turn(e - 1)
                project(e, UP, 2)
                x_turn(e + 1)
                if not first:
                    down(e - 1, e)

            x_turn(0)
            turn(0, first=True)
            turn(1)
            with pe.Fori(2, N_EXPERTS) as e:
                turn(e)
            h_turn(N_EXPERTS - 1)
            down(N_EXPERTS - 1, N_EXPERTS)
    g["clear"](s, s_raw)

    over_e = g["over_e"]
    s = {n: sem("o_" + n) for n in "xg0 w xg xt xc gu sg hid ht hc down y ysc".split()}
    g["gathers"] += [s["xg"], s["ysc"]]
    with ExitStack() as tmp:
        def sb(name, shape, dt=F32):
            return tmp.enter_context(nc.sbuf_tensor(name, shape, dt))

        wg, wu = sb("wg_o", [P, KD, FF]), sb("wu_o", [P, KD, FF])
        wd = sb("wd_o", [P, FF // P, D])
        xg, xT = sb("xg_o", [P, D]), sb("xT_o", [P, KD, P])
        sg, hid, hidT = sb("sg_o", [P, FF]), sb("hid_o", [P, FF]), sb("hidT_o", [P, FF // P, P])
        y = sb("y_o", [P, D])
        block = tmp.enter_context(nc.Block())

        def blocks(eng, turn):
            n = eng.value_load(over_e[0:1, OVER:OVER + 1], min_val=0, max_val=OVER)
            with eng.If(n > 0):
                turn(0)
                with eng.Fori(1, OVER) as j:
                    turn(j)

        def later(j):
            return not isinstance(j, int)

        @block.sync
        def _(sp):
            def turn(j):
                if later(j):
                    sp.wait_ge(s["down"], j)
                e = sp.value_load(over_e[0:1, bass.ds(j, 1)] if later(j) else over_e[0:1, 0:1], min_val=0, max_val=N_EXPERTS - 1)
                for w, t in ((w_gate, wg), (w_up, wu), (w_down, wd)):
                    sp.dma_start(t[:, :, :], w[:, bass.ds(e, 1), :, :].rearrange("p o k f -> p (o k) f")).then_inc(s["w"], 16)

            blocks(sp, turn)

        @block.gpsimd
        def _(pool):
            n = pool.value_load(over_e[0:1, OVER:OVER + 1], min_val=0, max_val=OVER)
            with pool.If(n > 0):
                pool.wait_ge(s["xg0"], 1)
                for j in range(OVER):
                    b = N_EXPERTS + j
                    if j >= 1:
                        pool.wait_ge(s["xt"], j)
                    pool.indirect_dma_start(xg[:, :], None, m_rows, bass.IndirectOffsetOnAxis(row_x[:, b:b + 1], 0),
                                            bounds_check=T - 1, oob_is_err=False).then_inc(s["xg"], 16)
                    pool.wait_ge(s["y"], 2 * j + 2)
                    pool.indirect_dma_start(y_rows, bass.IndirectOffsetOnAxis(row_y[:, b:b + 1], 0), y[:, :], None,
                                            bounds_check=2 * T - 1, oob_is_err=False).then_inc(s["ysc"], 16)
                pool.wait_ge(s["ysc"], 16 * OVER)

        @block.scalar
        def _(act):
            def turn(j):
                act.wait_ge(s["xt"], j + 1)
                if later(j):
                    act.wait_ge(s["gu"], j)
                for half in range(2):
                    nc.scalar.copy(xT[:, 4 * half:4 * half + 4, :],
                                   banks[2 + half].rearrange("p (k t) -> p k t", k=4)).then_inc(s["xc"], 1)
                act.wait_ge(s["gu"], j + 1)
                if later(j):
                    act.wait_ge(s["hid"], j)
                nc.scalar.activation(sg[:, :], banks[0], ACT.Silu).then_inc(s["sg"], 1)
                act.wait_ge(s["ht"], j + 1)
                if later(j):
                    act.wait_ge(s["down"], j)
                nc.scalar.copy(hidT[:, :, :], banks[4].rearrange("p (k t) -> p k t", k=4)).then_inc(s["hc"], 1)
                act.wait_ge(s["down"], j + 1)
                if later(j):
                    act.wait_ge(s["ysc"], j * 16)
                for half in range(2):
                    nc.scalar.copy(y[:, 512 * half:512 * half + 512], banks[5 + half]).then_inc(s["y"], 1)

            blocks(act, turn)

        @block.vector
        def _(dve):
            nc.vector.memset(xg[:, :], 0.0).then_inc(s["xg0"], 1)

            def turn(j):
                dve.wait_ge(s["sg"], j + 1)
                if later(j):
                    dve.wait_ge(s["ht"], j)
                nc.vector.tensor_tensor(hid[:, :], sg[:, :], banks[1], ALU.mult).then_inc(s["hid"], 1)

            blocks(dve, turn)

        @block.tensor
        def _(pe):
            def turn(j):
                pe.wait_ge(s["xg"], j * 16 + 16)
                for k in range(KD):
                    last = nc.tensor.transpose(banks[2 + k // 4][:, (k % 4) * P:(k % 4 + 1) * P], xg[:, k * P:k * P + P], ident[:, :])
                last.then_inc(s["xt"], 1)
                pe.wait_ge(s["xc"], j * 2 + 2)
                pe.wait_ge(s["w"], j * 48 + 48)
                for o, t in ((0, wg), (1, wu)):
                    for k in range(KD):
                        last = nc.tensor.matmul(banks[o], xT[:, k, :], t[:, k, :], start=k == 0, stop=k == KD - 1)
                last.then_inc(s["gu"], 1)
                pe.wait_ge(s["hid"], j + 1)
                for k in range(FF // P):
                    last = nc.tensor.transpose(banks[4][:, k * P:k * P + P], hid[:, k * P:k * P + P], ident[:, :])
                last.then_inc(s["ht"], 1)
                pe.wait_ge(s["hc"], j + 1)
                if later(j):
                    pe.wait_ge(s["y"], j * 2)
                for half in range(2):
                    for k in range(FF // P):
                        last = nc.tensor.matmul(banks[5 + half], hidT[:, k, :], wd[:, k, 512 * half:512 * half + 512], start=k == 0,
                                                stop=k == FF // P - 1)
                last.then_inc(s["down"], 1)

            blocks(pe, turn)
    g["clear"](s)


class Weights:

    def __init__(self, nc, sem, sb, tag, sources, raw):
        self.nc, self.sources, self.raw = nc, sources, raw
        self.s_raw = [sem(f"{tag}_raw{i}") for i in range(len(raw))]
        self.s_hi, self.s_lo, self.out = sem(tag + "_whi"), sem(tag + "_wlo"), sem(tag + "_out")
        self.hi = [sb(f"whi_{tag}{i}", [P, UNIT], F32R) for i in range(2)]
        self.lo = [sb(f"wlo_{tag}{i}", [P, UNIT], F32R) for i in range(2)]

    def sems(self):
        return self.s_raw + [self.s_hi, self.s_lo, self.out]

    def load(self, sp, u):
        n = len(self.raw)
        if u >= n:
            sp.wait_ge(self.s_lo, u - n + 1)
        for place, src in self.sources[u]:
            sp.dma_start(place(self.raw[u % n]), src).then_inc(self.s_raw[u % n], 16)

    def make_hi(self, act, u):
        n = len(self.raw)
        act.wait_ge(self.s_raw[u % n], 32 * (u // n + 1))
        if u >= 2:
            act.wait_ge(self.out, 2 * (u - 1))
        self.nc.scalar.copy(self.hi[u % 2][:, :], self.raw[u % n]).then_inc(self.s_hi, 1)

    def make_lo(self, dve, u):
        dve.wait_ge(self.s_hi, u + 1)
        self.nc.vector.tensor_tensor(self.lo[u % 2][:, :], self.raw[u % len(self.raw)], self.hi[u % 2][:, :].bitcast(F32),
                                     ALU.subtract).then_inc(self.s_lo, 1)

    def halves(self, u, k):
        return (self.hi[u % 2][:, :].rearrange("p (k c) -> p k c", k=k),
                self.lo[u % 2][:, :].rearrange("p (k c) -> p k c", k=k))


def columns(w, c0, c1, width):
    def place(j):
        return lambda r: r.rearrange("p (k c) -> p k c", k=KD)[:, :, j * width:j * width + width]
    return [(place(0), w[:, :, c0:c0 + width]), (place(1), w[:, :, c1:c1 + width])]


def rows(w, k0, kn, c0, cn):
    def place(j):
        return lambda r: r.rearrange("p (k c) -> p k c", k=kn)[:, j * (kn // 2):(j + 1) * (kn // 2), :]
    return [(place(j), w[:, k0 + j * (kn // 2):k0 + (j + 1) * (kn // 2), c0:c0 + cn]) for j in range(2)]


def rms_root(nc, act, s, n, src, sq, ssq, rt, eps):
    nc.scalar.activation(sq, src, ACT.Square, accum_out=ssq).then_inc(s["ssq"], 1)
    act.wait_ge(s["ssq"], n + 1)
    nc.scalar.activation(rt, ssq, ACT.Sqrt, bias=eps[:, 0:1], scale=1.0 / D).then_inc(s["rt"], 1)


def rms_scale(nc, dve, s, n, rt, rs):
    dve.wait_ge(s["rt"], n + 1)
    nc.vector.reciprocal(rs, rt).then_inc(s["rs"], 1)
    dve.wait_ge(s["rs"], n + 1)


def turn_rows(nc, pe, s, i, xn, banks, ident):
    pe.wait_ge(s["xn"], i + 1)
    for half in range(2):
        if i >= 1:
            pe.wait_ge(s["lo"], 2 * (i - 1) + half + 1)
        for k in range(4):
            last = nc.tensor.transpose(banks[6 + half][:, k * P:k * P + P], xn[:, (4 * half + k) * P:(4 * half + k + 1) * P],
                                       ident[:, :])
        last.then_inc(s["tr"], 1)


def turned_hi(nc, act, s, i, banks, hi):
    for half in range(2):
        act.wait_ge(s["tr"], 2 * i + half + 1)
        nc.scalar.copy(hi[:, 4 * half:4 * half + 4, i * P:i * P + P],
                       banks[6 + half].rearrange("p (k t) -> p k t", k=4)).then_inc(s["hi"], 1)


def turned_lo(nc, dve, s, i, banks, hi, lo):
    for half in range(2):
        dve.wait_ge(s["hi"], 2 * i + half + 1)
        nc.vector.tensor_tensor(lo[:, 4 * half:4 * half + 4, i * P:i * P + P],
                                banks[6 + half].rearrange("p (k t) -> p k t", k=4),
                                hi[:, 4 * half:4 * half + 4, i * P:i * P + P].bitcast(F32), ALU.subtract).then_inc(s["lo"], 1)


def stage_c(nc, dram, g, sem, banks, out):
    with ExitStack() as keep:
        hT = [keep.enter_context(nc.sbuf_tensor(n, [P, KD, T], F32R)) for n in ("hT2_hi", "hT2_lo")]
        join(nc, dram, g, sem, banks, hT)
        conv_branch(nc, dram, g, sem, banks, hT)
        with ExitStack() as ssm:
            yT = ssm.enter_context(nc.sbuf_tensor("yT", [P, D_INNER // P, T], F32))
            ssd_branch(nc, dram, g, sem, banks, hT, yT)
            mix(nc, dram, g, sem, banks, hT, yT)
        ffn(nc, dram, g, sem, banks, hT, out)


def join(nc, dram, g, sem, banks, hT):
    h, eps, ident = g["h"], g["eps"], g["ident"]
    s = {n: sem("j_" + n) for n in "gf gp y sum ssq rt rs x xn tr hi lo".split()}
    s_y = [sem(f"j_y{i}") for i in range(NT)]
    y_rows = g["y_rows"].rearrange("(k i p) d -> p k i d", p=P, k=2)
    with ExitStack() as tmp:
        def sb(name, shape, dt=F32):
            return tmp.enter_context(nc.sbuf_tensor(name, shape, dt))

        yk = sb("yk", [P, 2, NT, D])
        gf, gp, sq = sb("gf", [P, D]), sb("gp", [P, D]), sb("sq_j", [P, D])
        xn = [sb(f"xn_j{i}", [P, D]) for i in range(2)]
        ssq, rt, rs = (sb(n, [P, 2 * NT]) for n in ("ssq_j", "rt_j", "rs_j"))
        block = tmp.enter_context(nc.Block())

        @block.sync
        def _(sp):
            for i in range(NT):
                for k in range(2):
                    sp.dma_start(yk[:, k, i, :], y_rows[:, k, i, :]).then_inc(s_y[i], 16)

        @block.scalar
        def _(act):
            act.dma_start(gf[:, :], dram["g_final"].unsqueeze(0)[0].partition_broadcast(P)).then_inc(s["gf"], 16)
            act.dma_start(gp[:, :], dram["mix_pre_g_2"][0].partition_broadcast(P)).then_inc(s["gp"], 16)
            for i in range(NT + 1):
                if i < NT:
                    act.wait_ge(s["sum"], 2 * i + 2)
                    rms_root(nc, act, s, 2 * i, h[:, i, :], sq[:, :], ssq[:, 2 * i:2 * i + 1], rt[:, 2 * i:2 * i + 1], eps)
                    act.wait_ge(s["x"], i + 1)
                    rms_root(nc, act, s, 2 * i + 1, h[:, i, :], sq[:, :], ssq[:, 2 * i + 1:2 * i + 2],
                             rt[:, 2 * i + 1:2 * i + 2], eps)
                if i >= 1:
                    turned_hi(nc, act, s, i - 1, banks, hT[0])

        @block.vector
        def _(dve):
            dve.wait_ge(s["gf"], 16)
            dve.wait_ge(s["gp"], 16)
            for i in range(NT):
                dve.wait_ge(s_y[i], 32)
                for k in range(2):
                    nc.vector.scalar_tensor_tensor(h[:, i, :], yk[:, k, i, :], g["gate"][k][:, i:i + 1], h[:, i, :], ALU.mult,
                                                   ALU.add).then_inc(s["sum"], 1)
                    dve.wait_ge(s["sum"], 2 * i + k + 1)
                rms_scale(nc, dve, s, 2 * i, rt[:, 2 * i:2 * i + 1], rs[:, 2 * i:2 * i + 1])
                nc.vector.scalar_tensor_tensor(h[:, i, :], h[:, i, :], rs[:, 2 * i:2 * i + 1], gf[:, :], ALU.mult,
                                               ALU.mult).then_inc(s["x"], 1)
                if i >= 1:
                    turned_lo(nc, dve, s, i - 1, banks, *hT)
                rms_scale(nc, dve, s, 2 * i + 1, rt[:, 2 * i + 1:2 * i + 2], rs[:, 2 * i + 1:2 * i + 2])
                dve.wait_ge(s["x"], i + 1)
                if i >= 2:
                    dve.wait_ge(s["tr"], 2 * (i - 1))
                nc.vector.scalar_tensor_tensor(xn[i % 2][:, :], h[:, i, :], rs[:, 2 * i + 1:2 * i + 2], gp[:, :], ALU.mult,
                                               ALU.mult).then_inc(s["xn"], 1)
            turned_lo(nc, dve, s, NT - 1, banks, *hT)

        @block.tensor
        def _(pe):
            for i in range(NT):
                turn_rows(nc, pe, s, i, xn[i % 2], banks, ident)
    g["clear"](s, s_y)


def product(nc, pe, W, u, v, out, hT):
    hi, lo = W.halves(u, KD)
    for k in range(KD):
        last = split_mm(nc, out, hi[:, k, v * P:v * P + P], lo[:, k, v * P:v * P + P], hT[0][:, k, :], hT[1][:, k, :],
                        k == 0, k == KD - 1)
    last.then_inc(W.out, 1)


def conv_branch(nc, dram, g, sem, banks, hT):
    cols, ones, eps = g["cols"], g["ones"], g["eps"]
    w = dram["w_in_2"][0].rearrange("(k p) c -> p k c", p=P)
    w_pw = dram["conv_pw_w_2"][0].rearrange("(k p) c -> p k c", p=P)
    mixT = g["mixed"][:, :, :].rearrange("p i d -> p (i d)").rearrange("p (c t) -> p c t", c=KD)
    PAD = CONV_K - 1
    GATES, PW = KD, KD + 4
    sources = ([columns(w, c * P, D + c * P, P) for c in range(KD)]
               + [columns(w, OFF_GATE + 2 * n * P, OFF_GATE + (2 * n + 1) * P, P) for n in range(4)]
               + [columns(w_pw, 2 * n * P, (2 * n + 1) * P, P) for n in range(4)])
    NU = len(sources)
    on_pool = [c for c in range(KD) if c % 3 == 2]
    on_dve = [c for c in range(KD) if c not in on_pool]

    def col(name, n):
        return cols[:, VEC_AT[name] + n:VEC_AT[name] + n + 1]

    s = {n: sem("f_" + n) for n in "pad sg v tap tapp cd cp gate mean mu xc sqd var rt rstd nrm act hi lo mixd".split()}
    with ExitStack() as tmp:
        def sb(name, shape, dt=F32):
            return tmp.enter_context(nc.sbuf_tensor(name, shape, dt))

        W = Weights(nc, sem, sb, "f", sources, [sb(f"raw_f{i}", [P, UNIT])[:, :] for i in range(3)])
        v = sb("v_pad", [P, KD, PAD + T])
        acc = sb("conv_acc", [P, KD, T])
        sT = [sb(n, [P, KD, T], F32R) for n in ("sT_hi", "sT_lo")]
        sg = [sb(f"sg_f{i}", [P, T]) for i in range(2)]
        mu, rtv = sb("mu", [P, T]), sb("rtv", [P, T])
        tp = sb("tp_f", [P, T])
        block = tmp.enter_context(nc.Block())

        def taps(dve, chain, c):
            dve.wait_ge(s["pad"], 1)
            for k in range(CONV_K):
                src = v[:, c, k:k + T]
                if k == 0:
                    ins = nc.vector.tensor_scalar(acc[:, c, :], src, col("dw_w_a", c), col("dw_b", c), ALU.mult, ALU.add)
                else:
                    ins = nc.vector.scalar_tensor_tensor(acc[:, c, :], src, col("dw_w_a", k * KD + c), acc[:, c, :], ALU.mult,
                                                         ALU.add)
                if k < CONV_K - 1:
                    chain[0] += 1
                    ins.then_inc(s["tap"], 1)
                    dve.wait_ge(s["tap"], chain[0])
            ins.then_inc(s["cd"], 1)

        def taps_in_two(pool, chain, c):
            for k in range(CONV_K):
                src = v[:, c, k:k + T]
                if k == 0:
                    ins = nc.gpsimd.tensor_scalar(acc[:, c, :], src, col("dw_w_a", c), col("dw_b", c), ALU.mult, ALU.add)
                else:
                    nc.gpsimd.tensor_scalar(tp[:, :], src, col("dw_w_a", k * KD + c), None, ALU.mult).then_inc(s["tapp"], 1)
                    chain[0] += 1
                    pool.wait_ge(s["tapp"], chain[0])
                    ins = nc.gpsimd.tensor_tensor(acc[:, c, :], acc[:, c, :], tp[:, :], ALU.add)
                if k < CONV_K - 1:
                    chain[0] += 1
                    ins.then_inc(s["tapp"], 1)
                    pool.wait_ge(s["tapp"], chain[0])
            ins.then_inc(s["cp"], 1)
            pool.wait_ge(s["cp"], on_pool.index(c) + 1)

        @block.sync
        def _(sp):
            for u in range(NU):
                W.load(sp, u)

        @block.gpsimd
        def _(pool):
            nc.gpsimd.memset(v[:, :, 0:PAD], 0.0).then_inc(s["pad"], 1)
            pool.wait_ge(s["pad"], 1)
            chain = [0]
            for c in on_pool:
                pool.wait_ge(s["v"], c + 1)
                taps_in_two(pool, chain, c)

        @block.scalar
        def _(act):
            W.make_hi(act, 0)
            W.make_hi(act, 1)
            for c in range(KD):
                act.wait_ge(W.out, 2 * c + 2)
                if c >= 2:
                    act.wait_ge(s["v"], c - 1)
                nc.scalar.activation(sg[c % 2][:, :], banks[(2 * c + 1) % 6], ACT.Sigmoid, bias=col("glu_b", KD + c)).then_inc(s["sg"], 1)
                W.make_hi(act, c + 2)
            for u in range(GATES, PW):
                for j in range(2):
                    n = 2 * (u - GATES) + j
                    act.wait_ge(W.out, 2 * u + j + 1)
                    nc.scalar.activation(mixT[:, n, :], banks[(2 * u + j) % 6], ACT.Sigmoid, bias=col("gate_b", n)).then_inc(s["gate"], 1)
                W.make_hi(act, u + 2)
            for c in range(KD):
                act.wait_ge(s["xc"], c + 1)
                nc.scalar.activation(v[:, c, 0:T], acc[:, c, :], ACT.Square).then_inc(s["sqd"], 1)
            act.wait_ge(s["var"], 1)
            nc.scalar.activation(rtv[:, :], banks[7], ACT.Sqrt, bias=eps[:, 1:2], scale=1.0 / D).then_inc(s["rt"], 1)
            for c in range(KD):
                act.wait_ge(s["nrm"], c + 1)
                nc.scalar.activation(acc[:, c, :], acc[:, c, :], ACT.Silu, bias=col("ln_b", c), scale=col("ln_g", c)).then_inc(s["act"], 1)
                act.wait_ge(s["act"], c + 1)
                nc.scalar.copy(sT[0][:, c, :], acc[:, c, :]).then_inc(s["hi"], 1)
            for u in range(PW + 2, NU):
                W.make_hi(act, u)

        @block.vector
        def _(dve):
            W.make_lo(dve, 0)
            W.make_lo(dve, 1)
            chain = [0]
            for c in range(KD):
                dve.wait_ge(s["sg"], c + 1)
                nc.vector.scalar_tensor_tensor(v[:, c, PAD:PAD + T], banks[2 * c % 6], col("glu_b", c), sg[c % 2][:, :], ALU.add,
                                               ALU.mult).then_inc(s["v"], 1)
                W.make_lo(dve, c + 2)
                if c in on_dve:
                    dve.wait_ge(s["v"], c + 1)
                    taps(dve, chain, c)
            for u in range(GATES + 2, PW + 2):
                W.make_lo(dve, u)
            dve.wait_ge(s["mean"], 1)
            nc.vector.tensor_scalar(mu[:, :], banks[6], 1.0 / D, None, ALU.mult).then_inc(s["mu"], 1)
            dve.wait_ge(s["mu"], 1)
            for c in range(KD):
                nc.vector.tensor_tensor(acc[:, c, :], acc[:, c, :], mu[:, :], ALU.subtract).then_inc(s["xc"], 1)
            dve.wait_ge(s["rt"], 1)
            nc.vector.reciprocal(rtv[:, :], rtv[:, :]).then_inc(s["rstd"], 1)
            dve.wait_ge(s["rstd"], 1)
            for c in range(KD):
                dve.wait_ge(s["xc"], c + 1)
                nc.vector.tensor_tensor(acc[:, c, :], acc[:, c, :], rtv[:, :], ALU.mult).then_inc(s["nrm"], 1)
            for c in range(KD):
                dve.wait_ge(s["hi"], c + 1)
                nc.vector.tensor_tensor(sT[1][:, c, :], acc[:, c, :], sT[0][:, c, :].bitcast(F32), ALU.subtract).then_inc(s["lo"], 1)
            for u in range(PW, NU):
                for j in range(2):
                    n = 2 * (u - PW) + j
                    dve.wait_ge(W.out, 2 * u + j + 1)
                    nc.vector.scalar_tensor_tensor(mixT[:, n, :], banks[(2 * u + j) % 6], col("pw_b", n), mixT[:, n, :], ALU.add,
                                                   ALU.mult).then_inc(s["mixd"], 1)
                if u + 2 < NU:
                    W.make_lo(dve, u + 2)

        @block.tensor
        def _(pe):
            def unit(u, of):
                pe.wait_ge(W.s_lo, u + 1)
                if 3 <= u < GATES + 3:
                    pe.wait_ge(s["v"], u - 2)
                elif GATES + 3 <= u < PW + 3:
                    pe.wait_ge(s["gate"], 2 * (u - 3 - GATES) + 2)
                elif u >= PW + 3:
                    pe.wait_ge(s["mixd"], 2 * (u - 3 - PW) + 2)
                for j in range(2):
                    product(nc, pe, W, u, j, banks[(2 * u + j) % 6], of)

            for u in range(PW):
                unit(u, hT)
            for c in range(KD):
                if c in on_pool:
                    pe.wait_ge(s["cp"], on_pool.index(c) + 1)
                else:
                    pe.wait_ge(s["cd"], on_dve.index(c) + 1)
                last = nc.tensor.matmul(banks[6], ones[:, :], acc[:, c, :], start=c == 0, stop=c == KD - 1)
            last.then_inc(s["mean"], 1)
            for c in range(KD):
                pe.wait_ge(s["sqd"], c + 1)
                last = nc.tensor.matmul(banks[7], ones[:, :], v[:, c, 0:T], start=c == 0, stop=c == KD - 1)
            last.then_inc(s["var"], 1)
            pe.wait_ge(s["lo"], KD)
            for u in range(PW, NU):
                unit(u, sT)
    g["clear"](s, W.sems())


def ssd_branch(nc, dram, g, sem, banks, hT, yT):
    cols, ident, tri, ones, eps = (g[n] for n in "cols ident tri ones eps".split())
    w = dram["w_in_2"][0].rearrange("(k p) c -> p k c", p=P)
    G, R, H, C = SSM_GROUPS, SSM_RANK, SSM_HEADS, NT
    PAD = SSM_K - 1
    GW = R * SSM_HD
    sources = []
    for n in range(G):
        sources.append(columns(w, OFF_XBC + n * GW, OFF_XBC + n * GW + P, P))
        sources.append(columns(w, OFF_B + n * P, OFF_C + n * P, P))
        sources.append(columns(w, OFF_Z + n * GW, OFF_Z + n * GW + P, P))
    NU = len(sources)
    s = {n: sem("s_" + n) for n in (
        "row wdt wdh wdl dtp dt e1 e2 acs acp acT acw pad pc tapd tapp cvd cvp sl zs tx tb cb xn bn cbm ar eal dtd dte seg ex "
        "A xdt xde xd stp st stc yd yo yr t0 yt ssq rt rs yn ty ye".split())}

    def col(name, n):
        return cols[:, VEC_AT[name] + n:VEC_AT[name] + n + 1]

    with ExitStack() as tmp:
        def sb(name, shape, dt=F32):
            return tmp.enter_context(nc.sbuf_tensor(name, shape, dt))

        W = Weights(nc, sem, sb, "s", sources, [sb(f"raw_s{i}", [P, UNIT])[:, :] for i in range(2)])
        wdh, wdl = sb("wdt_hi", [P, KD, H], F32R), sb("wdt_lo", [P, KD, H], F32R)
        dtb, al, dsk = sb("dtb", [P, H]), sb("al", [P, H]), sb("dsk", [P, H])
        dt, adt, acs, eacs = (sb(n, [P, C, H]) for n in ("dt", "adt", "acs", "eacs"))
        pc = sb("pc", [P, 4, PAD + T])
        xbc = sb("xbc", [P, 4, T])
        zs = sb("zs", [P, C, GW])
        x_nat, xdt, xde, y = (sb(n, [P, C, GW]) for n in ("x_nat", "xdt", "xde", "y_s"))
        yo = xde
        b_nat = sb("b_nat", [P, C, P])
        cbm = sb("cbm", [P, C, P])
        A = sb("A", [P, R, T])
        eal = sb("eal", [P, R, C])
        dte = sb("dte", [P, C, R])
        tp = sb("tp_s", [P, T])
        st = sb("st_s", [P, C, GW])
        ssq, rt, rs = (sb(n, [P, C]) for n in ("ssq_s", "rt_s", "rs_s"))
        wdt = zs[:, 0, :].rearrange("p (k h) -> p k h", k=KD)
        dtz, dta = (x_nat[:, 0, i * C * H:(i + 1) * C * H].rearrange("p (c h) -> p c h", c=C) for i in range(2))
        acT = xde[0:H, 0:2, :].rearrange("p c d -> p (c d)")
        acs_rows = g["acs_rows"]
        block = tmp.enter_context(nc.Block())

        def heads(t):
            return t[:, :, :].rearrange("p c (r d) -> p c r d", r=R)

        def by_head(t, n):
            return t[:, :, n * R:n * R + R].unsqueeze(3).to_broadcast([P, C, R, SSM_HD])

        def conv_tile(n, j):
            return (2 * n + j) if j < 2 else 2 * G + (n if j == 2 else G + n)

        def taps(dve, chain, n, j):
            tile = conv_tile(n, j)
            for k in range(SSM_K):
                src, wk = pc[:, j, k:k + T], col("ssm_w", k * 4 * G + tile)
                if k == 0:
                    ins = nc.vector.tensor_scalar(xbc[:, j, :], src, wk, col("ssm_b", tile), ALU.mult, ALU.add)
                else:
                    ins = nc.vector.scalar_tensor_tensor(xbc[:, j, :], src, wk, xbc[:, j, :], ALU.mult, ALU.add)
                if k < SSM_K - 1:
                    chain[0] += 1
                    ins.then_inc(s["tapd"], 1)
                    dve.wait_ge(s["tapd"], chain[0])
            ins.then_inc(s["cvd"], 1)

        def taps_in_two(pool, chain, n, j):
            tile = conv_tile(n, j)
            for k in range(SSM_K):
                src, wk = pc[:, j, k:k + T], col("ssm_w", k * 4 * G + tile)
                if k == 0:
                    ins = nc.gpsimd.tensor_scalar(xbc[:, j, :], src, wk, col("ssm_b", tile), ALU.mult, ALU.add)
                else:
                    nc.gpsimd.tensor_scalar(tp[:, :], src, wk, None, ALU.mult).then_inc(s["tapp"], 1)
                    chain[0] += 1
                    pool.wait_ge(s["tapp"], chain[0])
                    ins = nc.gpsimd.tensor_tensor(xbc[:, j, :], xbc[:, j, :], tp[:, :], ALU.add)
                if k < SSM_K - 1:
                    chain[0] += 1
                    ins.then_inc(s["tapp"], 1)
                    pool.wait_ge(s["tapp"], chain[0])
            ins.then_inc(s["cvp"], 1)
            pool.wait_ge(s["cvp"], 2 * n + j - 1)

        @block.sync
        def _(sp):
            for u in range(4):
                W.load(sp, u)
            sp.wait_ge(s["acT"], 1)
            sp.dma_start(acs_rows, acT).then_inc(s["acw"], 16)
            sp.wait_ge(s["acw"], 16)
            for n in range(G):
                if n >= 1:
                    sp.wait_ge(s["yd"], 2 * n)
                sp.dma_start(A[:, :, :].rearrange("p r t -> p (r t)"), acs_rows[n * R:n * R + R, :].rearrange("r t -> (r t)")
                             .partition_broadcast(P)).then_inc(s["ar"], 16)
                for u in range(3 * n + 4, min(3 * n + 7, NU)):
                    W.load(sp, u)

        @block.gpsimd
        def _(pool):
            nc.gpsimd.memset(pc[:, :, 0:PAD], 0.0).then_inc(s["pad"], 1)
            chain = [0]
            pool.wait_ge(s["pad"], 1)
            pool.wait_ge(s["row"], 48)
            for n in range(G):
                for j in (2, 3):
                    pool.wait_ge(s["pc"], 4 * n + j + 1)
                    if n >= 1:
                        pool.wait_ge(s["cb"], n)
                        if j == 2:
                            pool.wait_ge(s["tb"], n)
                        else:
                            pool.wait_ge(s["yo"], 2 * n)
                    taps_in_two(pool, chain, n, j)
                pool.wait_ge(s["xn"], 2 * n + 2)
                if n >= 1:
                    pool.wait_ge(s["ty"], 2 * n)
                nc.gpsimd.tensor_tensor(heads(y), heads(x_nat),
                                        dsk[:, n * R:n * R + R].unsqueeze(1).unsqueeze(3).to_broadcast([P, C, R, SSM_HD]),
                                        ALU.mult).then_inc(s["xd"], 1)

        @block.scalar
        def _(act):
            act.dma_start(wdt, w[:, :, OFF_DT:OFF_GATE]).then_inc(s["wdt"], 16)
            act.dma_start(dtb[:, :], dram["dt_bias_2"][0].partition_broadcast(P)).then_inc(s["row"], 16)
            act.dma_start(al[:, :], dram["a_log_2"][0].partition_broadcast(P)).then_inc(s["row"], 16)
            act.dma_start(dsk[:, :], dram["d_skip_2"][0].partition_broadcast(P)).then_inc(s["row"], 16)
            act.wait_ge(s["wdt"], 16)
            nc.scalar.copy(wdh[:, :, :], wdt).then_inc(s["wdh"], 1)
            W.make_hi(act, 0)
            W.make_hi(act, 1)
            act.wait_ge(s["row"], 48)
            nc.scalar.activation(al[:, :], al[:, :], ACT.Exp).then_inc(s["e1"], 1)
            act.wait_ge(s["dt"], 3)
            nc.scalar.activation(dta, dta, ACT.Exp, scale=-1.0).then_inc(s["e1"], 1)
            act.wait_ge(s["e1"], 2)
            nc.scalar.activation(dta, dta, ACT.Ln, bias=1.0).then_inc(s["e1"], 1)
            act.wait_ge(s["acp"], 1)
            nc.scalar.activation(eacs[:, :, :], banks[5][:, 0:C * H].rearrange("p (c h) -> p c h", c=C), ACT.Exp).then_inc(s["e2"], 1)
            nc.scalar.copy(acT, banks[6][0:H, :]).then_inc(s["acT"], 1)

            def evacuate(n, tiles):
                for j in tiles:
                    act.wait_ge(W.out, 6 * n + j + 1)
                    act.wait_ge(s["pad"], 1)
                    if n >= 1:
                        if j < 2:
                            act.wait_ge(s["cvd"], 2 * (n - 1) + j + 1)
                        else:
                            act.wait_ge(s["cvp"], 2 * (n - 1) + j - 1)
                    nc.scalar.copy(pc[:, j, PAD:PAD + T], banks[j]).then_inc(s["pc"], 1)

            def gate(n):
                if n >= 1:
                    act.wait_ge(s["yt"], n)
                for j in range(2):
                    act.wait_ge(W.out, 6 * n + 4 + j + 1)
                    nc.scalar.activation(zs[:, 2 * j:2 * j + 2, :], banks[j].rearrange("p (c d) -> p c d", c=2),
                                         ACT.Silu).then_inc(s["zs"], 1)

            def store(n):
                for j in range(2):
                    act.wait_ge(s["ty"], 2 * n + j + 1)
                    nc.scalar.activation(yT[:, 2 * n + j, :], banks[6 + j], ACT.Copy, scale=col("norm_g", 2 * n + j)).then_inc(s["ye"], 1)

            evacuate(0, (0, 1))
            W.make_hi(act, 2)
            evacuate(0, (2, 3))
            W.make_hi(act, 3)
            gate(0)
            for n in range(G):
                more = n + 1 < G
                for j in range(4):
                    if j < 2:
                        act.wait_ge(s["cvd"], 2 * n + j + 1)
                    else:
                        act.wait_ge(s["cvp"], 2 * n + j - 1)
                    nc.scalar.activation(xbc[:, j, :], xbc[:, j, :], ACT.Silu).then_inc(s["sl"], 1)
                if more:
                    W.make_hi(act, 3 * n + 4)
                    evacuate(n + 1, (0, 1))
                if n >= 1:
                    store(n - 1)
                act.wait_ge(s["ar"], 16 * n + 16)
                if n >= 1:
                    act.wait_ge(s["stc"], 3 * n)
                nc.scalar.activation(eal[:, :, :], A[:, :, P - 1:T:P], ACT.Exp).then_inc(s["eal"], 1)
                act.wait_ge(s["dtd"], n + 1)
                nc.scalar.activation(dte[:, :, :], dte[:, :, :], ACT.Exp).then_inc(s["dte"], 1)
                act.wait_ge(s["seg"], 2 * n + 2)
                nc.scalar.activation(A[:, :, :], A[:, :, :], ACT.Exp).then_inc(s["ex"], 1)
                for j in range(2):
                    act.wait_ge(s["tx"], 2 * n + j + 1)
                    if n >= 1:
                        act.wait_ge(s["xdt"], n)
                        act.wait_ge(s["xd"], n)
                    nc.scalar.copy(x_nat[:, 2 * j:2 * j + 2, :], banks[4 + j].rearrange("p (c d) -> p c d", c=2)).then_inc(s["xn"], 1)
                act.wait_ge(s["tb"], n + 1)
                if n >= 1:
                    act.wait_ge(s["stp"], 2 * n)
                nc.scalar.copy(b_nat[:, :, :], banks[6].rearrange("p (c d) -> p c d", c=C)).then_inc(s["bn"], 1)
                if more:
                    W.make_hi(act, 3 * n + 5)
                    evacuate(n + 1, (2, 3))
                    if 3 * n + 6 < NU:
                        W.make_hi(act, 3 * n + 6)
                act.wait_ge(s["yt"], n + 1)
                for c in range(C):
                    if n or c:
                        act.wait_ge(s["ssq"], C * n + c)
                    if n >= 1 and c == 0:
                        act.wait_ge(s["rt"], n)
                    nc.scalar.activation(yo[:, 0, :], y[:, c, :], ACT.Square, accum_out=ssq[:, c:c + 1]).then_inc(s["ssq"], 1)
                act.wait_ge(s["ssq"], C * n + C)
                if n >= 1:
                    act.wait_ge(s["rs"], n)
                nc.scalar.activation(rt[:, :], ssq[:, :], ACT.Sqrt, bias=eps[:, 0:1], scale=1.0 / GW).then_inc(s["rt"], 1)
                if more:
                    gate(n + 1)
            store(G - 1)

        @block.vector
        def _(dve):
            V = nc.vector
            dve.wait_ge(s["wdh"], 1)
            V.tensor_tensor(wdl[:, :, :], wdt, wdh[:, :, :].bitcast(F32), ALU.subtract).then_inc(s["wdl"], 1)
            W.make_lo(dve, 0)
            W.make_lo(dve, 1)
            dve.wait_ge(s["dtp"], 1)
            dve.wait_ge(s["row"], 48)
            V.tensor_tensor(dtz, banks[4][:, 0:C * H].rearrange("p (c h) -> p c h", c=C),
                            dtb[:, :].unsqueeze(1).to_broadcast([P, C, H]), ALU.add).then_inc(s["dt"], 1)
            dve.wait_ge(s["dt"], 1)
            V.tensor_scalar(dta, dtz, -1.0, None, ALU.mult).then_inc(s["dt"], 1)
            dve.wait_ge(s["dt"], 2)
            V.tensor_tensor(dta, dta, dtz, ALU.max).then_inc(s["dt"], 1)
            dve.wait_ge(s["e1"], 3)
            V.scalar_tensor_tensor(dt[:, :, :], dtz, 0.0, dta, ALU.max, ALU.add).then_inc(s["dt"], 1)
            dve.wait_ge(s["dt"], 4)
            V.scalar_tensor_tensor(adt[:, :, :], dt[:, :, :], -1.0, al[:, :].unsqueeze(1).to_broadcast([P, C, H]), ALU.mult,
                                   ALU.mult).then_inc(s["dt"], 1)
            dve.wait_ge(s["e2"], 1)
            V.tensor_copy(acs[:, :, :], banks[5][:, 0:C * H].rearrange("p (c h) -> p c h", c=C)).then_inc(s["acs"], 1)
            dve.wait_ge(s["acs"], 1)
            dve.wait_ge(s["pad"], 1)
            chain = [0]

            def normed(n):
                dve.wait_ge(s["rt"], n + 1)
                V.reciprocal(rs[:, :], rt[:, :]).then_inc(s["rs"], 1)
                dve.wait_ge(s["rs"], n + 1)
                V.tensor_tensor(y[:, :, :], y[:, :, :], rs[:, :].unsqueeze(2).to_broadcast([P, C, GW]), ALU.mult).then_inc(s["yn"], 1)

            W.make_lo(dve, 2)
            W.make_lo(dve, 3)
            for n in range(G):
                more = n + 1 < G
                for j in range(2):
                    dve.wait_ge(s["pc"], 4 * n + j + 1)
                    if n >= 1:
                        dve.wait_ge(s["tx"], 2 * n)
                    taps(dve, chain, n, j)
                if n >= 1:
                    normed(n - 1)
                dve.wait_ge(s["ar"], 16 * n + 16)
                if n >= 1:
                    dve.wait_ge(s["xde"], n)
                a_s = acs[:, :, n * R:n * R + R].rearrange("p c r -> p r c")
                V.tensor_tensor(dte[:, :, :].rearrange("p c r -> p r c"), A[:, :, P - 1:T:P], a_s, ALU.subtract).then_inc(s["dtd"], 1)
                dve.wait_ge(s["eal"], n + 1)
                dve.wait_ge(s["dtd"], n + 1)
                A4 = A[:, :, :].rearrange("p r (c l) -> p r c l", c=C)
                V.tensor_tensor(A4, A4, a_s.unsqueeze(3).to_broadcast([P, R, C, P]), ALU.subtract).then_inc(s["seg"], 1)
                dve.wait_ge(s["seg"], 2 * n + 1)
                V.tensor_scalar(A[:, :, :], A[:, :, :], 0.0, None, ALU.min).then_inc(s["seg"], 1)
                if more:
                    W.make_lo(dve, 3 * n + 4)
                dve.wait_ge(s["cb"], n + 1)
                if n >= 1:
                    dve.wait_ge(s["A"], n)
                V.tensor_tensor(cbm[:, :, :], banks[7].rearrange("p (c l) -> p c l", c=C),
                                tri[:, :].unsqueeze(1).to_broadcast([P, C, P]), ALU.mult).then_inc(s["cbm"], 1)
                dve.wait_ge(s["xn"], 2 * n + 2)
                if n >= 1:
                    dve.wait_ge(s["yd"], 2 * n)
                    dve.wait_ge(s["stp"], 2 * n)
                V.tensor_tensor(heads(xdt), heads(x_nat), by_head(dt, n), ALU.mult).then_inc(s["xdt"], 1)
                dve.wait_ge(s["xdt"], n + 1)
                dve.wait_ge(s["dte"], n + 1)
                V.tensor_tensor(heads(xde), heads(xdt), dte[:, :, :].unsqueeze(3).to_broadcast([P, C, R, SSM_HD]),
                                ALU.mult).then_inc(s["xde"], 1)
                dve.wait_ge(s["ex"], n + 1)
                dve.wait_ge(s["cbm"], n + 1)
                V.tensor_tensor(A[:, :, :], A[:, :, :], cbm[:, :, :].rearrange("p c l -> p (c l)").unsqueeze(1)
                                .to_broadcast([P, R, T]), ALU.mult).then_inc(s["A"], 1)
                if more:
                    W.make_lo(dve, 3 * n + 5)
                if n >= 1:
                    dve.wait_ge(s["yo"], 2 * n)
                for c in range(1, C):
                    dve.wait_ge(s["stp"], 2 * n + (1 if c < 3 else 2))
                    b = banks[6][:, (c - 1) * GW:c * GW] if c < 3 else banks[7][:, 0:GW]
                    if c == 1:
                        V.tensor_copy(st[:, 1, :], b).then_inc(s["stc"], 1)
                    else:
                        dve.wait_ge(s["stc"], 3 * n + c - 1)
                        for r in range(R):
                            q = slice(r * SSM_HD, r * SSM_HD + SSM_HD)
                            last = V.scalar_tensor_tensor(st[:, c, q], st[:, c - 1, q], eal[:, r, c - 1:c], b[:, q], ALU.mult, ALU.add)
                        last.then_inc(s["stc"], 1)
                for j in range(2):
                    dve.wait_ge(s["yd"], 2 * n + j + 1)
                    dve.wait_ge(s["xd"], n + 1)
                    yj = y[:, 2 * j:2 * j + 2, :]
                    V.tensor_tensor(yj, yj, banks[4 + j].rearrange("p (c d) -> p c d", c=2), ALU.add).then_inc(s["t0"], 1)
                dve.wait_ge(s["yo"], 2 * n + 2)
                e4 = by_head(eacs, n)
                V.tensor_tensor(heads(yo)[:, 1, :, :], banks[2][:, GW:2 * GW].rearrange("p (r d) -> p r d", r=R), e4[:, 1, :, :],
                                ALU.mult).then_inc(s["t0"], 1)
                V.tensor_tensor(heads(yo)[:, 2:4, :, :], banks[3].rearrange("p (c r d) -> p c r d", c=2, r=R), e4[:, 2:4, :, :],
                                ALU.mult).then_inc(s["yr"], 1)
                dve.wait_ge(s["t0"], 4 * n + 3)
                dve.wait_ge(s["yr"], n + 1)
                V.tensor_tensor(y[:, 1:C, :], y[:, 1:C, :], yo[:, 1:C, :], ALU.add).then_inc(s["t0"], 1)
                dve.wait_ge(s["t0"], 4 * n + 4)
                dve.wait_ge(s["zs"], 2 * n + 2)
                V.tensor_tensor(y[:, :, :], y[:, :, :], zs[:, :, :], ALU.mult).then_inc(s["yt"], 1)
                if more and 3 * n + 6 < NU:
                    W.make_lo(dve, 3 * n + 6)
            normed(G - 1)

        @block.tensor
        def _(pe):
            mm = nc.tensor.matmul

            def unit(n, j):
                u = 3 * n + j
                pe.wait_ge(W.s_lo, u + 1)
                if j < 2:
                    for v in range(2):
                        product(nc, pe, W, u, v, banks[2 * j + v], hT)
                    return
                hi, lo = W.halves(u, KD)
                for i in range(C):
                    for k in range(KD):
                        t = slice(i * P, i * P + P)
                        last = split_mm(nc, banks[i // 2][:, (i % 2) * GW:(i % 2 + 1) * GW], hT[0][:, k, t], hT[1][:, k, t], hi[:, k, :],
                                        lo[:, k, :], k == 0, k == KD - 1)
                    if i % 2:
                        last.then_inc(W.out, 1)

            def turn_out(n):
                pe.wait_ge(s["yn"], n + 1)
                pe.wait_ge(s["stc"], 3 * n + 3)
                for j in range(2):
                    for c in range(C):
                        last = nc.tensor.transpose(banks[6 + j][:, c * P:c * P + P], y[:, c, j * P:j * P + P], ident[:, :])
                    last.then_inc(s["ty"], 1)

            pe.wait_ge(s["wdl"], 1)
            for i in range(C):
                for k in range(KD):
                    t = slice(i * P, i * P + P)
                    last = split_mm(nc, banks[4][:, i * H:i * H + H], hT[0][:, k, t], hT[1][:, k, t], wdh[:, k, :], wdl[:, k, :],
                                    k == 0, k == KD - 1)
            last.then_inc(s["dtp"], 1)
            unit(0, 0)
            unit(0, 1)
            pe.wait_ge(s["dt"], 5)
            for c in range(C):
                last = mm(banks[5][:, c * H:c * H + H], tri[:, :], adt[:, c, :], start=True, stop=True)
            for c in range(C):
                last = mm(banks[6][0:H, c * P:c * P + P], adt[:, c, :], tri[:, :], start=True, stop=True)
            last.then_inc(s["acp"], 1)
            pe.wait_ge(s["pc"], 2)
            unit(0, 2)
            for n in range(G):
                more = n + 1 < G
                if more:
                    pe.wait_ge(s["zs"], 2 * n + 2)
                    unit(n + 1, 0)
                if n >= 1:
                    turn_out(n - 1)
                pe.wait_ge(s["sl"], 4 * n + 2)
                if n >= 1:
                    pe.wait_ge(s["yr"], n)
                else:
                    pe.wait_ge(s["acs"], 1)
                    pe.wait_ge(s["acT"], 1)
                for j in range(2):
                    for c in (2 * j, 2 * j + 1):
                        for d in range(2):
                            o = (c % 2) * GW + d * P
                            last = nc.tensor.transpose(banks[4 + j][:, o:o + P], xbc[:, d, c * P:c * P + P], ident[:, :])
                    last.then_inc(s["tx"], 1)
                pe.wait_ge(s["sl"], 4 * n + 4)
                if n >= 1:
                    pe.wait_ge(s["ye"], 2 * n)
                for c in range(C):
                    last = nc.tensor.transpose(banks[6][:, c * P:c * P + P], xbc[:, 2, c * P:c * P + P], ident[:, :])
                last.then_inc(s["tb"], 1)
                for c in range(C):
                    t = slice(c * P, c * P + P)
                    last = mm(banks[7][:, t], xbc[:, 2, t], xbc[:, 3, t], start=True, stop=True)
                last.then_inc(s["cb"], 1)
                if more:
                    if n >= 1:
                        pe.wait_ge(s["yr"], n)
                    unit(n + 1, 1)
                pe.wait_ge(s["xde"], n + 1)
                pe.wait_ge(s["bn"], n + 1)
                pe.wait_ge(s["cbm"], n + 1)
                for c in range(3):
                    o = banks[6][:, c * GW:c * GW + GW] if c < 2 else banks[7][:, 0:GW]
                    last = mm(o, b_nat[:, c, :], xde[:, c, :], start=True, stop=True)
                    if c >= 1:
                        last.then_inc(s["stp"], 1)
                if more:
                    pe.wait_ge(s["pc"], 4 * n + 6)
                    unit(n + 1, 2)
                pe.wait_ge(s["A"], n + 1)
                for c in range(C):
                    for r in range(R):
                        q = slice(r * SSM_HD, r * SSM_HD + SSM_HD)
                        o = (c % 2) * GW + r * SSM_HD
                        last = mm(banks[4 + c // 2][:, o:o + SSM_HD], A[:, r, c * P:c * P + P], xdt[:, c, q], start=True, stop=True)
                    if c % 2:
                        last.then_inc(s["yd"], 1)
                pe.wait_ge(s["stc"], 3 * n + 3)
                pe.wait_ge(s["pc"], 4 * (n + 1) + 4 if more else 4 * n + 4)
                for c in range(1, C):
                    o = (c % 2) * GW
                    last = mm(banks[2 + c // 2][:, o:o + GW], xbc[:, 3, c * P:c * P + P], st[:, c, :], start=True, stop=True)
                    if c % 2:
                        last.then_inc(s["yo"], 1)
            turn_out(G - 1)
    g["clear"](s, W.sems())


def mix(nc, dram, g, sem, banks, hT, yT):
    h, eps, ident = g["h"], g["eps"], g["ident"]
    mixT = g["mixed"][:, :, :].rearrange("p i d -> p (i d)").rearrange("p (c t) -> p c t", c=KD)
    mm_nat = g["mixed"]
    w = dram["w_in_2"][0].rearrange("(k p) c -> p k c", p=P)
    w_so = dram["ssm_out_w_2"][0].rearrange("(k p) c -> p k c", p=P)
    w_out = dram["w_out_2"][0].rearrange("(k p) c -> p k c", p=P)
    KY = D_INNER // P
    SO, WO = 4, 4 + KY // 2
    sources = ([columns(w, OFF_GATE + D + 2 * n * P, OFF_GATE + D + (2 * n + 1) * P, P) for n in range(4)]
               + [rows(w_so, 2 * n, 2, 0, D) for n in range(KY // 2)]
               + [rows(w_out, 4 * half, 4, 512 * n, 512) for n in range(2) for half in range(2)])
    NU = len(sources)
    s = {n: sem("m_" + n) for n in "gate yh yl gm mx mh ml cp gpo gpr ssq rt rs pn x xn tr hi lo".split()}

    def col(name, n):
        return g["cols"][:, VEC_AT[name] + n:VEC_AT[name] + n + 1]

    with ExitStack() as tmp:
        def sb(name, shape, dt=F32):
            return tmp.enter_context(nc.sbuf_tensor(name, shape, dt))

        W = Weights(nc, sem, sb, "m", sources, [sb(f"raw_m{i}", [P, UNIT])[:, :] for i in range(3)])
        gs = sb("gs", [P, KD, T])
        yh = [sb(f"yh{i}", [P, 2, T], F32R) for i in range(2)]
        yl = [sb(f"yl{i}", [P, 2, T], F32R) for i in range(2)]
        gpo, gpr = sb("gpo", [P, D]), sb("gpr", [P, D])
        xn = [gs[:, 2 * i:2 * i + 2, :].rearrange("p c t -> p (c t)") for i in range(2)]
        sq = gs[:, 4:6, :].rearrange("p c t -> p (c t)")
        ssq, rt, rs = (sb(n, [P, 2 * NT]) for n in ("ssq_m", "rt_m", "rs_m"))
        block = tmp.enter_context(nc.Block())

        @block.sync
        def _(sp):
            for u in range(NU):
                W.load(sp, u)

        @block.scalar
        def _(act):
            act.dma_start(gpo[:, :], dram["mix_post_g_2"][0].partition_broadcast(P)).then_inc(s["gpo"], 16)
            act.dma_start(gpr[:, :], dram["ffn_pre_g_2"][0].partition_broadcast(P)).then_inc(s["gpr"], 16)

            def y_hi(n):
                if n >= 2:
                    act.wait_ge(W.out, 2 * (SO + n - 1))
                nc.scalar.copy(yh[n % 2][:, :, :], yT[:, 2 * n:2 * n + 2, :]).then_inc(s["yh"], 1)

            W.make_hi(act, 0)
            W.make_hi(act, 1)
            y_hi(0)
            y_hi(1)
            for u in range(SO):
                for j in range(2):
                    n = 2 * u + j
                    act.wait_ge(W.out, 2 * u + j + 1)
                    nc.scalar.activation(gs[:, n, :], banks[n], ACT.Sigmoid, bias=col("gate_b", KD + n)).then_inc(s["gate"], 1)
                W.make_hi(act, u + 2)
            for n in range(KY // 2):
                W.make_hi(act, SO + n + 2)
                if n + 2 < KY // 2:
                    y_hi(n + 2)
            for n in range(KD):
                act.wait_ge(s["mx"], n + 1)
                nc.scalar.copy(hT[0][:, n, :], mixT[:, n, :]).then_inc(s["mh"], 1)
            W.make_hi(act, WO + 2)
            W.make_hi(act, WO + 3)
            for i in range(NT + 1):
                if i < NT:
                    act.wait_ge(s["cp"], NT + i + 1)
                    rms_root(nc, act, s, 2 * i, mm_nat[:, i, :], sq, ssq[:, 2 * i:2 * i + 1], rt[:, 2 * i:2 * i + 1], eps)
                    act.wait_ge(s["x"], i + 1)
                    rms_root(nc, act, s, 2 * i + 1, h[:, i, :], sq, ssq[:, 2 * i + 1:2 * i + 2],
                             rt[:, 2 * i + 1:2 * i + 2], eps)
                if i >= 1:
                    turned_hi(nc, act, s, i - 1, banks, hT[0])

        @block.vector
        def _(dve):
            V = nc.vector

            def y_lo(n):
                dve.wait_ge(s["yh"], n + 1)
                V.tensor_tensor(yl[n % 2][:, :, :], yT[:, 2 * n:2 * n + 2, :], yh[n % 2][:, :, :].bitcast(F32),
                                ALU.subtract).then_inc(s["yl"], 1)

            W.make_lo(dve, 0)
            W.make_lo(dve, 1)
            y_lo(0)
            y_lo(1)
            for u in range(2, SO + 2):
                W.make_lo(dve, u)
            for n in range(KY // 2):
                W.make_lo(dve, SO + n + 2)
                if n + 2 < KY // 2:
                    y_lo(n + 2)
            for n in range(KD):
                dve.wait_ge(W.out, 2 * WO - 1 if n < KD // 2 else 2 * WO)
                V.tensor_tensor(gs[:, n, :], gs[:, n, :], banks[n], ALU.mult).then_inc(s["gm"], 1)
                dve.wait_ge(s["gm"], n + 1)
                V.tensor_tensor(mixT[:, n, :], mixT[:, n, :], gs[:, n, :], ALU.add).then_inc(s["mx"], 1)
            for n in range(KD):
                dve.wait_ge(s["mh"], n + 1)
                V.tensor_tensor(hT[1][:, n, :], mixT[:, n, :], hT[0][:, n, :].bitcast(F32), ALU.subtract).then_inc(s["ml"], 1)
            W.make_lo(dve, WO + 2)
            W.make_lo(dve, WO + 3)
            dve.wait_ge(s["ml"], KD)
            for n in range(2):
                for i in range(NT):
                    dve.wait_ge(W.out, 2 * (WO + 2 * n + 1) + (1 if i < 2 else 2))
                    V.tensor_copy(mm_nat[:, i, 512 * n:512 * n + 512], banks[2 * i + n]).then_inc(s["cp"], 1)
            dve.wait_ge(s["gpo"], 16)
            dve.wait_ge(s["gpr"], 16)
            for i in range(NT):
                rms_scale(nc, dve, s, 2 * i, rt[:, 2 * i:2 * i + 1], rs[:, 2 * i:2 * i + 1])
                V.scalar_tensor_tensor(mm_nat[:, i, :], mm_nat[:, i, :], rs[:, 2 * i:2 * i + 1], gpo[:, :], ALU.mult,
                                       ALU.mult).then_inc(s["pn"], 1)
                dve.wait_ge(s["pn"], i + 1)
                V.tensor_tensor(h[:, i, :], h[:, i, :], mm_nat[:, i, :], ALU.add).then_inc(s["x"], 1)
                if i >= 1:
                    turned_lo(nc, dve, s, i - 1, banks, *hT)
                rms_scale(nc, dve, s, 2 * i + 1, rt[:, 2 * i + 1:2 * i + 2], rs[:, 2 * i + 1:2 * i + 2])
                dve.wait_ge(s["x"], i + 1)
                if i >= 2:
                    dve.wait_ge(s["tr"], 2 * (i - 1))
                V.scalar_tensor_tensor(xn[i % 2], h[:, i, :], rs[:, 2 * i + 1:2 * i + 2], gpr[:, :], ALU.mult,
                                       ALU.mult).then_inc(s["xn"], 1)
            turned_lo(nc, dve, s, NT - 1, banks, *hT)

        @block.tensor
        def _(pe):
            for u in range(SO):
                pe.wait_ge(W.s_lo, u + 1)
                for j in range(2):
                    product(nc, pe, W, u, j, banks[2 * u + j], hT)
            pe.wait_ge(s["gate"], KD)
            for n in range(KY // 2):
                u = SO + n
                pe.wait_ge(W.s_lo, u + 1)
                pe.wait_ge(s["yl"], n + 1)
                hi, lo = W.halves(u, 2)
                for c in range(KD):
                    for k in range(2):
                        last = split_mm(nc, banks[c], hi[:, k, c * P:c * P + P], lo[:, k, c * P:c * P + P], yh[n % 2][:, k, :],
                                        yl[n % 2][:, k, :], n == 0 and k == 0, n == KY // 2 - 1 and k == 1)
                    if c % 4 == 3:
                        last.then_inc(W.out, 1)
            pe.wait_ge(s["ml"], KD)
            for n in range(2):
                for half in range(2):
                    u = WO + 2 * n + half
                    pe.wait_ge(W.s_lo, u + 1)
                    hi, lo = W.halves(u, 4)
                    for i in range(NT):
                        t = slice(i * P, i * P + P)
                        for k in range(4):
                            kk = 4 * half + k
                            last = split_mm(nc, banks[2 * i + n], hT[0][:, kk, t], hT[1][:, kk, t], hi[:, k, :], lo[:, k, :],
                                            kk == 0, kk == KD - 1)
                        if i % 2:
                            last.then_inc(W.out, 1)
            pe.wait_ge(s["cp"], 2 * NT)
            for i in range(NT):
                turn_rows(nc, pe, s, i, xn[i % 2], banks, ident)
    g["clear"](s, W.sems())


def ffn(nc, dram, g, sem, banks, hT, out):
    h, eps = g["h"], g["eps"]
    KH = HIDDEN // P
    w_gu = dram["w_gate_up_2"][0].rearrange("(k p) c -> p k c", p=P)
    w_down = dram["w_down_2"][0].rearrange("(k p) c -> p k c", p=P)
    sources = ([columns(w_gu, c * P, HIDDEN + c * P, P) for c in range(KH)]
               + [rows(w_down, 2 * n, 2, 0, D) for n in range(KH // 2)])
    NU = len(sources)
    out_t = out[0].rearrange("(i p) d -> p i d", p=P)
    s = {n: sem("g_" + n) for n in "gpo sg hd hi lo ssq sum rt rs pn x stored".split()}
    with ExitStack() as tmp:
        def sb(name, shape, dt=F32):
            return tmp.enter_context(nc.sbuf_tensor(name, shape, dt))

        spare = g["mixed"]
        raw = [spare[:, 2 * i:2 * i + 2, :].rearrange("p a d -> p (a d)") for i in range(2)] + [sb("raw_g", [P, UNIT])[:, :]]
        W = Weights(nc, sem, sb, "g", sources, raw)
        hid = [sb(n, [P, KH, T], F32R) for n in ("hid_hi", "hid_lo")]
        sg = sb("sg_g", [P, T])
        hd = sb("hd", [P, T])
        gpo, sq = sb("gpo_g", [P, D]), hd
        ssq = sb("ssq_g", [P, NT, 2])
        sums, rt, rs = (sb(n, [P, NT]) for n in ("sums_g", "rt_g", "rs_g"))
        block = tmp.enter_context(nc.Block())

        @block.sync
        def _(sp):
            for u in range(NU):
                W.load(sp, u)
            for i in range(NT):
                sp.wait_ge(s["x"], i + 1)
                sp.dma_start(out_t[:, i, :], h[:, i, :]).then_inc(s["stored"], 16)
            sp.wait_ge(s["stored"], 16 * NT)

        @block.scalar
        def _(act):
            act.dma_start(gpo[:, :], dram["ffn_post_g_2"][0].partition_broadcast(P)).then_inc(s["gpo"], 16)
            W.make_hi(act, 0)
            W.make_hi(act, 1)
            for c in range(KH):
                act.wait_ge(W.out, 2 * c + 1)
                if c >= 1:
                    act.wait_ge(s["hd"], c)
                nc.scalar.activation(sg[:, :], banks[2 * c % 8], ACT.Silu).then_inc(s["sg"], 1)
                W.make_hi(act, c + 2)
                act.wait_ge(s["hd"], c + 1)
                nc.scalar.copy(hid[0][:, c, :], hd[:, :]).then_inc(s["hi"], 1)
            for u in range(KH + 2, NU):
                W.make_hi(act, u)
            act.wait_ge(s["lo"], KH)
            for i in range(NT):
                act.wait_ge(W.out, 2 * NU - 1 if i < 2 else 2 * NU)
                for half in range(2):
                    if i or half:
                        act.wait_ge(s["ssq"], 2 * i + half)
                    nc.scalar.activation(sq[:, :], banks[2 * i + half], ACT.Square,
                                         accum_out=ssq[:, i, half:half + 1]).then_inc(s["ssq"], 1)
                act.wait_ge(s["sum"], i + 1)
                nc.scalar.activation(rt[:, i:i + 1], sums[:, i:i + 1], ACT.Sqrt, bias=eps[:, 0:1], scale=1.0 / D).then_inc(s["rt"], 1)

        @block.vector
        def _(dve):
            V = nc.vector
            W.make_lo(dve, 0)
            W.make_lo(dve, 1)
            for c in range(KH):
                dve.wait_ge(W.out, 2 * c + 2)
                dve.wait_ge(s["sg"], c + 1)
                if c >= 1:
                    dve.wait_ge(s["lo"], c)
                V.tensor_tensor(hd[:, :], sg[:, :], banks[(2 * c + 1) % 8], ALU.mult).then_inc(s["hd"], 1)
                W.make_lo(dve, c + 2)
                dve.wait_ge(s["hi"], c + 1)
                V.tensor_tensor(hid[1][:, c, :], hd[:, :], hid[0][:, c, :].bitcast(F32), ALU.subtract).then_inc(s["lo"], 1)
            for u in range(KH + 2, NU):
                W.make_lo(dve, u)
            dve.wait_ge(W.s_lo, NU)
            dve.wait_ge(s["gpo"], 16)
            for i in range(NT):
                dve.wait_ge(s["ssq"], 2 * i + 2)
                V.tensor_tensor(sums[:, i:i + 1], ssq[:, i, 0:1], ssq[:, i, 1:2], ALU.add).then_inc(s["sum"], 1)
                rms_scale(nc, dve, s, i, rt[:, i:i + 1], rs[:, i:i + 1])
                for half in range(2):
                    c = slice(512 * half, 512 * half + 512)
                    V.scalar_tensor_tensor(spare[:, i, c], banks[2 * i + half], rs[:, i:i + 1], gpo[:, c], ALU.mult,
                                           ALU.mult).then_inc(s["pn"], 1)
                dve.wait_ge(s["pn"], 2 * i + 2)
                V.tensor_tensor(h[:, i, :], h[:, i, :], spare[:, i, :], ALU.add).then_inc(s["x"], 1)

        @block.tensor
        def _(pe):
            for u in range(KH):
                pe.wait_ge(W.s_lo, u + 1)
                if u >= 4:
                    pe.wait_ge(s["hd"], u - 3)
                for j in range(2):
                    product(nc, pe, W, u, j, banks[(2 * u + j) % 8], hT)
            pe.wait_ge(s["lo"], KH)
            for n in range(KH // 2):
                u = KH + n
                pe.wait_ge(W.s_lo, u + 1)
                hi, lo = W.halves(u, 2)
                for i in range(NT):
                    t = slice(i * P, i * P + P)
                    for half in range(2):
                        c = slice(512 * half, 512 * half + 512)
                        for k in range(2):
                            kk = 2 * n + k
                            last = split_mm(nc, banks[2 * i + half], hid[0][:, kk, t], hid[1][:, kk, t], hi[:, k, c], lo[:, k, c],
                                            kk == 0, kk == KH - 1)
                    if i % 2:
                        last.then_inc(W.out, 1)
    g["clear"](s, W.sems())


def build(nc, dram, out):
    with ExitStack() as ctx:
        def sb(name, shape, dt=F32):
            return ctx.enter_context(nc.sbuf_tensor(name, shape, dt))

        def sem(name):
            return nc.alloc_semaphore(name)

        def clear(named, *lists):
            done = list(named.values()) + [x for group in lists for x in group]
            with nc.Block() as block:
                @block.gpsimd
                def _(pool):
                    for x in done:
                        pool.sem_clear(x)
            for x in done:
                if x not in g["gathers"]:
                    nc.release_semaphore(x)

        pall = ctx.enter_context(nc.psum_tensor("pall", [P, 8, BANK], F32))
        banks = [pall[:, b, :] for b in range(8)]
        g = {"h": sb("h", [P, NT, D]), "cols": sb("cols", [P, VEC_COLS]), "ident": sb("ident", [P, P]),
             "ones": sb("ones", [P, P]), "up": sb("up", [P, P]), "tri": sb("tri", [P, P]), "mixed": sb("mixed", [P, NT, D]), "eps": sb("eps", [P, 2]), "pall": pall}
        g["clear"] = clear
        g["gathers"] = []
        g["m_rows"] = nc.dram_tensor("m_rows", [T, D], F32, kind="Internal").ap()
        g["y_rows"] = nc.dram_tensor("y_rows", [2 * T, D], F32, kind="Internal").ap()
        g["acs_rows"] = nc.dram_tensor("acs_rows", [SSM_HEADS, T], F32, kind="Internal").ap()
        g["gate"] = [sb(f"gate{k}", [P, NT]) for k in range(2)]
        g["row_x"], g["row_y"] = sb("row_x", [P, NB], U32), sb("row_y", [P, NB], U32)
        g["over_e"] = sb("over_e", [P, OVER + 1], I32)
        stage_a(nc, dram, g, sem, banks)
        stage_b(nc, dram, g, sem, banks)
        stage_c(nc, dram, g, sem, banks, out)


_INS = ['x', 'meta_tokens', 'lb_logits', 'g_mix', 'w_in', 'sb_gain', 'hg_gain', 'w_out', 'g_ffn', 'w_router_group',
 'b_router_group', 'w_router_expert', 'b_router_expert', 'w_expert_gate', 'w_expert_up', 'w_expert_down', 'g_final',
 'mix_pre_g_2', 'w_in_2', 'gate_b_2', 'glu_b_2', 'conv_dw_w_2', 'conv_dw_b_2', 'conv_ln_g_2', 'conv_ln_b_2',
 'conv_pw_w_2', 'conv_pw_b_2', 'ssm_conv_w_2', 'ssm_conv_b_2', 'dt_bias_2', 'a_log_2', 'd_skip_2', 'ssm_norm_g_2',
 'ssm_out_w_2', 'w_out_2', 'mix_post_g_2', 'ffn_pre_g_2', 'w_gate_up_2', 'w_down_2', 'ffn_post_g_2']
_OUTS = [((1, 512, 1024), 'float32')]


def kernel(**inputs):
    import numpy as _np
    import concourse.bacc as _bacc
    from concourse import mybir as _mybir
    from concourse.bass_utils import run_bass_kernel_spmd as _run

    nc = _bacc.Bacc("TRN2", target_bir_lowering=False, num_devices=1)
    arrays, dram = {}, {}
    for name in _INS:
        a = _np.ascontiguousarray(inputs[name])
        arrays[f"in_{name}_dram"] = a
        dram[name] = nc.dram_tensor(f"in_{name}_dram", a.shape, _mybir.dt.from_np(a.dtype), kind="ExternalInput").ap()
    shape, dtype = _OUTS[0]
    out = nc.dram_tensor("out_0_dram", shape, _mybir.dt.from_np(_np.dtype(dtype)), kind="ExternalOutput").ap()
    build(nc, dram, out)
    r = _run(nc, [arrays], core_ids=[0])
    return r.results[0]["out_0_dram"]
```

```python
from contextlib import ExitStack

import concourse.bass as bass
from concourse import mybir

ALU = mybir.AluOpType
ACT = mybir.ActivationFunctionType
AX = mybir.AxisListType
F32 = mybir.dt.float32
F32R = mybir.dt.float32r
I32 = mybir.dt.int32
U32 = mybir.dt.uint32

P = 128
T = 512
NT = T // P
D = 1024
KD = D // P
META = 16
TM = T + META
BANK = 512
UNIT = 2048
EPS = 1e-6
SB_HEADS, SB_DIM = 8, 64
HG_HEADS, HG_DIM = 4, 128
N_GROUPS, PER_GROUP, N_EXPERTS, FF = 4, 8, 32, 512
SLOTS = 64
OVER = (2 * T - 1) // SLOTS
NB = N_EXPERTS + OVER
CONV_K = 31
SSM_K = 4
SSM_GROUPS, SSM_STATE, SSM_HD, SSM_RANK = 8, 128, 64, 4
SSM_HEADS = SSM_GROUPS * SSM_RANK
D_INNER = 2 * D
OFF_Z = 2 * D
OFF_XBC = OFF_Z + D_INNER
OFF_B = OFF_XBC + D_INNER
OFF_C = OFF_B + SSM_GROUPS * SSM_STATE
OFF_DT = OFF_C + SSM_GROUPS * SSM_STATE
OFF_GATE = OFF_DT + SSM_HEADS
HIDDEN = 2816


def split_mm(nc, out, w_hi, w_lo, m_hi, m_lo, start, stop):
    nc.tensor.matmul(out, w_lo, m_hi, start=start, stop=False)
    nc.tensor.matmul(out, w_hi, m_lo, start=False, stop=False)
    return nc.tensor.matmul(out, w_hi, m_hi, start=False, stop=stop)


VEC_TILES = [
    [("lb", 8), ("sb_gain", 4), ("hg_gain", 4), ("gate_b", 16), ("glu_b", 16), ("dw_b", 8), ("ln_g", 8), ("ln_b", 8),
     ("pw_b", 8), ("ssm_b", 32), ("norm_g", 16)],
    [("dw_w_a", 128)],
    [("dw_w_b", CONV_K * 8 - 128)],
    [("ssm_w", 128)],
]
VEC_AT, VEC_ROWS = {}, []
_at = 0
for _tile in VEC_TILES:
    VEC_ROWS.append(sum(n for _, n in _tile))
    for _name, _n in _tile:
        VEC_AT[_name] = _at
        _at += _n
VEC_COLS = _at


def stage_a(nc, dram, g, sem, banks):
    h, cols, ident, ones, eps = g["h"], g["cols"], g["ident"], g["ones"], g["eps"]
    x_t = dram["x"][0].rearrange("(i p) d -> p i d", p=P)
    w_in = dram["w_in"][0].rearrange("(k p) c -> p k c", p=P)

    with ExitStack() as keep:
        def sb(name, shape, dt=F32, ctx=None):
            return (ctx or keep).enter_context(nc.sbuf_tensor(name, shape, dt))

        qT = sb("qT", [P, 4, T])
        kT = sb("kT", [P, 4, TM])
        v_nat = sb("v_nat", [P, NT + 1, 512])
        hqT = sb("hqT", [P, HG_HEADS, T])
        hfT = sb("hfT", [P, HG_HEADS, TM])
        sgn = sb("sgn", [P, HG_HEADS, TM])
        hv_nat = sb("hv_nat", [P, NT + 1, 512])
        hg_nat = sb("hg_nat", [P, NT, 512])
        lb = sb("lb", [P, HG_HEADS])
        omlb = sb("omlb", [P, HG_HEADS])
        masks = sb("masks", [P, 8, P], I32)

        s = {n: sem("a_" + n) for n in (
            "x meta vec gbc ident ones eps hm0 ssq rt rs xn tr hi lo vtr cols lbd lb whi wlo wused out evac "
            "it xor xf up ge mask".split())}
        s_x = [sem(f"a_x{i}") for i in range(NT)]
        s_raw = [sem(f"a_raw{i}") for i in range(3)]
        with ExitStack() as tmp:
            hm = hv_nat[:, 0:2, :].rearrange("p i d -> p (i d)")
            gbc = hg_nat[:, 0:2, :].rearrange("p i d -> p (i d)")
            sq = sb("sq_a", [P, D], ctx=tmp)
            xn = [sb(f"xn_a{i}", [P, D], ctx=tmp) for i in range(2)]
            ssq, rt, rs = (sb(n, [P, NT + 1], ctx=tmp) for n in ("ssq_a", "rt_a", "rs_a"))
            aT_hi = sb("aT_hi", [P, KD, T + P], F32R, ctx=tmp)
            aT_lo = sb("aT_lo", [P, KD, T + P], F32R, ctx=tmp)
            raw = [g["mixed"][:, 2 * i:2 * i + 2, :].rearrange("p a d -> p (a d)") for i in range(2)]
            raw.append(sb("raw_a", [P, UNIT], ctx=tmp)[:, :])
            whi = [sb(f"whi_a{i}", [P, UNIT], F32R, ctx=tmp) for i in range(2)]
            wlo = [sb(f"wlo_a{i}", [P, UNIT], F32R, ctx=tmp) for i in range(2)]
            vrow = sb("vrow", [P, len(VEC_TILES), P], ctx=tmp)
            s_i = sb("s_i", [P, P], I32, ctx=tmp)
            t_i = sb("t_i", [P, P], I32, ctx=tmp)
            x_i = sb("x_i", [P, P], I32, ctx=tmp)
            x_f = sb("x_f", [P, P], ctx=tmp)
            up_f = g["up"]
            ge_f = sq[:, :].rearrange("p (b t) -> p b t", b=8)
            lbd = sb("lbd", [P, HG_HEADS], ctx=tmp)

            groups = [("q", True), ("k", True), ("v", False), ("hq", True), ("hf", True), ("hi", False), ("hg", False)]
            units = []
            for n, (what, turned) in enumerate(groups):
                for half in range(2):
                    units.append((n, what, turned, half))
            outs, finished = [], []
            RING = 6
            TILES = [0, 1, 2, 3, NT]

            def tiles_of(what):
                return [0, 1, 2, 3] if what == "hg" else [0, 1, 2, 3, 4]

            singles = 0
            for u, (n, what, turned, half) in enumerate(units):
                made = [2 * half, 2 * half + 1] if turned else tiles_of(what) if half else []
                for e in made:
                    singles += e != made[-1]
                    finished.append(("out", singles) if e != made[-1] else ("wused", u + 1))
                    outs.append((what, e))

            def is_meta_turned(what):
                return what in ("k", "hf")

            block = tmp.enter_context(nc.Block())

            @block.sync
            def _(sp):
                for i in range(NT):
                    sp.dma_start(h[:, i, :], x_t[:, i, :]).then_inc(s_x[i], 16)
                for u, (n, what, turned, half) in enumerate(units):
                    if u >= 3:
                        sp.wait_ge(s["wlo"], u - 2)
                    c = n * 512
                    if turned:
                        src = w_in[:, :, c + half * 256:c + half * 256 + 256]
                        dst = raw[u % 3].rearrange("p (k c) -> p k c", k=KD)
                    else:
                        src = w_in[:, half * 4:half * 4 + 4, c:c + 512]
                        dst = raw[u % 3].rearrange("p (k c) -> p k c", k=4)
                    sp.dma_start(dst, src).then_inc(s_raw[u % 3], 16)

            @block.gpsimd
            def _(pool):
                nc.gpsimd.memset(ident[:, :], 0.0).then_inc(s["ident"], 1)
                nc.gpsimd.memset(ones[:, :], 1.0).then_inc(s["ones"], 1)
                nc.gpsimd.memset(eps[:, 0:1], EPS)
                nc.gpsimd.memset(eps[:, 1:2], 1e-5).then_inc(s["eps"], 1)
                pool.wait_ge(s["ident"], 1)
                nc.gpsimd.affine_select(out=ident[:, :], in_=ident[:, :], compare_op=ALU.not_equal, fill=1.0, base=0,
                                        pattern=[[-1, P]], channel_multiplier=1).then_inc(s["ident"], 1)
                nc.gpsimd.iota(s_i[:, :], [[0, P]], 0, 1).then_inc(s["it"], 1)
                nc.gpsimd.iota(t_i[:, :], [[1, P]], 0, 0).then_inc(s["it"], 1)
                pool.wait_ge(s["ones"], 1)
                nc.gpsimd.affine_select(out=up_f[:, :], in_=ones[:, :], compare_op=ALU.is_gt, fill=0.0, base=0,
                                        pattern=[[1, P]], channel_multiplier=-1).then_inc(s["up"], 1)
                nc.gpsimd.affine_select(out=g["tri"][:, :], in_=ones[:, :], compare_op=ALU.is_ge, fill=0.0, base=0,
                                        pattern=[[1, P]], channel_multiplier=-1)

            @block.scalar
            def _(act):
                act.wait_ge(s["hm0"], 1)
                act.dma_start(hm[0:META, :], dram["meta_tokens"]).then_inc(s["meta"], 16)
                act.dma_start(gbc, dram["g_mix"][0].partition_broadcast(P)).then_inc(s["gbc"], 16)
                srcs = {
                    "lb": dram["lb_logits"].rearrange("l (c p) -> (l c) p", p=P),
                    "sb_gain": dram["sb_gain"].rearrange("l (c p) -> (l c) p", p=P),
                    "hg_gain": dram["hg_gain"].rearrange("l (c p) -> (l c) p", p=P),
                    "gate_b": dram["gate_b_2"].rearrange("l (c p) -> (l c) p", p=P),
                    "glu_b": dram["glu_b_2"].rearrange("l (c p) -> (l c) p", p=P),
                    "dw_b": dram["conv_dw_b_2"].rearrange("l (c p) -> (l c) p", p=P),
                    "ln_g": dram["conv_ln_g_2"].rearrange("l (c p) -> (l c) p", p=P),
                    "ln_b": dram["conv_ln_b_2"].rearrange("l (c p) -> (l c) p", p=P),
                    "pw_b": dram["conv_pw_b_2"].rearrange("l (c p) -> (l c) p", p=P),
                    "ssm_b": dram["ssm_conv_b_2"].rearrange("l (c p) -> (l c) p", p=P),
                    "norm_g": dram["ssm_norm_g_2"].rearrange("l (c p) -> (l c) p", p=P),
                    "dw_w_a": dram["conv_dw_w_2"][0].rearrange("k (c p) -> (k c) p", p=P)[0:128],
                    "dw_w_b": dram["conv_dw_w_2"][0].rearrange("k (c p) -> (k c) p", p=P)[128:CONV_K * 8],
                    "ssm_w": dram["ssm_conv_w_2"][0].rearrange("k (c p) -> (k c) p", p=P),
                }
                act.wait_ge(s["eps"], 1)
                for j, i in enumerate(TILES):
                    if i == NT:
                        act.wait_ge(s["meta"], 16)
                    else:
                        act.wait_ge(s_x[i], 16)
                    nc.scalar.activation(sq[:, :], hm if i == NT else h[:, i, :], ACT.Square,
                                         accum_out=ssq[:, i:i + 1]).then_inc(s["ssq"], 1)
                    act.wait_ge(s["ssq"], j + 1)
                    nc.scalar.activation(rt[:, i:i + 1], ssq[:, i:i + 1], ACT.Sqrt, bias=eps[:, 0:1],
                                         scale=1.0 / D).then_inc(s["rt"], 1)
                for t, tile in enumerate(VEC_TILES):
                    at = 0
                    for name, n in tile:
                        act.dma_start(vrow[at:at + n, t, :], srcs[name]).then_inc(s["vec"], 16)
                        at += n
                def make_hi(u):
                    act.wait_ge(s_raw[u % 3], 16 * (u // 3 + 1))
                    if u >= 2:
                        act.wait_ge(s["wused"], u - 1)
                    nc.scalar.copy(whi[u % 2][:, :], raw[u % 3]).then_inc(s["whi"], 1)

                for j, i in enumerate(TILES):
                    for half in range(2):
                        act.wait_ge(s["tr"], 2 * j + half + 1)
                        nc.scalar.copy(aT_hi[:, 4 * half:4 * half + 4, i * P:i * P + P],
                                       banks[6 + half][:, :].rearrange("p (k t) -> p k t", k=4)).then_inc(s["hi"], 1)
                    if 1 <= j < 3:
                        make_hi(j - 1)
                def evacuate(o):
                    what, e = outs[o]
                    name, value = finished[o]
                    act.wait_ge(s[name], value)
                    b = banks[o % RING]
                    if what == "q":
                        last = nc.scalar.activation(qT[:, e, :], b[:, :], ACT.Copy, scale=SB_DIM ** -0.5)
                    elif what == "k":
                        nc.scalar.copy(kT[:, e, META:TM], b[:, :])
                        last = nc.scalar.copy(kT[:, e, 0:META], banks[6 + e % 2][:, 0:META])
                    elif what == "hf":
                        for dst, sign in ((hfT, 1.0), (sgn, -1.0)):
                            nc.scalar.activation(dst[:, e, META:TM], b[:, :], ACT.Sigmoid, scale=sign)
                            last = nc.scalar.activation(dst[:, e, 0:META], banks[6 + e % 2][:, 0:META], ACT.Sigmoid, scale=sign)
                    elif what == "v":
                        last = nc.scalar.copy(v_nat[:, e, :], b[:, :])
                    elif what == "hq":
                        last = nc.scalar.activation(hqT[:, e, :], b[:, :], ACT.Silu)
                    elif what == "hi":
                        last = nc.scalar.copy(hv_nat[:, e, :], b[:, :])
                    else:
                        last = nc.scalar.activation(hg_nat[:, e, :], b[:, :], ACT.Silu)
                    last.then_inc(s["evac"], 1)

                o = 0
                for u, (n, what, turned, half) in enumerate(units):
                    made = 2 if turned else (len(tiles_of(what)) if half else 0)
                    for _ in range(made):
                        evacuate(o)
                        o += 1
                    if u == 0:
                        act.wait_ge(s["lbd"], 1)
                        nc.scalar.activation(lb[:, :], lbd[:, :], ACT.Sigmoid).then_inc(s["lb"], 1)
                        nc.scalar.activation(omlb[:, :], lbd[:, :], ACT.Sigmoid, scale=-1.0).then_inc(s["lb"], 1)
                    if u + 2 < len(units):
                        make_hi(u + 2)

            @block.vector
            def _(dve):
                nc.vector.memset(hm, 0.0).then_inc(s["hm0"], 1)

                def make_lo(u):
                    dve.wait_ge(s["whi"], u + 1)
                    if u >= 2:
                        dve.wait_ge(s["wused"], u - 1)
                    nc.vector.tensor_tensor(wlo[u % 2][:, :], raw[u % 3], whi[u % 2][:, :].bitcast(F32),
                                            ALU.subtract).then_inc(s["wlo"], 1)

                def lower(j, i):
                    for half in range(2):
                        dve.wait_ge(s["hi"], 2 * j + half + 1)
                        nc.vector.tensor_tensor(aT_lo[:, 4 * half:4 * half + 4, i * P:i * P + P],
                                                banks[6 + half][:, :].rearrange("p (k t) -> p k t", k=4),
                                                aT_hi[:, 4 * half:4 * half + 4, i * P:i * P + P].bitcast(F32),
                                                ALU.subtract).then_inc(s["lo"], 1)

                dve.wait_ge(s["gbc"], 16)
                for j, i in enumerate(TILES):
                    dve.wait_ge(s["rt"], j + 1)
                    nc.vector.reciprocal(rs[:, i:i + 1], rt[:, i:i + 1]).then_inc(s["rs"], 1)
                    dve.wait_ge(s["rs"], j + 1)
                    if j >= 2:
                        dve.wait_ge(s["tr"], 2 * (j - 1))
                    nc.vector.scalar_tensor_tensor(xn[j % 2][:, :], hm if i == NT else h[:, i, :], rs[:, i:i + 1],
                                                   gbc, ALU.mult, ALU.mult).then_inc(s["xn"], 1)
                    if j >= 1:
                        lower(j - 1, TILES[j - 1])
                    if j >= 3:
                        make_lo(j - 3)
                lower(4, TILES[4])
                dve.wait_ge(s["vtr"], 1)
                first = sum(VEC_ROWS[:3])
                nc.vector.tensor_copy(cols[:, 0:first], banks[4][:, 0:first])
                nc.vector.tensor_copy(cols[:, first:VEC_COLS], banks[5][:, 0:VEC_ROWS[3]]).then_inc(s["cols"], 1)
                dve.wait_ge(s["cols"], 1)
                a = VEC_AT["lb"]
                nc.vector.tensor_tensor(lbd[:, :], cols[:, a:a + 4], cols[:, a + 4:a + 8],
                                        ALU.subtract).then_inc(s["lbd"], 1)
                dve.wait_ge(s["it"], 2)
                nc.vector.tensor_tensor(x_i[:, :], s_i[:, :], t_i[:, :], ALU.bitwise_xor).then_inc(s["xor"], 1)
                dve.wait_ge(s["xor"], 1)
                nc.vector.tensor_copy(x_f[:, :], x_i[:, :]).then_inc(s["xf"], 1)
                dve.wait_ge(s["xf"], 1)
                dve.wait_ge(s["up"], 1)
                for b in range(8):
                    nc.vector.scalar_tensor_tensor(ge_f[:, b, :], x_f[:, :], float(1 << b), up_f[:, :], ALU.is_ge,
                                                   ALU.mult).then_inc(s["ge"], 1)
                dve.wait_ge(s["ge"], 8)
                for b in range(7):
                    nc.vector.tensor_tensor(masks[:, b, :], ge_f[:, b, :], ge_f[:, b + 1, :], ALU.subtract)
                dve.wait_ge(s["ident"], 2)
                nc.vector.tensor_copy(masks[:, 7, :], ident[:, :]).then_inc(s["mask"], 1)
                for u in range(2, len(units)):
                    make_lo(u)

            @block.tensor
            def _(pe):
                def vectors():
                    pe.wait_ge(s["vec"], 16 * sum(len(t) for t in VEC_TILES))
                    at = 0
                    for t, n in enumerate(VEC_ROWS):
                        dst = banks[4][:, at:at + n] if t < 3 else banks[5][:, 0:n]
                        last = nc.tensor.transpose(dst, vrow[0:n, t, :], ident[0:n, 0:n])
                        at += n
                    last.then_inc(s["vtr"], 1)

                pe.wait_ge(s["ident"], 2)
                for j, i in enumerate(TILES):
                    pe.wait_ge(s["xn"], j + 1)
                    for half in range(2):
                        if j >= 1:
                            pe.wait_ge(s["lo"], 2 * (j - 1) + half + 1)
                        for k in range(4):
                            last = nc.tensor.transpose(banks[6 + half][:, k * P:k * P + P],
                                                       xn[j % 2][:, (4 * half + k) * P:(4 * half + k + 1) * P], ident[:, :])
                        last.then_inc(s["tr"], 1)
                pe.wait_ge(s["lo"], 10)
                o = 0
                for u, (n, what, turned, half) in enumerate(units):
                    if u == 1:
                        vectors()
                    if u == 2:
                        pe.wait_ge(s["cols"], 1)
                    pe.wait_ge(s["wlo"], u + 1)
                    wh, wl = whi[u % 2], wlo[u % 2]
                    if turned:
                        wh = wh[:, :].rearrange("p (k c) -> p k c", k=KD)
                        wl = wl[:, :].rearrange("p (k c) -> p k c", k=KD)
                        for e in range(2):
                            if o >= RING:
                                pe.wait_ge(s["evac"], o - RING + 1)
                            if is_meta_turned(what):
                                if o >= 2:
                                    pe.wait_ge(s["evac"], o - 1)
                            b, bm = banks[o % RING], banks[6 + e]
                            for k in range(KD):
                                a_hi, a_lo = aT_hi[:, k, 0:T], aT_lo[:, k, 0:T]
                                m_hi, m_lo = aT_hi[:, k, T:T + META], aT_lo[:, k, T:T + META]
                                w_h, w_l = wh[:, k, e * P:e * P + P], wl[:, k, e * P:e * P + P]
                                st, sp_ = k == 0, k == KD - 1
                                nc.tensor.matmul(b[:, :], w_l, a_hi, start=st, stop=False)
                                if is_meta_turned(what):
                                    nc.tensor.matmul(bm[:, 0:META], w_l, m_hi, start=st, stop=False)
                                    nc.tensor.matmul(bm[:, 0:META], w_h, m_lo, start=False, stop=False)
                                    nc.tensor.matmul(bm[:, 0:META], w_h, m_hi, start=False, stop=sp_)
                                nc.tensor.matmul(b[:, :], w_h, a_lo, start=False, stop=False)
                                last = nc.tensor.matmul(b[:, :], w_h, a_hi, start=False, stop=sp_)
                            last.then_inc(s["out" if e == 0 else "wused"], 1)
                            o += 1
                    else:
                        wh = wh[:, :].rearrange("p (k c) -> p k c", k=4)
                        wl = wl[:, :].rearrange("p (k c) -> p k c", k=4)
                        for j in tiles_of(what):
                            if half == 0 and o + j >= RING:
                                pe.wait_ge(s["evac"], o + j - RING + 1)
                            for k in range(4):
                                kk = 4 * half + k
                                last = split_mm(nc, banks[(o + j) % RING][:, :], aT_hi[:, kk, j * P:j * P + P],
                                                aT_lo[:, kk, j * P:j * P + P], wh[:, k, :], wl[:, k, :],
                                                kk == 0, kk == KD - 1)
                            if j == tiles_of(what)[-1]:
                                last.then_inc(s["wused"], 1)
                            elif half:
                                last.then_inc(s["out"], 1)
                        if half:
                            o += len(tiles_of(what))

        g["clear"](s, s_x, s_raw)

        HC = HG_HEADS * T
        kx = sb("kx", [P, HG_HEADS, T])
        km = sb("km", [P, HG_HEADS, META])
        lf = hfT
        bx = sb("bx", [P, HC])
        bm = sb("bm", [P, HG_HEADS, META])
        rst = sb("rst", [P, T])
        qz, kz = ([sb(f"{n}{i}", [P, HC]) for i in range(2)] for n in ("qz", "kz"))
        mixed = g["mixed"]
        steps = [(i, hd) for i in range(NT) for hd in range(SB_HEADS)]
        NSTEP = len(steps)
        pall = g["pall"]
        s = {n: sem("b_" + n) for n in (
            "z ab u sp_l sp spm scan lw w wm tr ev evm o oev osq ossq ort ors on ones lf k rst bx".split())}
        with ExitStack() as tmp:
            ab, uu, ll, sp_, cc, lw, ww = ([sb(f"{n}{i}", [P, TM], ctx=tmp) for i in range(2)]
                                           for n in ("ab", "uu", "ll", "sp", "cc", "lw", "ww"))
            wT = [sb(f"wT{i}", [P, NT, P], ctx=tmp) for i in range(2)]
            wTm = [sb(f"wTm{i}", [META, P], ctx=tmp) for i in range(2)]
            one_row = sb("one_row", [P, TM], ctx=tmp)
            o_sb = sb("o_sb", [P, NT, 512], ctx=tmp)
            osq = sb("osq", [P, 512], ctx=tmp)
            ossq, ort, ors = (sb(n, [P, NT, SB_HEADS], ctx=tmp) for n in ("ossq", "ort", "ors"))

            def width(n):
                return META + P * (steps[n][0] + 1)

            def z_of(n):
                b = 2 * (n % 2)
                return pall[:, b:b + 2, :].rearrange("p b n -> p (b n)")[:, 0:width(n)]

            def o_of(n):
                return pall[:, 6 + n % 2, 0:SB_DIM]

            block = tmp.enter_context(nc.Block())

            @block.tensor
            def _(pe):
                def scores(n):
                    i, hd = steps[n]
                    if n >= 2:
                        pe.wait_ge(s["lw"], n - 1)
                    q = qT[64 * (hd % 2):64 * (hd % 2) + 64, hd // 2, i * P:i * P + P]
                    k = kT[64 * (hd % 2):64 * (hd % 2) + 64, hd // 2, :]
                    w = width(n)
                    b = 2 * (n % 2)
                    last = nc.tensor.matmul(pall[:, b, 0:min(w, BANK)], q, k[:, 0:min(w, BANK)], start=True, stop=True)
                    if w > BANK:
                        last = nc.tensor.matmul(pall[:, b + 1, 0:w - BANK], q, k[:, BANK:w], start=True, stop=True)
                    last.then_inc(s["z"], 1)

                def turn(n):
                    i, hd = steps[n]
                    pe.wait_ge(s["wm"], n + 1)
                    if n >= 1:
                        pe.wait_ge(s["ev"], n)
                        pe.wait_ge(s["evm"], n)
                    w = ww[n % 2]
                    nc.tensor.transpose(pall[0:META, 5, 0:P], w[:, 0:META], ident[:, :])
                    for c in range(i + 1):
                        last = nc.tensor.transpose(pall[:, 4, c * P:c * P + P], w[:, META + c * P:META + c * P + P], ident[:, :])
                    last.then_inc(s["tr"], 1)

                def values(n):
                    i, hd = steps[n]
                    pe.wait_ge(s["ev"], n + 1)
                    pe.wait_ge(s["evm"], n + 1)
                    if n >= 2:
                        pe.wait_ge(s["oev"], n - 1)
                    vc = slice(hd * SB_DIM, hd * SB_DIM + SB_DIM)
                    nc.tensor.matmul(o_of(n), wTm[n % 2][:, :], v_nat[0:META, NT, vc], start=True, stop=False)
                    for c in range(i + 1):
                        last = nc.tensor.matmul(o_of(n), wT[n % 2][:, c, :], v_nat[:, c, vc], start=False, stop=c == i)
                    last.then_inc(s["o"], 1)

                for n in range(NSTEP + 3):
                    if n < NSTEP:
                        scores(n)
                    if 2 <= n < NSTEP + 2:
                        turn(n - 2)
                    if n >= 3:
                        values(n - 3)

            @block.scalar
            def _(act):
                def front(n):
                    w = width(n)
                    act.wait_ge(s["z"], n + 1)
                    nc.scalar.activation(ab[n % 2][:, 0:w], z_of(n), ACT.Abs).then_inc(s["ab"], 1)
                    act.wait_ge(s["ab"], n + 1)
                    nc.scalar.activation(uu[n % 2][:, 0:w], ab[n % 2][:, 0:w], ACT.Exp, scale=-1.0).then_inc(s["u"], 1)
                    act.wait_ge(s["u"], n + 1)
                    if n >= 2:
                        act.wait_ge(s["sp"], n - 1)
                    nc.scalar.activation(ll[n % 2][:, 0:w], uu[n % 2][:, 0:w], ACT.Ln, bias=1.0).then_inc(s["sp_l"], 1)

                def weights(n):
                    w = width(n)
                    act.wait_ge(s["lw"], n + 1)
                    if n >= 2:
                        act.wait_ge(s["tr"], n - 1)
                    nc.scalar.activation(ww[n % 2][:, 0:w], lw[n % 2][:, 0:w], ACT.Exp).then_inc(s["w"], 1)

                def evacuate(n):
                    i, hd = steps[n]
                    act.wait_ge(s["tr"], n + 1)
                    if n >= 2:
                        act.wait_ge(s["o"], n - 1)
                    nc.scalar.copy(wT[n % 2][:, 0:i + 1, :],
                                   pall[:, 4, 0:(i + 1) * P].rearrange("p (c t) -> p c t", c=i + 1)).then_inc(s["ev"], 1)

                def log_forget(e):
                    nc.scalar.activation(lf[:, e, :], hfT[:, e, :], ACT.Ln, bias=lb[:, e:e + 1],
                                         scale=omlb[:, e:e + 1]).then_inc(s["lf"], 1)

                nc.scalar.preload_act_table_set("natural_log_exp_and_others")
                for n in range(NSTEP + 2):
                    if n < HG_HEADS:
                        log_forget(n)
                    if n < NSTEP:
                        front(n)
                    if 1 <= n < NSTEP + 1:
                        weights(n - 1)
                    if n >= 2:
                        evacuate(n - 2)
                for i in range(NT):
                    act.wait_ge(s["ossq"], i + 1)
                    nc.scalar.activation(ort[:, i, :], ossq[:, i, :], ACT.Sqrt, bias=eps[:, 0:1],
                                         scale=1.0 / SB_DIM).then_inc(s["ort"], 1)

            @block.gpsimd
            def _(pool):
                def mask_keep(n):
                    w = width(n)
                    pool.wait_ge(s["sp"], n + 1)
                    d = sp_[n % 2][:, w - P:w]
                    nc.gpsimd.affine_select(out=d, in_=d, compare_op=ALU.is_gt, fill=0.0, base=0, pattern=[[-1, P]],
                                            channel_multiplier=1).then_inc(s["spm"], 1)

                def mask_weights(n):
                    w = width(n)
                    pool.wait_ge(s["w"], n + 1)
                    d = ww[n % 2][:, w - P:w]
                    nc.gpsimd.affine_select(out=d, in_=d, compare_op=ALU.is_gt, fill=0.0, base=0, pattern=[[-1, P]],
                                            channel_multiplier=1).then_inc(s["wm"], 1)

                nc.gpsimd.memset(rst[:, :], 1.0).then_inc(s["rst"], 1)
                pool.wait_ge(s["rst"], 1)
                nc.gpsimd.memset(rst[:, 0:T:P], 0.0).then_inc(s["rst"], 1)
                cleared = [t for pair in zip(qz, kz) for t in pair]
                for n in range(NSTEP + 1):
                    if n < NSTEP:
                        mask_keep(n)
                    if n >= 1:
                        mask_weights(n - 1)
                    if n < len(cleared):
                        nc.gpsimd.memset(cleared[n][:, :], 0.0)

            @block.vector
            def _(dve):
                nc.vector.memset(one_row[:, :], 1.0).then_inc(s["ones"], 1)
                dve.wait_ge(s["ones"], 1)

                def softplus(n):
                    w = width(n)
                    dve.wait_ge(s["sp_l"], n + 1)
                    if n >= 2:
                        dve.wait_ge(s["scan"], n - 1)
                    nc.vector.scalar_tensor_tensor(sp_[n % 2][:, 0:w], z_of(n), 0.0, ll[n % 2][:, 0:w], ALU.max,
                                                   ALU.add).then_inc(s["sp"], 1)

                def log_weights(n):
                    w = width(n)
                    dve.wait_ge(s["spm"], n + 1)
                    nc.vector.tensor_tensor_scan(cc[n % 2][:, 0:w][:, ::-1], one_row[:, 0:w], sp_[n % 2][:, 0:w][:, ::-1],
                                                 0.0, ALU.mult, ALU.add).then_inc(s["scan"], 1)
                    dve.wait_ge(s["scan"], n + 1)
                    if n >= 2:
                        dve.wait_ge(s["w"], n - 1)
                    nc.vector.tensor_tensor(lw[n % 2][:, 0:w], z_of(n), cc[n % 2][:, 0:w],
                                            ALU.subtract).then_inc(s["lw"], 1)

                def meta_evacuate(n):
                    dve.wait_ge(s["tr"], n + 1)
                    if n >= 2:
                        dve.wait_ge(s["o"], n - 1)
                    nc.vector.tensor_copy(wTm[n % 2][:, :], pall[0:META, 5, 0:P]).then_inc(s["evm"], 1)

                def out_evacuate(n):
                    i, hd = steps[n]
                    dve.wait_ge(s["o"], n + 1)
                    nc.vector.tensor_copy(o_sb[:, i, hd * SB_DIM:hd * SB_DIM + SB_DIM], o_of(n)).then_inc(s["oev"], 1)

                def square(i):
                    dve.wait_ge(s["oev"], SB_HEADS * (i + 1))
                    nc.vector.tensor_tensor(osq[:, :], o_sb[:, i, :], o_sb[:, i, :], ALU.mult).then_inc(s["osq"], 1)
                    dve.wait_ge(s["osq"], i + 1)
                    nc.vector.tensor_reduce(ossq[:, i, :], osq[:, :].rearrange("p (h d) -> p h d", h=SB_HEADS), AX.X,
                                            ALU.add).then_inc(s["ossq"], 1)

                def decays(e):
                    nc.vector.tensor_scalar(km[:, e, :], sgn[:, e, 0:META], omlb[:, e:e + 1], None, ALU.mult)
                    nc.vector.tensor_scalar(kx[:, e, :], sgn[:, e, META:TM], omlb[:, e:e + 1], None,
                                            ALU.mult).then_inc(s["k"], 1)
                    dve.wait_ge(s["rst"], 2)
                    dve.wait_ge(s["lf"], e + 1)
                    nc.vector.tensor_tensor_scan(bm[:, e, :], ones[:, 0:META], lf[:, e, 0:META], 0.0, ALU.mult, ALU.add)
                    nc.vector.tensor_tensor_scan(bx[:, e * T:e * T + T], rst[:, :], lf[:, e, META:TM], 0.0, ALU.mult,
                                                 ALU.add).then_inc(s["bx"], 1)

                for n in range(NSTEP + 4):
                    if HG_HEADS <= n < 2 * HG_HEADS:
                        decays(n - HG_HEADS)
                    if 1 <= n < NSTEP + 1:
                        log_weights(n - 1)
                    if n < NSTEP:
                        softplus(n)
                    if 2 <= n < NSTEP + 2:
                        meta_evacuate(n - 2)
                    if 4 <= n:
                        out_evacuate(n - 4)
                        if (n - 4) % SB_HEADS == SB_HEADS - 1:
                            square((n - 4) // SB_HEADS)
                for i in range(NT):
                    dve.wait_ge(s["ort"], i + 1)
                    nc.vector.reciprocal(ors[:, i, :], ort[:, i, :]).then_inc(s["ors"], 1)
                    dve.wait_ge(s["ors"], i + 1)
                    nc.vector.tensor_tensor(mixed[:, i, 0:512].rearrange("p (h d) -> p h d", h=SB_HEADS),
                                            o_sb[:, i, :].rearrange("p (h d) -> p h d", h=SB_HEADS),
                                            ors[:, i, :].unsqueeze(2).to_broadcast([P, SB_HEADS, SB_DIM]),
                                            ALU.mult).then_inc(s["on"], 1)

        g["clear"](s)

        s = {n: sem("c_" + n) for n in (
            "scaled d e qz kz sc squares cleared acc be qe kd kdt kdn st stp os ssq rt rs on og".split())}
        with ExitStack() as tmp:
            dd = [sb(f"dd{i}", [P, HC], ctx=tmp) for i in range(2)]
            ee = [sb(f"ee{i}", [P, HC], ctx=tmp) for i in range(2)]
            acc = v_nat[:, 0:NT, :]
            dm = sb("dm", [P, HG_HEADS, META], ctx=tmp)
            em = sb("em", [P, HG_HEADS, META], ctx=tmp)
            kdm = sb("kdm", [P, HG_HEADS, META], ctx=tmp)
            kdn = sb("kdn", [P, 3, HG_HEADS, P], ctx=tmp)
            kdnm = sb("kdnm", [META, HG_HEADS, P], ctx=tmp)
            st = qT[:, :, :].rearrange("p c (e d) -> p c e d", e=HG_HEADS)
            elast = sb("elast", [P, HG_HEADS * NT], ctx=tmp)
            sqo = sb("sqo", [P, 512], ctx=tmp)
            ssq, rt, rs = (sb(n, [P, NT, HG_HEADS], ctx=tmp) for n in ("ssq_c", "rt_c", "rs_c"))
            q_in = hqT[:, :, :].rearrange("p e t -> p (e t)")
            k_in = kx[:, :, :].rearrange("p e t -> p (e t)")
            LEVELS = 7

            def halves(t, lv):
                return t.rearrange("p (n two w) -> p n two w", two=2, w=64 >> lv)

            block = tmp.enter_context(nc.Block())

            @block.scalar
            def _(act):
                for lv in range(LEVELS):
                    act.wait_ge(s["d"], lv + 1)
                    if lv >= 2:
                        act.wait_ge(s["kz"], lv - 1)
                        act.wait_ge(s["qz"], lv - 1)
                    nc.scalar.activation(ee[lv % 2][:, :], dd[lv % 2][:, :], ACT.Exp).then_inc(s["e"], 1)
                act.wait_ge(s["kz"], LEVELS)
                act.wait_ge(s["qz"], LEVELS)
                nc.scalar.activation(ee[1][:, :], bx[:, :], ACT.Exp).then_inc(s["be"], 1)
                act.wait_ge(s["d"], LEVELS + 1)
                nc.scalar.activation(ee[0][:, :], dd[1][:, :], ACT.Exp).then_inc(s["be"], 1)
                nc.scalar.activation(em[:, :, :], dm[:, :, :], ACT.Exp).then_inc(s["be"], 1)
                nc.scalar.activation(elast[:, :], bx[:, :].rearrange("p (n w) -> p n w", w=P)[:, :, P - 1],
                                     ACT.Exp).then_inc(s["be"], 1)
                act.wait_ge(s["kdt"], 1)
                nc.scalar.copy(kdnm[:, :, :], pall[0:META, 0, :].rearrange("p (e d) -> p e d", e=HG_HEADS)).then_inc(s["kdn"], 1)
                for c in range(3):
                    act.wait_ge(s["kdt"], c + 2)
                    nc.scalar.copy(kdn[:, c, :, :], pall[:, 1 + c, :].rearrange("p (e d) -> p e d", e=HG_HEADS)).then_inc(s["kdn"], 1)
                for c in range(NT):
                    act.wait_ge(s["ssq"], c + 1)
                    nc.scalar.activation(rt[:, c, :], ssq[:, c, :], ACT.Sqrt, bias=eps[:, 0:1],
                                         scale=1.0 / HG_DIM).then_inc(s["rt"], 1)

            @block.vector
            def _(dve):

                def exponents(lv):
                    if lv >= 2:
                        dve.wait_ge(s["e"], lv - 1)
                    w = 64 >> lv
                    b, d = halves(bx[:, :], lv), halves(dd[lv % 2][:, :], lv)
                    ref = b[:, :, 0, w - 1:w].to_broadcast([P, HC // (2 * w), w])
                    nc.vector.tensor_tensor(d[:, :, 0, :], ref, b[:, :, 0, :], ALU.subtract)
                    nc.vector.tensor_tensor(d[:, :, 1, :], b[:, :, 1, :], ref, ALU.subtract).then_inc(s["d"], 1)

                def query_factors(lv):
                    dve.wait_ge(s["e"], lv + 1)
                    if lv >= 2:
                        dve.wait_ge(s["sc"], HG_HEADS * (lv - 1))
                    nc.vector.tensor_tensor(halves(qz[lv % 2][:, :], lv)[:, :, 1, :], halves(q_in, lv)[:, :, 1, :],
                                            halves(ee[lv % 2][:, :], lv)[:, :, 1, :], ALU.mult).then_inc(s["qz"], 1)

                def select(n):
                    lv, e = divmod(n, HG_HEADS)
                    dve.wait_ge(s["sc"], n + 1)
                    if n >= HG_HEADS:
                        dve.wait_ge(s["acc"], n - HG_HEADS + 1)
                    nc.vector.copy_predicated(acc[:, e, :].rearrange("p (c t) -> p c t", c=NT),
                                              masks[:, (6 - lv) if lv < 7 else 7, :].unsqueeze(1).to_broadcast([P, NT, P]),
                                              pall[:, n % 8, :].rearrange("p (c t) -> p c t", c=NT)).then_inc(s["acc"], 1)

                exponents(0)
                exponents(1)
                dve.wait_ge(s["cleared"], 1)
                for lv in range(LEVELS):
                    query_factors(lv)
                    if lv + 2 < LEVELS:
                        exponents(lv + 2)
                    if lv >= 1:
                        for e in range(HG_HEADS):
                            select(HG_HEADS * (lv - 1) + e)
                dve.wait_ge(s["e"], LEVELS)
                bc = bx[:, :].rearrange("p (n w) -> p n w", w=P)
                nc.vector.tensor_tensor(dm[:, :, :], bm[:, :, META - 1:META].to_broadcast([P, HG_HEADS, META]), bm[:, :, :],
                                        ALU.subtract)
                nc.vector.tensor_tensor(dd[1][:, :].rearrange("p (n w) -> p n w", w=P),
                                        bc[:, :, P - 1:P].to_broadcast([P, HC // P, P]), bc,
                                        ALU.subtract).then_inc(s["d"], 1)
                for n in range(HG_HEADS * 6, HG_HEADS * 8):
                    select(n)
                dve.wait_ge(s["be"], 4)
                nc.vector.tensor_tensor(qz[0][:, :], q_in, ee[1][:, :], ALU.mult).then_inc(s["qe"], 1)
                nc.vector.tensor_tensor(kdm[:, :, :], km[:, :, :], em[:, :, :], ALU.mult).then_inc(s["kd"], 1)
                nc.vector.tensor_tensor(kz[0][:, :], k_in, ee[0][:, :], ALU.mult).then_inc(s["kd"], 1)
                for c in range(NT):
                    dve.wait_ge(s["stp"], c + 1)
                    b = pall[:, 4 + c % 2, :].rearrange("p (e d) -> p e d", e=HG_HEADS)
                    if c == 0:
                        nc.vector.tensor_copy(st[:, 0, :, :], b).then_inc(s["st"], 1)
                    else:
                        dve.wait_ge(s["st"], c)
                        for e in range(HG_HEADS):
                            last = nc.vector.scalar_tensor_tensor(
                                st[:, c, e, :], st[:, c - 1, e, :], elast[:, e * NT + c - 1:e * NT + c], b[:, e, :], ALU.mult, ALU.add)
                        last.then_inc(s["st"], 1)
                for c in range(NT):
                    o = mixed[:, c, 512:D]
                    dve.wait_ge(s["os"], c + 1)
                    nc.vector.tensor_copy(o, pall[:, 6 + c % 2, :]).then_inc(s["on"], 1)
                    dve.wait_ge(s["on"], c + 1)
                    if c >= 1:
                        dve.wait_ge(s["ssq"], c)
                    nc.vector.tensor_tensor(sqo[:, :], o, o, ALU.mult).then_inc(s["squares"], 1)
                    dve.wait_ge(s["squares"], c + 1)
                    nc.vector.tensor_reduce(ssq[:, c, :], sqo[:, :].rearrange("p (e d) -> p e d", e=HG_HEADS), AX.X,
                                            ALU.add).then_inc(s["ssq"], 1)
                for c in range(NT):
                    o = mixed[:, c, 512:D]
                    dve.wait_ge(s["rt"], c + 1)
                    nc.vector.reciprocal(rs[:, c, :], rt[:, c, :]).then_inc(s["rs"], 1)
                    dve.wait_ge(s["rs"], c + 1)
                    heads = o.rearrange("p (e d) -> p e d", e=HG_HEADS)
                    nc.vector.tensor_tensor(heads, heads, rs[:, c, :].unsqueeze(2).to_broadcast([P, HG_HEADS, P]),
                                            ALU.mult).then_inc(s["scaled"], 1)
                    dve.wait_ge(s["scaled"], c + 1)
                    nc.vector.tensor_tensor(o, o, hg_nat[:, c, :], ALU.mult).then_inc(s["og"], 1)

            @block.gpsimd
            def _(pool):
                nc.gpsimd.memset(acc, 0.0).then_inc(s["cleared"], 1)
                for lv in range(LEVELS):
                    pool.wait_ge(s["e"], lv + 1)
                    if lv >= 2:
                        pool.wait_ge(s["sc"], HG_HEADS * (lv - 1))
                    nc.gpsimd.tensor_tensor(halves(kz[lv % 2][:, :], lv)[:, :, 0, :], halves(k_in, lv)[:, :, 0, :],
                                            halves(ee[lv % 2][:, :], lv)[:, :, 0, :], ALU.mult).then_inc(s["kz"], 1)

            @block.tensor
            def _(pe):
                def products(n):
                    lv, e = divmod(n, HG_HEADS)
                    if lv < LEVELS:
                        pe.wait_ge(s["qz"], lv + 1)
                        pe.wait_ge(s["kz"], lv + 1)
                    ks, qs = (kz[lv % 2][:, :], qz[lv % 2][:, :]) if lv < LEVELS else (k_in, q_in)
                    if n >= 8:
                        pe.wait_ge(s["acc"], n - 7)
                    for c in range(NT):
                        a = e * T + c * P
                        last = nc.tensor.matmul(pall[:, n % 8, c * P:c * P + P], ks[:, a:a + P], qs[:, a:a + P],
                                                start=True, stop=True)
                    last.then_inc(s["sc"], 1)

                for n in range(HG_HEADS * (LEVELS + 1)):
                    products(n)
                pe.wait_ge(s["acc"], HG_HEADS * (LEVELS + 1))
                pe.wait_ge(s["kd"], 1)
                for e in range(HG_HEADS):
                    last = nc.tensor.transpose(pall[0:META, 0, e * P:e * P + P], kdm[:, e, :], ident[:, :])
                last.then_inc(s["kdt"], 1)
                pe.wait_ge(s["kd"], 2)
                for c in range(3):
                    for e in range(HG_HEADS):
                        last = nc.tensor.transpose(pall[:, 1 + c, e * P:e * P + P], kz[0][:, e * T + c * P:e * T + c * P + P],
                                                   ident[:, :])
                    last.then_inc(s["kdt"], 1)
                for c in range(NT):
                    pe.wait_ge(s["kdn"], c + 1)
                    if c >= 2:
                        pe.wait_ge(s["st"], c - 1)
                    for e in range(HG_HEADS):
                        lhs = kdnm[:, e, :] if c == 0 else kdn[:, c - 1, e, :]
                        rhs = hv_nat[0:META, NT, e * P:e * P + P] if c == 0 else hv_nat[:, c - 1, e * P:e * P + P]
                        last = nc.tensor.matmul(pall[:, 4 + c % 2, e * P:e * P + P], lhs, rhs, start=True, stop=True)
                    last.then_inc(s["stp"], 1)
                pe.wait_ge(s["qe"], 1)
                for c in range(NT):
                    pe.wait_ge(s["st"], c + 1)
                    if c >= 2:
                        pe.wait_ge(s["on"], c - 1)
                    for e in range(HG_HEADS):
                        o = pall[:, 6 + c % 2, e * P:e * P + P]
                        a = e * T + c * P
                        nc.tensor.matmul(o, acc[:, e, c * P:c * P + P], hv_nat[:, c, e * P:e * P + P], start=True, stop=False)
                        last = nc.tensor.matmul(o, qz[0][:, a:a + P], st[:, c, e, :], start=False, stop=True)
                    last.then_inc(s["os"], 1)
        g["clear"](s)


BIG = 60000.0


def stage_b(nc, dram, g, sem, banks):
    h, cols, ident, ones, eps, mixed = (g[k] for k in "h cols ident ones eps mixed".split())
    w_out = dram["w_out"][0].rearrange("(k p) c -> p k c", p=P)
    m_rows, y_rows = g["m_rows"], g["y_rows"]
    NR = N_GROUPS + N_EXPERTS

    U = 6
    ex = ExitStack()
    raw_e = [ex.enter_context(nc.sbuf_tensor(f"raw_e{j}", [P, UNIT], F32)) for j in range(U)]
    s_raw_e = [sem(f"e_raw{j}") for j in range(U)]
    w_gate = dram["w_expert_gate"][0].rearrange("e (k p) f -> p e k f", p=P)
    w_up = dram["w_expert_up"][0].rearrange("e (k p) f -> p e k f", p=P)
    w_down = dram["w_expert_down"][0].rearrange("e (k p) f -> p e k f", p=P)

    def unit_source(e, j):
        if j < 4:
            w = w_gate if j < 2 else w_up
            k = 4 * (j % 2)
            return w[:, bass.ds(e, 1), k:k + 4, :].rearrange("p o k f -> p (o k) f")
        k = 2 * (j - 4)
        return w_down[:, bass.ds(e, 1), k:k + 2, :].rearrange("p o k f -> p (o k) f")

    def load(sp, j, of):
        place = raw_e[j][:, :].rearrange("p (k c) -> p k c", k=4 if j < 4 else 2)
        sp.dma_start(place, unit_source(of, j)).then_inc(s_raw_e[j], 16)

    s = {n: sem("d_" + n) for n in (
        "gbc wr rb wrh wrl tr hi lo whi wlo wused out res ssq rt rs xn mtr mhi mlo log io lg mx pe gs v "
        "tab pfx tabf".split())}
    s_raw = [sem(f"d_raw{i}") for i in range(3)]
    s_mrow = [sem(f"d_mrow{i}") for i in range(2)]
    with ExitStack() as tmp:
        def sb(name, shape, dt=F32):
            return tmp.enter_context(nc.sbuf_tensor(name, shape, dt))

        gbc = sb("gbc_d", [P, D])
        mixT_hi, mixT_lo = sb("mixT_hi", [P, KD, T], F32R), sb("mixT_lo", [P, KD, T], F32R)
        raw = raw_e[0:3]
        whi = [sb(f"whi_d{i}", [P, UNIT], F32R) for i in range(2)]
        wlo = [sb(f"wlo_d{i}", [P, UNIT], F32R) for i in range(2)]
        wr = sb("wr", [P, KD, NR])
        wr_hi, wr_lo = sb("wr_hi", [P, KD, NR], F32R), sb("wr_lo", [P, KD, NR], F32R)
        rb = sb("rb", [P, NR])
        sq = sb("sq_d", [P, D])
        xn = [sb(f"xn_d{i}", [P, D]) for i in range(2)]
        ssq, rt, rs = (sb(n, [P, NT]) for n in ("ssq_d", "rt_d", "rs_d"))
        mT_hi = [sb(f"mT_hi{i}", [P, KD, P], F32R) for i in range(2)]
        mT_lo = [sb(f"mT_lo{i}", [P, KD, P], F32R) for i in range(2)]
        lg = sb("lg", [P, NT, NR])
        gpad = sb("gpad", [P, NT, 8])
        gm, tv = sb("gm", [P, NT, 8]), sb("tv", [P, NT, 8])
        gi, ti = sb("gi", [P, NT, 8], U32), sb("ti", [P, NT, 8], U32)
        ngm, gsum, pg = sb("ngm", [P, NT]), sb("gsum", [P, NT]), sb("pg", [P, NT])
        gex = sb("gex", [P, NT, N_GROUPS])
        gidx = sb("gidx", [P, NT])
        oh4 = sb("oh4", [P, NT, N_GROUPS])
        pick = sb("pick", [P, NT, N_GROUPS, PER_GROUP])
        ing = sb("ing", [P, NT, PER_GROUP])
        td, te, tden, trec = (sb(n, [P, NT]) for n in ("td", "te", "tden", "trec"))
        tif = sb("tif", [P, NT, 2])
        eid = [sb(f"eid{k}", [P, NT]) for k in range(2)]
        oh = [sb(f"oh{k}", [P, NT, N_EXPERTS]) for k in range(2)]
        oha = sb("oha", [P, NT, N_EXPERTS])
        iota = sb("iota_f", [P, P])
        arow = [sb(f"arow{k}", [P, NT]) for k in range(2)]
        ohp = sb("ohp", [P, NT, N_EXPERTS])
        rank, over, rin, isov, ovb, blk, blo = ([sb(f"{n}{k}", [P, NT]) for k in range(2)]
                                                for n in ("rank", "over", "rin", "isov", "ovb", "blk", "blo"))
        nov, ovi, ove = (sb(n, [P, N_EXPERTS]) for n in ("nov", "ovi", "ove"))
        cmp = sb("cmp", [P, OVER, N_EXPERTS])
        oexp = sb("oexp", [P, OVER])
        ohr = [sb(f"ohr{i}", [P, P]) for i in range(2 * NT)]
        ohb = [sb(f"ohb{i}", [P, NB]) for i in range(2 * NT)]
        tab, tmiss, trow, txs = (sb(n, [P, NB]) for n in ("tab", "tmiss", "trow", "txs"))

        block = tmp.enter_context(nc.Block())

        @block.sync
        def _(sp):
            for u in range(4):
                if u >= 3:
                    sp.wait_ge(s["wlo"], u - 2)
                n, half = divmod(u, 2)
                sp.dma_start(raw[u % 3][:, :].rearrange("p (k c) -> p k c", k=4),
                             w_out[:, 4 * half:4 * half + 4, n * 512:n * 512 + 512]).then_inc(s_raw[u % 3], 16)
            for j in range(3, U):
                load(sp, j, 0)
            sp.wait_ge(s["wlo"], 4)
            for j in range(3):
                load(sp, j, 0)
            for i in range(NT):
                sp.wait_ge(s["xn"], i + 1)
                sp.dma_start(m_rows[i * P:i * P + P, :], xn[i % 2][:, :]).then_inc(s_mrow[i % 2], 16)
            for x in s_mrow:
                sp.wait_ge(x, 16 * NT // 2)

        @block.gpsimd
        def _(pool):
            nc.gpsimd.iota(iota[:, :], [[1, P]], 0, 0, allow_small_or_imprecise_dtypes=True).then_inc(s["io"], 1)
            for k in range(2):
                nc.gpsimd.iota(arow[k][:, :], [[P, NT]], 1 + k * T, 1, allow_small_or_imprecise_dtypes=True).then_inc(s["io"], 1)
            nc.gpsimd.memset(gpad[:, :, :], -3.0e38).then_inc(s["io"], 1)

        @block.scalar
        def _(act):
            act.dma_start(gbc[:, :], dram["g_ffn"][0].partition_broadcast(P)).then_inc(s["gbc"], 16)
            act.dma_start(wr[:, :, 0:N_GROUPS], dram["w_router_group"][0].rearrange("(k p) c -> p k c", p=P)).then_inc(s["wr"], 16)
            act.dma_start(wr[:, :, N_GROUPS:NR], dram["w_router_expert"][0].rearrange("(k p) c -> p k c", p=P)).then_inc(s["wr"], 16)
            act.dma_start(rb[:, 0:N_GROUPS], dram["b_router_group"][0].partition_broadcast(P)).then_inc(s["rb"], 16)
            act.dma_start(rb[:, N_GROUPS:NR], dram["b_router_expert"][0].partition_broadcast(P)).then_inc(s["rb"], 16)

            def make_hi(u):
                act.wait_ge(s_raw[u % 3], 16 * (u // 3 + 1))
                if u >= 2:
                    act.wait_ge(s["wused"], u - 1)
                nc.scalar.copy(whi[u % 2][:, :], raw[u % 3][:, :]).then_inc(s["whi"], 1)

            for k in range(KD):
                act.wait_ge(s["tr"], k + 1)
                a = VEC_AT["sb_gain"] + k if k < 4 else VEC_AT["hg_gain"] + k - 4
                nc.scalar.activation(mixT_hi[:, k, :], banks[6 + k % 2], ACT.Copy, scale=cols[:, a:a + 1]).then_inc(s["hi"], 1)
            make_hi(0)
            make_hi(1)
            act.wait_ge(s["wr"], 32)
            nc.scalar.copy(wr_hi[:, :, :], wr[:, :, :]).then_inc(s["wrh"], 1)
            make_hi(2)
            make_hi(3)
            for i in range(NT):
                act.wait_ge(s["res"], NT + i + 1)
                nc.scalar.activation(sq[:, :], h[:, i, :], ACT.Square, accum_out=ssq[:, i:i + 1]).then_inc(s["ssq"], 1)
                act.wait_ge(s["ssq"], i + 1)
                nc.scalar.activation(rt[:, i:i + 1], ssq[:, i:i + 1], ACT.Sqrt, bias=eps[:, 0:1],
                                     scale=1.0 / D).then_inc(s["rt"], 1)
            for i in range(NT):
                for half in range(2):
                    act.wait_ge(s["mtr"], 2 * i + half + 1)
                    if i >= 2:
                        act.wait_ge(s["log"], i - 1)
                    nc.scalar.copy(mT_hi[i % 2][:, 4 * half:4 * half + 4, :],
                                   banks[6 + half].rearrange("p (k t) -> p k t", k=4)).then_inc(s["mhi"], 1)
            act.wait_ge(s["mx"], 2)
            for i in range(NT):
                nc.scalar.activation(gex[:, i, :], lg[:, i, 0:N_GROUPS], ACT.Exp, bias=ngm[:, i:i + 1],
                                     accum_out=gsum[:, i:i + 1]).then_inc(s["gs"], 1)
            act.wait_ge(s["v"], 1)
            nc.scalar.activation(te[:, :], td[:, :], ACT.Exp).then_inc(s["pe"], 1)

        @block.vector
        def _(dve):
            def make_lo(u):
                dve.wait_ge(s["whi"], u + 1)
                if u >= 2:
                    dve.wait_ge(s["wused"], u - 1)
                nc.vector.tensor_tensor(wlo[u % 2][:, :], raw[u % 3][:, :], whi[u % 2][:, :].bitcast(F32),
                                        ALU.subtract).then_inc(s["wlo"], 1)

            for k in range(KD):
                dve.wait_ge(s["hi"], k + 1)
                a = VEC_AT["sb_gain"] + k if k < 4 else VEC_AT["hg_gain"] + k - 4
                nc.vector.scalar_tensor_tensor(mixT_lo[:, k, :], banks[6 + k % 2], cols[:, a:a + 1],
                                               mixT_hi[:, k, :].bitcast(F32), ALU.mult, ALU.subtract).then_inc(s["lo"], 1)
            make_lo(0)
            make_lo(1)
            dve.wait_ge(s["wrh"], 1)
            nc.vector.tensor_tensor(wr_lo[:, :, :], wr[:, :, :], wr_hi[:, :, :].bitcast(F32), ALU.subtract).then_inc(s["wrl"], 1)

            def residual(o):
                n, i = divmod(o, NT)
                dve.wait_ge(s["out"] if i < NT - 1 else s["wused"], (NT - 1) * n + i + 1 if i < NT - 1 else 2 * n + 2)
                hh = h[:, i, n * 512:n * 512 + 512]
                nc.vector.tensor_tensor(hh, hh, banks[o % 6], ALU.add).then_inc(s["res"], 1)

            make_lo(2)
            for i in range(NT):
                residual(i)
            make_lo(3)
            for i in range(NT):
                residual(NT + i)
            dve.wait_ge(s["gbc"], 16)

            def lower(i):
                for half in range(2):
                    dve.wait_ge(s["mhi"], 2 * i + half + 1)
                    nc.vector.tensor_tensor(mT_lo[i % 2][:, 4 * half:4 * half + 4, :],
                                            banks[6 + half].rearrange("p (k t) -> p k t", k=4),
                                            mT_hi[i % 2][:, 4 * half:4 * half + 4, :].bitcast(F32),
                                            ALU.subtract).then_inc(s["mlo"], 1)

            for i in range(NT):
                dve.wait_ge(s["rt"], i + 1)
                nc.vector.reciprocal(rs[:, i:i + 1], rt[:, i:i + 1]).then_inc(s["rs"], 1)
                dve.wait_ge(s["rs"], i + 1)
                if i >= 2:
                    dve.wait_ge(s["mtr"], 2 * (i - 1))
                    dve.wait_ge(s_mrow[i % 2], 16 * (i // 2))
                nc.vector.scalar_tensor_tensor(xn[i % 2][:, :], h[:, i, :], rs[:, i:i + 1], gbc[:, :], ALU.mult,
                                               ALU.mult).then_inc(s["xn"], 1)
                if i >= 1:
                    lower(i - 1)
            lower(NT - 1)

            chain = [0]

            def step(ins):
                chain[0] += 1
                ins.then_inc(s["lg"], 1)
                dve.wait_ge(s["lg"], chain[0])

            V = nc.vector
            dve.wait_ge(s["log"], NT)
            dve.wait_ge(s["rb"], 32)
            step(V.tensor_tensor(lg[:, :, :], banks[0][:, 0:NT * NR].rearrange("p (i n) -> p i n", i=NT),
                                 rb[:, :].unsqueeze(1).to_broadcast([P, NT, NR]), ALU.add))
            dve.wait_ge(s["io"], 4)
            step(V.tensor_copy(gpad[:, :, 0:N_GROUPS], lg[:, :, 0:N_GROUPS]))
            for i in range(NT):
                step(V.max(gm[:, i, :], gpad[:, i, :]))
                step(V.max_index(gi[:, i, :], gm[:, i, :], gpad[:, i, :]))
            V.tensor_copy(gidx[:, :], gi[:, :, 0]).then_inc(s["mx"], 1)
            V.tensor_scalar(ngm[:, :], gm[:, :, 0], -1.0, None, ALU.mult).then_inc(s["mx"], 1)
            dve.wait_ge(s["mx"], 1)
            step(V.tensor_tensor(oh4[:, :, :], iota[:, 0:N_GROUPS].unsqueeze(1).to_broadcast([P, NT, N_GROUPS]),
                                 gidx[:, :].unsqueeze(2).to_broadcast([P, NT, N_GROUPS]), ALU.is_equal))
            for i in range(NT):
                last = V.tensor_tensor(pick[:, i, :, :], lg[:, i, N_GROUPS:NR].rearrange("p (g j) -> p g j", g=N_GROUPS),
                                       oh4[:, i, :].unsqueeze(2).to_broadcast([P, N_GROUPS, PER_GROUP]), ALU.mult)
            step(last)
            step(V.tensor_reduce(ing[:, :, :], pick[:, :, :, :].rearrange("p i g j -> p i j g"), AX.X, ALU.add))
            for i in range(NT):
                step(V.max(tv[:, i, :], ing[:, i, :]))
                step(V.max_index(ti[:, i, :], tv[:, i, :], ing[:, i, :]))
            V.tensor_tensor(td[:, :], tv[:, :, 1], tv[:, :, 0], ALU.subtract).then_inc(s["v"], 1)
            step(V.tensor_copy(tif[:, :, :], ti[:, :, 0:2]))
            dve.wait_ge(s["gs"], NT)
            step(V.reciprocal(pg[:, :], gsum[:, :]))
            dve.wait_ge(s["pe"], 1)
            step(V.tensor_scalar(tden[:, :], te[:, :], 1.0, None, ALU.add))
            step(V.reciprocal(trec[:, :], tden[:, :]))
            step(V.tensor_tensor(g["gate"][0][:, :], trec[:, :], pg[:, :], ALU.mult))
            step(V.tensor_tensor(g["gate"][1][:, :], g["gate"][0][:, :], te[:, :], ALU.mult))
            for k in range(2):
                step(V.scalar_tensor_tensor(eid[k][:, :], gidx[:, :], float(PER_GROUP), tif[:, :, k], ALU.mult, ALU.add))
                step(V.tensor_tensor(oh[k][:, :, :], iota[:, 0:N_EXPERTS].unsqueeze(1).to_broadcast([P, NT, N_EXPERTS]),
                                     eid[k][:, :].unsqueeze(2).to_broadcast([P, NT, N_EXPERTS]), ALU.is_equal))
            V.tensor_tensor(oha[:, :, :], oh[0][:, :, :], oh[1][:, :, :], ALU.add).then_inc(s["v"], 1)
            dve.wait_ge(s["pfx"], 1)
            count = banks[1][:, NT * N_EXPERTS:(NT + 1) * N_EXPERTS]
            step(V.tensor_scalar(nov[:, :], count, float(SLOTS + 1), None, ALU.is_ge))
            for o in range(2, T // SLOTS):
                step(V.scalar_tensor_tensor(nov[:, :], count, float(o * SLOTS + 1), nov[:, :], ALU.is_ge, ALU.add))
            step(V.tensor_tensor_scan(ovi[:, :], ones[:, 0:N_EXPERTS], nov[:, :], 0.0, ALU.mult, ALU.add))
            step(V.tensor_tensor(ove[:, :], ovi[:, :], nov[:, :], ALU.subtract))
            step(V.tensor_tensor(cmp[:, :, :], ovi[:, :].unsqueeze(1).to_broadcast([P, OVER, N_EXPERTS]),
                                 iota[:, 0:OVER].unsqueeze(2).to_broadcast([P, OVER, N_EXPERTS]), ALU.is_le))
            step(V.tensor_reduce(oexp[:, :], cmp[:, :, :], AX.X, ALU.add))
            step(V.tensor_scalar(g["over_e"][:, 0:OVER], oexp[:, :], float(N_EXPERTS - 1), None, ALU.min))
            step(V.tensor_copy(g["over_e"][:, OVER:OVER + 1], ovi[:, N_EXPERTS - 1:N_EXPERTS]))
            pfx = banks[1][:, 0:NT * N_EXPERTS].rearrange("p (i e) -> p i e", i=NT)
            for k in range(2):
                step(V.tensor_tensor(ohp[:, :, :], oh[k][:, :, :], pfx, ALU.mult))
                step(V.tensor_reduce(rank[k][:, :], ohp[:, :, :], AX.X, ALU.add))
                step(V.tensor_tensor(ohp[:, :, :], oh[k][:, :, :], ove[:, :].unsqueeze(1).to_broadcast([P, NT, N_EXPERTS]),
                                     ALU.mult))
                step(V.tensor_reduce(ovb[k][:, :], ohp[:, :, :], AX.X, ALU.add))
                step(V.tensor_scalar(isov[k][:, :], rank[k][:, :], float(SLOTS), None, ALU.is_ge))
                step(V.tensor_copy(over[k][:, :], isov[k][:, :]))
                for o in range(2, T // SLOTS):
                    step(V.scalar_tensor_tensor(over[k][:, :], rank[k][:, :], float(o * SLOTS), over[k][:, :], ALU.is_ge, ALU.add))
                step(V.scalar_tensor_tensor(rin[k][:, :], over[k][:, :], -float(SLOTS), rank[k][:, :], ALU.mult, ALU.add))
                step(V.scalar_tensor_tensor(blo[k][:, :], over[k][:, :], float(N_EXPERTS - 1), ovb[k][:, :], ALU.add, ALU.add))
                step(V.tensor_tensor(blo[k][:, :], blo[k][:, :], eid[k][:, :], ALU.subtract))
                step(V.tensor_tensor(blo[k][:, :], blo[k][:, :], isov[k][:, :], ALU.mult))
                step(V.tensor_tensor(blk[k][:, :], blo[k][:, :], eid[k][:, :], ALU.add))
                for i in range(NT):
                    V.tensor_scalar(ohr[NT * k + i][:, :], iota[:, :], rin[k][:, i:i + 1], None, ALU.is_equal)
                    V.tensor_scalar(ohb[NT * k + i][:, :], iota[:, 0:NB], blk[k][:, i:i + 1], arow[k][:, i:i + 1], ALU.is_equal,
                                    ALU.mult).then_inc(s["tab"], 1)
            dve.wait_ge(s["tabf"], 1)
            step(V.tensor_copy(tab[:, :], banks[2][:, 0:NB]))
            step(V.tensor_scalar(tmiss[:, :], tab[:, :], 0.5, BIG, ALU.is_lt, ALU.mult))
            step(V.scalar_tensor_tensor(trow[:, :], tab[:, :], -1.0, tmiss[:, :], ALU.add, ALU.add))
            step(V.tensor_copy(g["row_y"][:, :], trow[:, :]))
            step(V.tensor_scalar(txs[:, :], trow[:, :], float(T), -float(T), ALU.is_ge, ALU.mult))
            step(V.tensor_tensor(txs[:, :], txs[:, :], trow[:, :], ALU.add))
            step(V.tensor_copy(g["row_x"][:, :], txs[:, :]))

        @block.tensor
        def _(pe):
            for k in range(KD):
                if k >= 2:
                    pe.wait_ge(s["lo"], k - 1)
                for i in range(NT):
                    last = nc.tensor.transpose(banks[6 + k % 2][:, i * P:i * P + P], mixed[:, i, k * P:k * P + P], ident[:, :])
                last.then_inc(s["tr"], 1)
            pe.wait_ge(s["lo"], KD)
            for u in range(4):
                n, half = divmod(u, 2)
                pe.wait_ge(s["wlo"], u + 1)
                wh = whi[u % 2][:, :].rearrange("p (k c) -> p k c", k=4)
                wl = wlo[u % 2][:, :].rearrange("p (k c) -> p k c", k=4)
                for i in range(NT):
                    o = NT * n + i
                    if half == 0 and o >= 6:
                        pe.wait_ge(s["res"], o - 5)
                    for k in range(4):
                        kk = 4 * half + k
                        last = split_mm(nc, banks[o % 6], mixT_hi[:, kk, i * P:i * P + P], mixT_lo[:, kk, i * P:i * P + P],
                                        wh[:, k, :], wl[:, k, :], kk == 0, kk == KD - 1)
                    if i == NT - 1:
                        last.then_inc(s["wused"], 1)
                    elif half:
                        last.then_inc(s["out"], 1)
            for i in range(NT + 1):
                if i < NT:
                    pe.wait_ge(s["xn"], i + 1)
                    for half in range(2):
                        if i >= 1:
                            pe.wait_ge(s["mlo"], 2 * (i - 1) + half + 1)
                        for k in range(4):
                            last = nc.tensor.transpose(banks[6 + half][:, k * P:k * P + P],
                                                       xn[i % 2][:, (4 * half + k) * P:(4 * half + k + 1) * P], ident[:, :])
                        last.then_inc(s["mtr"], 1)
                if i >= 1:
                    j = i - 1
                    pe.wait_ge(s["mlo"], 2 * j + 2)
                    if j == 0:
                        pe.wait_ge(s["wrl"], 1)
                        pe.wait_ge(s["res"], 2 * NT)
                    for k in range(KD):
                        last = split_mm(nc, banks[0][:, j * NR:j * NR + NR], mT_hi[j % 2][:, k, :], mT_lo[j % 2][:, k, :],
                                        wr_hi[:, k, :], wr_lo[:, k, :], k == 0, k == KD - 1)
                    last.then_inc(s["log"], 1)
            pe.wait_ge(s["v"], 2)
            E = N_EXPERTS
            for i in range(NT):
                for j in range(i):
                    nc.tensor.matmul(banks[1][:, i * E:i * E + E], ones[:, :], oha[:, j, :], start=j == 0, stop=False)
                nc.tensor.matmul(banks[1][:, i * E:i * E + E], g["up"][:, :], oha[:, i, :], start=i == 0, stop=True)
            for j in range(NT):
                last = nc.tensor.matmul(banks[1][:, NT * E:NT * E + E], ones[:, :], oha[:, j, :], start=j == 0, stop=j == NT - 1)
            last.then_inc(s["pfx"], 1)
            for n in range(2 * NT):
                pe.wait_ge(s["tab"], n + 1)
                last = nc.tensor.matmul(banks[2][:, 0:NB], ohr[n][:, :], ohb[n][:, :], start=n == 0, stop=n == 2 * NT - 1)
            last.then_inc(s["tabf"], 1)
    g["clear"](s, s_raw, s_mrow)

    s = {n: sem("e_" + n) for n in "hi lo used xg0 xg xt xhi xlo sg hid ht hhi hlo ya yd ysc".split()}
    s_raw = s_raw_e
    g["gathers"] += [s["xg"], s["ysc"]]
    with ExitStack() as tmp:
        def sb(name, shape, dt=F32):
            return tmp.enter_context(nc.sbuf_tensor(name, shape, dt))

        raw = raw_e
        whi = [sb(f"whi_e{j}", [P, UNIT], F32R) for j in range(U)]
        wlo = [sb(f"wlo_e{j}", [P, UNIT], F32R) for j in range(U)]
        xg = sb("xg", [P, D])
        xT_hi, xT_lo = sb("xT_hi", [P, KD, P], F32R), sb("xT_lo", [P, KD, P], F32R)
        sg, hid = sb("sg", [P, FF]), sb("hid", [P, FF])
        hT_hi, hT_lo = sb("hT_hi", [P, 4, P], F32R), sb("hT_lo", [P, 4, P], F32R)
        y = sb("y_e", [P, D])
        row_x, row_y = g["row_x"], g["row_y"]
        GATE, UP, XT, HT, Y = banks[0], banks[1], (banks[2], banks[3]), banks[4], (banks[5], banks[6])

        def turned(e):
            return P if isinstance(e, int) and e == 0 else SLOTS

        def k4(t):
            return t[:, :].rearrange("p (k c) -> p k c", k=4)

        def k2(t):
            return t[:, :].rearrange("p (k c) -> p k c", k=2)

        block = tmp.enter_context(nc.Block())

        @block.sync
        def _(sp):
            for j in range(4):
                sp.wait_ge(s["lo"], j + 1)
                load(sp, j, 1)
            with sp.Fori(2, N_EXPERTS) as e:
                for j in range(U):
                    sp.wait_ge(s["lo"], e * U - U + j + 1)
                    load(sp, j, e if j < 4 else e - 1)
            for j in range(4, U):
                sp.wait_ge(s["lo"], N_EXPERTS * U - U + j + 1)
                load(sp, j, N_EXPERTS - 1)

        @block.scalar
        def _(act):
            def hi(e, j):
                act.wait_ge(s_raw[j], e * 16 + 16 if j < 4 else e * 16)
                if not (isinstance(e, int) and (e == 0 or (e == 1 and j >= 4))):
                    act.wait_ge(s["used"], e * U - U + j + 1)
                ins = nc.scalar.copy(whi[j][:, :], raw[j][:, :])
                ins.then_inc(s["hi"], 3 if isinstance(e, int) and e == 0 and j == 3 else 1)

            def x_hi(e):
                for half in range(2):
                    act.wait_ge(s["xt"], e * 2 + half + 1)
                    w = turned(e)
                    nc.scalar.copy(xT_hi[:, 4 * half:4 * half + 4, 0:w],
                                   XT[half].rearrange("p (k t) -> p k t", k=4)[:, :, 0:w]).then_inc(s["xhi"], 1)

            def silu(e):
                act.wait_ge(s["used"], e * U + 2)
                if not isinstance(e, int) or e >= 1:
                    act.wait_ge(s["hid"], e)
                nc.scalar.activation(sg[:, :], GATE, ACT.Silu).then_inc(s["sg"], 1)

            def h_hi(e):
                act.wait_ge(s["ht"], e + 1)
                if not isinstance(e, int) or e >= 1:
                    act.wait_ge(s["used"], e * U + U)
                w = turned(e)
                nc.scalar.copy(hT_hi[:, :, 0:w], HT.rearrange("p (k t) -> p k t", k=4)[:, :, 0:w]).then_inc(s["hhi"], 1)

            def y_out(e):
                act.wait_ge(s["used"], e * U + 2 * U)
                if not isinstance(e, int) or e >= 1:
                    act.wait_ge(s["ysc"], e * 16)
                nc.scalar.copy(y[:, 0:512], Y[0]).then_inc(s["ya"], 1)

            def turn(e, first=False, last=False):
                hi(e, 3)
                silu(e)
                if not first:
                    h_hi(e - 1)
                    hi(e, 4)
                    hi(e, 5)
                x_hi(e + 1)
                if not last:
                    hi(e + 1, 0)
                    hi(e + 1, 1)
                if not first:
                    y_out(e - 1)
                if not last:
                    hi(e + 1, 2)

            x_hi(0)
            for j in range(3):
                hi(0, j)
            turn(0, first=True)
            turn(1)
            with act.Fori(2, N_EXPERTS - 1) as e:
                turn(e)
            turn(N_EXPERTS - 1, last=True)
            h_hi(N_EXPERTS - 1)
            hi(N_EXPERTS, 4)
            hi(N_EXPERTS, 5)
            y_out(N_EXPERTS - 1)

        @block.vector
        def _(dve):
            nc.vector.memset(xg[:, :], 0.0).then_inc(s["xg0"], 1)

            def lo(e, j):
                dve.wait_ge(s["hi"], (j + 1 if j < 3 else 6) if isinstance(e, int) and e == 0 else
                            e * U + j + 1 if not (isinstance(e, int) and e == N_EXPERTS) else e * U + j - 3)
                ins = nc.vector.tensor_tensor(wlo[j][:, :], raw[j][:, :], whi[j][:, :].bitcast(F32), ALU.subtract)
                ins.then_inc(s["lo"], 3 if isinstance(e, int) and e == 0 and j == 3 else 1)

            def x_lo(e):
                for half in range(2):
                    dve.wait_ge(s["xhi"], e * 2 + half + 1)
                    w, k = turned(e), slice(4 * half, 4 * half + 4)
                    nc.vector.tensor_tensor(xT_lo[:, k, 0:w], XT[half].rearrange("p (k t) -> p k t", k=4)[:, :, 0:w],
                                            xT_hi[:, k, 0:w].bitcast(F32), ALU.subtract).then_inc(s["xlo"], 1)

            def hidden(e):
                dve.wait_ge(s["sg"], e + 1)
                dve.wait_ge(s["used"], e * U + 4 if not (isinstance(e, int) and e == 0) else 4)
                if not isinstance(e, int) or e >= 1:
                    dve.wait_ge(s["ht"], e)
                nc.vector.tensor_tensor(hid[:, :], sg[:, :], UP, ALU.mult).then_inc(s["hid"], 1)

            def h_lo(e):
                dve.wait_ge(s["hhi"], e + 1)
                w = turned(e)
                nc.vector.tensor_tensor(hT_lo[:, :, 0:w], HT.rearrange("p (k t) -> p k t", k=4)[:, :, 0:w],
                                        hT_hi[:, :, 0:w].bitcast(F32), ALU.subtract).then_inc(s["hlo"], 1)

            def y_out(e):
                dve.wait_ge(s["used"], e * U + 2 * U)
                if not isinstance(e, int) or e >= 1:
                    dve.wait_ge(s["ysc"], e * 16)
                nc.vector.tensor_copy(y[:, 512:D], Y[1]).then_inc(s["yd"], 1)

            def turn(e, first=False, last=False):
                lo(e, 3)
                if not first:
                    h_lo(e - 1)
                    lo(e, 4)
                    lo(e, 5)
                hidden(e)
                x_lo(e + 1)
                if not last:
                    lo(e + 1, 0)
                    lo(e + 1, 1)
                if not first:
                    y_out(e - 1)
                if not last:
                    lo(e + 1, 2)

            x_lo(0)
            for j in range(3):
                lo(0, j)
            turn(0, first=True)
            turn(1)
            with dve.Fori(2, N_EXPERTS - 1) as e:
                turn(e)
            turn(N_EXPERTS - 1, last=True)
            h_lo(N_EXPERTS - 1)
            lo(N_EXPERTS, 4)
            lo(N_EXPERTS, 5)
            y_out(N_EXPERTS - 1)

        @block.gpsimd
        def _(pool):
            def gather(b):
                pool.indirect_dma_start(xg[0:SLOTS, :], None, m_rows, bass.IndirectOffsetOnAxis(row_x[0:SLOTS, b:b + 1], 0),
                                        bounds_check=T - 1, oob_is_err=False).then_inc(s["xg"], 16)

            def scatter(b):
                pool.indirect_dma_start(y_rows, bass.IndirectOffsetOnAxis(row_y[0:SLOTS, b:b + 1], 0), y[0:SLOTS, :], None,
                                        bounds_check=2 * T - 1, oob_is_err=False).then_inc(s["ysc"], 16)

            pool.wait_ge(s["xg0"], 1)
            gather(0)
            for e in range(N_EXPERTS):
                pool.wait_ge(s["xt"], e * 2 + 2)
                gather(e + 1)
                if e >= 1:
                    pool.wait_ge(s["ya"], e)
                    pool.wait_ge(s["yd"], e)
                    scatter(e - 1)
            pool.wait_ge(s["ya"], N_EXPERTS)
            pool.wait_ge(s["yd"], N_EXPERTS)
            scatter(N_EXPERTS - 1)
            pool.wait_ge(s["ysc"], 16 * N_EXPERTS)

        @block.tensor
        def _(pe):
            def x_turn(e):
                pe.wait_ge(s["xg"], e * 16 + 16)
                if not isinstance(e, int) or e >= 1:
                    pe.wait_ge(s["xlo"], e * 2)
                for half in range(2):
                    for k in range(4):
                        w = P if half == k == 0 else turned(e)
                        last = nc.tensor.transpose(XT[half][:, k * P:k * P + w], xg[0:w, (4 * half + k) * P:(4 * half + k + 1) * P],
                                                   ident[0:w, 0:w])
                    last.then_inc(s["xt"], 1)

            def project(e, out, j0):
                for j in (j0, j0 + 1):
                    pe.wait_ge(s["lo"], e * U + j + 1 if not (isinstance(e, int) and e == 0 and j == 3) else U)
                    for k in range(4):
                        kk = 4 * (j % 2) + k
                        last = split_mm(nc, out, xT_hi[:, kk, :], xT_lo[:, kk, :], k4(whi[j])[:, k, :], k4(wlo[j])[:, k, :],
                                        kk == 0, kk == KD - 1)
                    last.then_inc(s["used"], 3 if isinstance(e, int) and e == 0 and j == 3 else 1)

            def h_turn(e):
                pe.wait_ge(s["hid"], e + 1)
                for k in range(4):
                    w = P if k == 0 else turned(e)
                    last = nc.tensor.transpose(HT[:, k * P:k * P + w], hid[0:w, k * P:k * P + P], ident[0:w, 0:w])
                last.then_inc(s["ht"], 1)

            def down(e, n):
                pe.wait_ge(s["hlo"], e + 1)
                if not isinstance(e, int) or e >= 1:
                    pe.wait_ge(s["ya"], e)
                    pe.wait_ge(s["yd"], e)
                for j in (4, 5):
                    pe.wait_ge(s["lo"], n * U + j + 1 if not (isinstance(e, int) and e == N_EXPERTS - 1) else n * U + j - 3)
                    for half in range(2):
                        for k in range(2):
                            kk = 2 * (j - 4) + k
                            c = slice(half * 512, half * 512 + 512)
                            last = split_mm(nc, Y[half], hT_hi[:, kk, :], hT_lo[:, kk, :], k2(whi[j])[:, k, c], k2(wlo[j])[:, k, c],
                                            kk == 0, kk == 3)
                    if isinstance(e, int) and e == N_EXPERTS - 1:
                        last.then_inc(s["used"], 1 if j == 4 else 5)
                    else:
                        last.then_inc(s["used"], 1)

            def turn(e, first=False):
                pe.wait_ge(s["xlo"], e * 2 + 2)
                if not isinstance(e, int) or e >= 1:
                    pe.wait_ge(s["sg"], e)
                project(e, GATE, 0)
                if not first:
                    h_turn(e - 1)
                project(e, UP, 2)
                x_turn(e + 1)
                if not first:
                    down(e - 1, e)

            x_turn(0)
            turn(0, first=True)
            turn(1)
            with pe.Fori(2, N_EXPERTS) as e:
                turn(e)
            h_turn(N_EXPERTS - 1)
            down(N_EXPERTS - 1, N_EXPERTS)
    g["clear"](s, s_raw)
    ex.close()

    over_e = g["over_e"]
    s = {n: sem("o_" + n) for n in "xg0 w xg xt xc gu sg hid ht hc down y ysc".split()}
    g["gathers"] += [s["xg"], s["ysc"]]
    with ExitStack() as tmp:
        def sb(name, shape, dt=F32):
            return tmp.enter_context(nc.sbuf_tensor(name, shape, dt))

        wg, wu = sb("wg_o", [P, KD, FF]), sb("wu_o", [P, KD, FF])
        wd = sb("wd_o", [P, FF // P, D])
        xg, xT = sb("xg_o", [P, D]), sb("xT_o", [P, KD, P])
        sg, hid, hidT = sb("sg_o", [P, FF]), sb("hid_o", [P, FF]), sb("hidT_o", [P, FF // P, P])
        y = sb("y_o", [P, D])
        block = tmp.enter_context(nc.Block())

        def blocks(eng, turn):
            n = eng.value_load(over_e[0:1, OVER:OVER + 1], min_val=0, max_val=OVER)
            with eng.If(n > 0):
                turn(0)
                with eng.Fori(1, OVER) as j:
                    turn(j)

        def later(j):
            return not isinstance(j, int)

        @block.sync
        def _(sp):
            def turn(j):
                if later(j):
                    sp.wait_ge(s["down"], j)
                e = sp.value_load(over_e[0:1, bass.ds(j, 1)] if later(j) else over_e[0:1, 0:1], min_val=0, max_val=N_EXPERTS - 1)
                for w, t in ((w_gate, wg), (w_up, wu), (w_down, wd)):
                    sp.dma_start(t[:, :, :], w[:, bass.ds(e, 1), :, :].rearrange("p o k f -> p (o k) f")).then_inc(s["w"], 16)

            blocks(sp, turn)

        @block.gpsimd
        def _(pool):
            n = pool.value_load(over_e[0:1, OVER:OVER + 1], min_val=0, max_val=OVER)
            with pool.If(n > 0):
                pool.wait_ge(s["xg0"], 1)
                for j in range(OVER):
                    b = N_EXPERTS + j
                    if j >= 1:
                        pool.wait_ge(s["xt"], j)
                    pool.indirect_dma_start(xg[0:SLOTS, :], None, m_rows, bass.IndirectOffsetOnAxis(row_x[0:SLOTS, b:b + 1], 0),
                                            bounds_check=T - 1, oob_is_err=False).then_inc(s["xg"], 16)
                    pool.wait_ge(s["y"], 2 * j + 2)
                    pool.indirect_dma_start(y_rows, bass.IndirectOffsetOnAxis(row_y[0:SLOTS, b:b + 1], 0), y[0:SLOTS, :], None,
                                            bounds_check=2 * T - 1, oob_is_err=False).then_inc(s["ysc"], 16)
                pool.wait_ge(s["ysc"], 16 * OVER)

        @block.scalar
        def _(act):
            def turn(j):
                act.wait_ge(s["xt"], j + 1)
                if later(j):
                    act.wait_ge(s["gu"], j)
                for half in range(2):
                    nc.scalar.copy(xT[:, 4 * half:4 * half + 4, :],
                                   banks[2 + half].rearrange("p (k t) -> p k t", k=4)).then_inc(s["xc"], 1)
                act.wait_ge(s["gu"], j + 1)
                if later(j):
                    act.wait_ge(s["hid"], j)
                nc.scalar.activation(sg[:, :], banks[0], ACT.Silu).then_inc(s["sg"], 1)
                act.wait_ge(s["ht"], j + 1)
                if later(j):
                    act.wait_ge(s["down"], j)
                nc.scalar.copy(hidT[:, :, :], banks[4].rearrange("p (k t) -> p k t", k=4)).then_inc(s["hc"], 1)
                act.wait_ge(s["down"], j + 1)
                if later(j):
                    act.wait_ge(s["ysc"], j * 16)
                for half in range(2):
                    nc.scalar.copy(y[:, 512 * half:512 * half + 512], banks[5 + half]).then_inc(s["y"], 1)

            blocks(act, turn)

        @block.vector
        def _(dve):
            nc.vector.memset(xg[:, :], 0.0).then_inc(s["xg0"], 1)

            def turn(j):
                dve.wait_ge(s["sg"], j + 1)
                if later(j):
                    dve.wait_ge(s["ht"], j)
                nc.vector.tensor_tensor(hid[:, :], sg[:, :], banks[1], ALU.mult).then_inc(s["hid"], 1)

            blocks(dve, turn)

        @block.tensor
        def _(pe):
            def turn(j):
                pe.wait_ge(s["xg"], j * 16 + 16)
                for k in range(KD):
                    last = nc.tensor.transpose(banks[2 + k // 4][:, (k % 4) * P:(k % 4 + 1) * P], xg[:, k * P:k * P + P], ident[:, :])
                last.then_inc(s["xt"], 1)
                pe.wait_ge(s["xc"], j * 2 + 2)
                pe.wait_ge(s["w"], j * 48 + 48)
                for o, t in ((0, wg), (1, wu)):
                    for k in range(KD):
                        last = nc.tensor.matmul(banks[o], xT[:, k, :], t[:, k, :], start=k == 0, stop=k == KD - 1)
                last.then_inc(s["gu"], 1)
                pe.wait_ge(s["hid"], j + 1)
                for k in range(FF // P):
                    last = nc.tensor.transpose(banks[4][:, k * P:k * P + P], hid[:, k * P:k * P + P], ident[:, :])
                last.then_inc(s["ht"], 1)
                pe.wait_ge(s["hc"], j + 1)
                if later(j):
                    pe.wait_ge(s["y"], j * 2)
                for half in range(2):
                    for k in range(FF // P):
                        last = nc.tensor.matmul(banks[5 + half], hidT[:, k, :], wd[:, k, 512 * half:512 * half + 512], start=k == 0,
                                                stop=k == FF // P - 1)
                last.then_inc(s["down"], 1)

            blocks(pe, turn)
    g["clear"](s)


class Weights:

    SLOTS = 2

    def __init__(self, nc, sem, sb, sources):
        self.nc, self.sources = nc, sources
        self.s_raw = [sem(f"w_raw{i}") for i in range(self.SLOTS)]
        self.s_hi, self.out = sem("w_hi"), sem("w_used")
        self.s_lo = [sem(f"w_lo{i}") for i in range(self.SLOTS)]
        self.raw = [sb(f"w_raw{i}", [P, UNIT]) for i in range(self.SLOTS)]
        self.hi = [sb(f"w_hi{i}", [P, UNIT], F32R) for i in range(self.SLOTS)]
        self.lo = [sb(f"w_lo{i}", [P, UNIT], F32R) for i in range(self.SLOTS)]

    def sems(self):
        return self.s_raw + self.s_lo + [self.s_hi, self.out]

    def load(self, sp, u):
        i = u % self.SLOTS
        if u >= len(self.sources):
            return
        if u >= self.SLOTS:
            sp.wait_ge(*self.made(u - self.SLOTS))
        for place, src in self.sources[u]:
            sp.dma_start(place(self.raw[i][:, :]), src).then_inc(self.s_raw[i], 16)

    def make_hi(self, act, u):
        i = u % self.SLOTS
        if u >= len(self.sources):
            return
        act.wait_ge(self.s_raw[i], 32 * (u // self.SLOTS + 1))
        if u >= self.SLOTS:
            act.wait_ge(self.out, 2 * (u - self.SLOTS + 1))
        self.nc.scalar.copy(self.hi[i][:, :], self.raw[i][:, :]).then_inc(self.s_hi, 1)

    def make_lo(self, eng, u, engine=None):
        i = u % self.SLOTS
        if u >= len(self.sources):
            return
        eng.wait_ge(self.s_hi, u + 1)
        (engine or self.nc.vector).tensor_tensor(self.lo[i][:, :], self.raw[i][:, :], self.hi[i][:, :].bitcast(F32),
                                                 ALU.subtract).then_inc(self.s_lo[i], 1)

    def made(self, u):
        return self.s_lo[u % self.SLOTS], u // self.SLOTS + 1

    def halves(self, u, k):
        return tuple(t[u % self.SLOTS][:, :].rearrange("p (k c) -> p k c", k=k) for t in (self.hi, self.lo))


def columns(w, c0, c1, width):
    def place(j):
        return lambda r: r.rearrange("p (k c) -> p k c", k=KD)[:, :, j * width:j * width + width]
    return [(place(0), w[:, :, c0:c0 + width]), (place(1), w[:, :, c1:c1 + width])]


def rows(w, k0, kn, c0, cn):
    def place(j):
        return lambda r: r.rearrange("p (k c) -> p k c", k=kn)[:, j * (kn // 2):(j + 1) * (kn // 2), :]
    return [(place(j), w[:, k0 + j * (kn // 2):k0 + (j + 1) * (kn // 2), c0:c0 + cn]) for j in range(2)]


def rms_root(nc, act, s, n, src, sq, ssq, rt, eps):
    nc.scalar.activation(sq, src, ACT.Square, accum_out=ssq).then_inc(s["ssq"], 1)
    act.wait_ge(s["ssq"], n + 1)
    nc.scalar.activation(rt, ssq, ACT.Sqrt, bias=eps[:, 0:1], scale=1.0 / D).then_inc(s["rt"], 1)


def rms_scale(nc, dve, s, n, rt, rs):
    dve.wait_ge(s["rt"], n + 1)
    nc.vector.reciprocal(rs, rt).then_inc(s["rs"], 1)
    dve.wait_ge(s["rs"], n + 1)


def turn_rows(nc, pe, s, i, xn, banks, ident):
    pe.wait_ge(s["xn"], i + 1)
    for half in range(2):
        if i >= 1:
            pe.wait_ge(s["lo"], 2 * (i - 1) + half + 1)
        for k in range(4):
            last = nc.tensor.transpose(banks[6 + half][:, k * P:k * P + P], xn[:, (4 * half + k) * P:(4 * half + k + 1) * P],
                                       ident[:, :])
        last.then_inc(s["tr"], 1)


def turned_hi(nc, act, s, i, banks, hi):
    for half in range(2):
        act.wait_ge(s["tr"], 2 * i + half + 1)
        nc.scalar.copy(hi[:, 4 * half:4 * half + 4, i * P:i * P + P],
                       banks[6 + half].rearrange("p (k t) -> p k t", k=4)).then_inc(s["hi"], 1)


def turned_lo(nc, dve, s, i, banks, hi, lo):
    for half in range(2):
        dve.wait_ge(s["hi"], 2 * i + half + 1)
        nc.vector.tensor_tensor(lo[:, 4 * half:4 * half + 4, i * P:i * P + P],
                                banks[6 + half].rearrange("p (k t) -> p k t", k=4),
                                hi[:, 4 * half:4 * half + 4, i * P:i * P + P].bitcast(F32), ALU.subtract).then_inc(s["lo"], 1)


def second_block_units(dram):
    w = dram["w_in_2"][0].rearrange("(k p) c -> p k c", p=P)
    w_pw, w_so, w_out, w_gu, w_down = (dram[n][0].rearrange("(k p) c -> p k c", p=P)
                                       for n in ("conv_pw_w_2", "ssm_out_w_2", "w_out_2", "w_gate_up_2", "w_down_2"))
    GW = SSM_RANK * SSM_HD
    units, at = [], {}
    for n in range(SSM_GROUPS):
        for kind in ("x", "bc", "glu", "z") + ("glu",) * (n == 0):
            c = sum(k[0] == "glu" for k in at)
            if kind == "glu" and c >= KD:
                continue
            at[kind, c if kind == "glu" else n] = len(units)
            units.append({"x": columns(w, OFF_XBC + n * GW, OFF_XBC + n * GW + P, P),
                          "bc": columns(w, OFF_B + n * P, OFF_C + n * P, P),
                          "glu": columns(w, c * P, D + c * P, P),
                          "z": columns(w, OFF_Z + n * GW, OFF_Z + n * GW + P, P)}[kind])
    at["conv_gate"] = len(units)
    units += [columns(w, OFF_GATE + 2 * n * P, OFF_GATE + (2 * n + 1) * P, P) for n in range(4)]
    at["pw"] = len(units)
    units += [rows(w_pw, 2 * n, 2, 0, D) for n in range(KD // 2)]
    at["ssm_gate"] = len(units)
    units += [columns(w, OFF_GATE + D + 2 * n * P, OFF_GATE + D + (2 * n + 1) * P, P) for n in range(4)]
    at["ssm_out"] = len(units)
    units += [rows(w_so, 2 * n, 2, 0, D) for n in range(D_INNER // P // 2)]
    at["w_out"] = len(units)
    units += [rows(w_out, 4 * half, 4, 512 * n, 512) for n in range(2) for half in range(2)]
    at["gate_up"] = len(units)
    units += [columns(w_gu, c * P, HIDDEN + c * P, P) for c in range(HIDDEN // P)]
    at["down"] = len(units)
    units += [rows(w_down, 2 * n, 2, 0, D) for n in range(HIDDEN // P // 2)]
    return units, at


def stage_c(nc, dram, g, sem, banks, out):
    with ExitStack() as keep:
        def sb(name, shape, dt=F32):
            return keep.enter_context(nc.sbuf_tensor(name, shape, dt))

        hT = [sb(n, [P, KD, T], F32R) for n in ("hT2_hi", "hT2_lo")]
        units, g["unit"] = second_block_units(dram)
        W = Weights(nc, sem, sb, units)
        join(nc, dram, g, sem, banks, W, hT)
        with ExitStack() as ssm:
            yT = ssm.enter_context(nc.sbuf_tensor("yT", [P, D_INNER // P, T], F32))
            groups(nc, dram, g, sem, banks, W, hT, yT)
            mix(nc, dram, g, sem, banks, W, hT, yT)
        ffn(nc, dram, g, sem, banks, W, hT, out)


def join(nc, dram, g, sem, banks, W, hT):
    h, eps, ident = g["h"], g["eps"], g["ident"]
    s = {n: sem("j_" + n) for n in "gf gp sum ssq rt rs x xn tr hi lo".split()}
    s_y = [sem(f"j_y{i}") for i in range(NT)]
    y_rows = g["y_rows"].rearrange("(k i p) d -> p k i d", p=P, k=2)
    with ExitStack() as tmp:
        def sb(name, shape, dt=F32):
            return tmp.enter_context(nc.sbuf_tensor(name, shape, dt))

        yk = sb("yk", [P, 2, NT, D])
        gf, gp, sq = sb("gf", [P, D]), sb("gp", [P, D]), sb("sq_j", [P, D])
        xn = [sb(f"xn_j{i}", [P, D]) for i in range(NT)]
        ssq, rt, rs = (sb(n, [P, 2 * NT]) for n in ("ssq_j", "rt_j", "rs_j"))
        NORMS = [0, 1, 2, 4, 3, 5, 6, 7]
        block = tmp.enter_context(nc.Block())

        @block.sync
        def _(sp):
            for i in range(NT):
                for k in range(2):
                    sp.dma_start(yk[:, k, i, :], y_rows[:, k, i, :]).then_inc(s_y[i], 16)
            for u in range(2):
                W.load(sp, u)

        @block.scalar
        def _(act):
            act.dma_start(gf[:, :], dram["g_final"].unsqueeze(0)[0].partition_broadcast(P)).then_inc(s["gf"], 16)
            act.dma_start(gp[:, :], dram["mix_pre_g_2"][0].partition_broadcast(P)).then_inc(s["gp"], 16)
            for at, n in enumerate(NORMS):
                i = n % NT
                if n < NT:
                    act.wait_ge(s["sum"], 2 * i + 2)
                else:
                    act.wait_ge(s["x"], i + 1)
                rms_root(nc, act, s, at, h[:, i, :], sq[:, :], ssq[:, n:n + 1], rt[:, n:n + 1], eps)
            for i in range(NT):
                turned_hi(nc, act, s, i, banks, hT[0])
                if i < 2:
                    W.make_hi(act, i)

        @block.vector
        def _(dve):
            dve.wait_ge(s["gf"], 16)
            dve.wait_ge(s["gp"], 16)

            def joined(i):
                dve.wait_ge(s_y[i], 32)
                for k in range(2):
                    nc.vector.scalar_tensor_tensor(h[:, i, :], yk[:, k, i, :], g["gate"][k][:, i:i + 1], h[:, i, :], ALU.mult,
                                                   ALU.add).then_inc(s["sum"], 1)
                    dve.wait_ge(s["sum"], 2 * i + k + 1)

            def normed(n):
                i = n % NT
                rms_scale(nc, dve, s, NORMS.index(n), rt[:, n:n + 1], rs[:, n:n + 1])
                if n < NT:
                    nc.vector.scalar_tensor_tensor(h[:, i, :], h[:, i, :], rs[:, n:n + 1], gf[:, :], ALU.mult,
                                                   ALU.mult).then_inc(s["x"], 1)
                else:
                    dve.wait_ge(s["x"], i + 1)
                    nc.vector.scalar_tensor_tensor(xn[i][:, :], h[:, i, :], rs[:, n:n + 1], gp[:, :], ALU.mult,
                                                   ALU.mult).then_inc(s["xn"], 1)

            joined(0)
            joined(1)
            normed(0)
            joined(2)
            normed(1)
            joined(3)
            for n in NORMS[2:]:
                normed(n)
            for i in range(NT):
                turned_lo(nc, dve, s, i, banks, *hT)
                if i < 2:
                    W.make_lo(dve, i)

        @block.tensor
        def _(pe):
            for i in range(NT):
                turn_rows(nc, pe, s, i, xn[i], banks, ident)
    g["clear"](s, s_y)


def product(nc, pe, W, u, v, out, hT):
    hi, lo = W.halves(u, KD)
    for k in range(KD):
        last = split_mm(nc, out, hi[:, k, v * P:v * P + P], lo[:, k, v * P:v * P + P], hT[0][:, k, :], hT[1][:, k, :],
                        k == 0, k == KD - 1)
    last.then_inc(W.out, 1)


def groups(nc, dram, g, sem, banks, W, hT, yT):
    cols, ident, tri, ones, eps = (g[n] for n in "cols ident tri ones eps".split())
    w = dram["w_in_2"][0].rearrange("(k p) c -> p k c", p=P)
    G, R, H, C = SSM_GROUPS, SSM_RANK, SSM_HEADS, NT
    PAD = SSM_K - 1
    GW = R * SSM_HD
    mixT = g["mixed"][:, :, :].rearrange("p i d -> p (i d)").rearrange("p (c t) -> p c t", c=KD)
    DPAD = CONV_K - 1
    yT_flat = yT[:, :, :].rearrange("p c t -> p (c t)")
    NV = 3
    v = [yT_flat[:, (D_INNER // P - 4) * T + i * (DPAD + T):(D_INNER // P - 4) * T + (i + 1) * (DPAD + T)] for i in range(NV)]
    unit_at, LAST = g["unit"], g["unit"]["conv_gate"]

    def first(n):
        return unit_at["x", n + 1]
    s = {n: sem("s_" + n) for n in (
        "row wdt wdh wdl dtp dt e1 e2 acs acp acT acw pad pc tapd tapp cvd cvp sl zs tx tb cb xn bn cbm ar eal dtd dte seg ex "
        "A xdt xde xd stp stc yd yo yr t0 yt ssq rt rs yn ty ye vpad sg v tap cd".split())}

    def col(name, n):
        return cols[:, VEC_AT[name] + n:VEC_AT[name] + n + 1]

    with ExitStack() as tmp:
        def sb(name, shape, dt=F32):
            return tmp.enter_context(nc.sbuf_tensor(name, shape, dt))

        wdh, wdl = sb("wdt_hi", [P, KD, H], F32R), sb("wdt_lo", [P, KD, H], F32R)
        dtb, al, dsk = sb("dtb", [P, H]), sb("al", [P, H]), sb("dsk", [P, H])
        dt, adt, acs, eacs = (sb(n, [P, C, H]) for n in ("dt", "adt", "acs", "eacs"))
        pc = sb("pc", [P, 4, PAD + T])
        xbc = sb("xbc", [P, 4, T])
        zs = sb("zs", [P, C, GW])
        x_nat, xdt, xde, y = (sb(n, [P, C, GW]) for n in ("x_nat", "xdt", "xde", "y_s"))
        yo = xde
        b_nat = sb("b_nat", [P, C, P])
        cbm = sb("cbm", [P, C, P])
        A = sb("A", [P, R, T])
        eal = sb("eal", [P, R, C])
        dte = sb("dte", [P, C, R])
        tp = sb("tp_s", [P, T])
        st = sb("st_s", [P, C, GW])
        ssq, rt, rs = (sb(n, [P, C]) for n in ("ssq_s", "rt_s", "rs_s"))
        wdt = zs[:, 0, :].rearrange("p (k h) -> p k h", k=KD)
        dtz, dta = (x_nat[:, 0, i * C * H:(i + 1) * C * H].rearrange("p (c h) -> p c h", c=C) for i in range(2))
        acT = xde[0:H, 0:2, :].rearrange("p c d -> p (c d)")
        acs_rows = g["acs_rows"]
        block = tmp.enter_context(nc.Block())

        def heads(t):
            return t[:, :, :].rearrange("p c (r d) -> p c r d", r=R)

        def by_head(t, n):
            return t[:, :, n * R:n * R + R].unsqueeze(3).to_broadcast([P, C, R, SSM_HD])

        def conv_tile(n, j):
            return (2 * n + j) if j < 2 else 2 * G + (n if j == 2 else G + n)

        def taps(dve, chain, n, j):
            tile = conv_tile(n, j)
            for k in range(SSM_K):
                src, wk = pc[:, j, k:k + T], col("ssm_w", k * 4 * G + tile)
                if k == 0:
                    ins = nc.vector.tensor_scalar(xbc[:, j, :], src, wk, col("ssm_b", tile), ALU.mult, ALU.add)
                else:
                    ins = nc.vector.scalar_tensor_tensor(xbc[:, j, :], src, wk, xbc[:, j, :], ALU.mult, ALU.add)
                if k < SSM_K - 1:
                    chain[0] += 1
                    ins.then_inc(s["tapd"], 1)
                    dve.wait_ge(s["tapd"], chain[0])
            ins.then_inc(s["cvd"], 1)

        def taps_in_two(pool, chain, n, j):
            tile = conv_tile(n, j)
            for k in range(SSM_K):
                src, wk = pc[:, j, k:k + T], col("ssm_w", k * 4 * G + tile)
                if k == 0:
                    ins = nc.gpsimd.tensor_scalar(xbc[:, j, :], src, wk, col("ssm_b", tile), ALU.mult, ALU.add)
                else:
                    nc.gpsimd.tensor_scalar(tp[:, :], src, wk, None, ALU.mult).then_inc(s["tapp"], 1)
                    chain[0] += 1
                    pool.wait_ge(s["tapp"], chain[0])
                    ins = nc.gpsimd.tensor_tensor(xbc[:, j, :], xbc[:, j, :], tp[:, :], ALU.add)
                if k < SSM_K - 1:
                    chain[0] += 1
                    ins.then_inc(s["tapp"], 1)
                    pool.wait_ge(s["tapp"], chain[0])
            ins.then_inc(s["cvp"], 1)
            pool.wait_ge(s["cvp"], 2 * n + j - 1)

        @block.sync
        def _(sp):
            for u in range(2, 4):
                W.load(sp, u)
            sp.wait_ge(s["acT"], 1)
            sp.dma_start(acs_rows, acT).then_inc(s["acw"], 16)
            sp.wait_ge(s["acw"], 16)
            loaded = 4
            for n in range(G):
                until = first(n) + 1 if n + 1 < G else LAST + 2
                for u in range(loaded, until):
                    W.load(sp, u)
                loaded = until
                if n >= 1:
                    sp.wait_ge(s["yd"], 2 * n)
                sp.dma_start(A[:, :, :].rearrange("p r t -> p (r t)"), acs_rows[n * R:n * R + R, :].rearrange("r t -> (r t)")
                             .partition_broadcast(P)).then_inc(s["ar"], 16)

        @block.gpsimd
        def _(pool):
            nc.gpsimd.memset(pc[:, :, 0:PAD], 0.0).then_inc(s["pad"], 1)
            for i in range(NV):
                nc.gpsimd.memset(v[i][:, 0:DPAD], 0.0).then_inc(s["vpad"], 1)
            chain = [0]
            pool.wait_ge(s["pad"], 1)
            pool.wait_ge(s["row"], 48)
            def conv_taps(n, j):
                pool.wait_ge(s["pc"], 4 * n + j + 1)
                if n >= 1:
                    pool.wait_ge(s["cb"], n)
                    if j == 2:
                        pool.wait_ge(s["tb"], n)
                    else:
                        pool.wait_ge(s["yo"], 2 * n)
                taps_in_two(pool, chain, n, j)

            conv_taps(0, 2)
            for n in range(G):
                conv_taps(n, 3)
                pool.wait_ge(s["xn"], 2 * n + 2)
                if n >= 1:
                    pool.wait_ge(s["ty"], 2 * n)
                nc.gpsimd.tensor_tensor(heads(y), heads(x_nat),
                                        dsk[:, n * R:n * R + R].unsqueeze(1).unsqueeze(3).to_broadcast([P, C, R, SSM_HD]),
                                        ALU.mult).then_inc(s["xd"], 1)
                if n + 1 < G:
                    W.make_lo(pool, first(n) + 3, nc.gpsimd)
                    conv_taps(n + 1, 2)
                    W.make_lo(pool, first(n) + 4, nc.gpsimd)

        @block.scalar
        def _(act):
            act.dma_start(wdt, w[:, :, OFF_DT:OFF_GATE]).then_inc(s["wdt"], 16)
            act.dma_start(dtb[:, :], dram["dt_bias_2"][0].partition_broadcast(P)).then_inc(s["row"], 16)
            act.dma_start(al[:, :], dram["a_log_2"][0].partition_broadcast(P)).then_inc(s["row"], 16)
            act.dma_start(dsk[:, :], dram["d_skip_2"][0].partition_broadcast(P)).then_inc(s["row"], 16)
            act.wait_ge(s["wdt"], 16)
            nc.scalar.copy(wdh[:, :, :], wdt).then_inc(s["wdh"], 1)
            act.wait_ge(s["row"], 48)
            nc.scalar.activation(al[:, :], al[:, :], ACT.Exp).then_inc(s["e1"], 1)
            act.wait_ge(s["dt"], 3)
            nc.scalar.activation(dta, dta, ACT.Exp, scale=-1.0).then_inc(s["e1"], 1)
            act.wait_ge(s["e1"], 2)
            nc.scalar.activation(dta, dta, ACT.Ln, bias=1.0).then_inc(s["e1"], 1)
            act.wait_ge(s["acp"], 1)
            nc.scalar.activation(eacs[:, :, :], banks[5][:, 0:C * H].rearrange("p (c h) -> p c h", c=C), ACT.Exp).then_inc(s["e2"], 1)
            nc.scalar.copy(acT, banks[6][0:H, :]).then_inc(s["acT"], 1)

            def evacuate(n, tiles):
                for j in tiles:
                    act.wait_ge(W.out, 2 * unit_at["x" if j < 2 else "bc", n] + j % 2 + 1)
                    act.wait_ge(s["pad"], 1)
                    if n >= 1:
                        if j < 2:
                            act.wait_ge(s["cvd"], 2 * (n - 1) + j + 1)
                        else:
                            act.wait_ge(s["cvp"], 2 * (n - 1) + j - 1)
                    nc.scalar.copy(pc[:, j, PAD:PAD + T], banks[j]).then_inc(s["pc"], 1)

            def gate(n):
                if n >= 1:
                    act.wait_ge(s["yt"], n)
                for j in range(2):
                    act.wait_ge(W.out, 2 * unit_at["z", n] + j + 1)
                    nc.scalar.activation(zs[:, 2 * j:2 * j + 2, :], banks[6 + j].rearrange("p (c d) -> p c d", c=2),
                                         ACT.Silu).then_inc(s["zs"], 1)

            def glu_gate(n):
                act.wait_ge(W.out, 2 * unit_at["glu", n] + 2)
                act.wait_ge(s["vpad"], NV)
                if n >= NV:
                    act.wait_ge(s["cd"], n - NV + 1)
                nc.scalar.activation(v[n % NV][:, DPAD:DPAD + T], banks[1], ACT.Sigmoid, bias=col("glu_b", KD + n)).then_inc(s["sg"], 1)

            def store(n):
                if n >= G - 2:
                    act.wait_ge(s["cd"], KD)
                for j in range(2):
                    act.wait_ge(s["ty"], 2 * n + j + 1)
                    nc.scalar.activation(yT[:, 2 * n + j, :], banks[6 + j], ACT.Copy, scale=col("norm_g", 2 * n + j)).then_inc(s["ye"], 1)

            def silu(n, tiles):
                for j in tiles:
                    if j < 2:
                        act.wait_ge(s["cvd"], 2 * n + j + 1)
                    else:
                        act.wait_ge(s["cvp"], 2 * n + j - 1)
                    nc.scalar.activation(xbc[:, j, :], xbc[:, j, :], ACT.Silu).then_inc(s["sl"], 1)

            evacuate(0, (0, 1))
            W.make_hi(act, 2)
            evacuate(0, (2, 3))
            W.make_hi(act, 3)
            W.make_hi(act, 4)
            glu_gate(0)
            silu(0, (0, 1, 2))
            W.make_hi(act, 5)
            gate(0)
            W.make_hi(act, 6)
            glu_gate(1)

            def chunk_decays(n):
                act.wait_ge(s["ar"], 16 * n + 16)
                if n >= 1:
                    act.wait_ge(s["stc"], 3 * n)
                nc.scalar.activation(eal[:, :, :], A[:, :, P - 1:T:P], ACT.Exp).then_inc(s["eal"], 1)

            chunk_decays(0)
            for n in range(G):
                more = n + 1 < G
                silu(n, (3,))
                act.wait_ge(s["dtd"], n + 1)
                nc.scalar.activation(dte[:, :, :], dte[:, :, :], ACT.Exp).then_inc(s["dte"], 1)
                act.wait_ge(s["seg"], 2 * n + 2)
                nc.scalar.activation(A[:, :, :], A[:, :, :], ACT.Exp).then_inc(s["ex"], 1)
                if more:
                    W.make_hi(act, first(n) + 2)
                    evacuate(n + 1, (0, 1))
                if n >= 1:
                    store(n - 1)
                for j in range(2):
                    act.wait_ge(s["tx"], 2 * n + j + 1)
                    if n >= 1:
                        act.wait_ge(s["xdt"], n)
                        act.wait_ge(s["xd"], n)
                    nc.scalar.copy(x_nat[:, 2 * j:2 * j + 2, :], banks[4 + j].rearrange("p (c d) -> p c d", c=2)).then_inc(s["xn"], 1)
                act.wait_ge(s["tb"], n + 1)
                if n >= 1:
                    act.wait_ge(s["stp"], 2 * n)
                nc.scalar.copy(b_nat[:, :, :], banks[6].rearrange("p (c d) -> p c d", c=C)).then_inc(s["bn"], 1)
                if more:
                    W.make_hi(act, first(n) + 3)
                    evacuate(n + 1, (2, 3))
                    W.make_hi(act, first(n) + 4)
                    if n + 2 < KD:
                        glu_gate(n + 2)
                    silu(n + 1, (0, 1, 2))
                    if n + 2 < KD:
                        W.make_hi(act, first(n) + 5)
                    chunk_decays(n + 1)
                act.wait_ge(s["yt"], n + 1)
                for c in range(C):
                    if n or c:
                        act.wait_ge(s["ssq"], C * n + c)
                    if n >= 1 and c == 0:
                        act.wait_ge(s["rt"], n)
                    nc.scalar.activation(yo[:, 0, :], y[:, c, :], ACT.Square, accum_out=ssq[:, c:c + 1]).then_inc(s["ssq"], 1)
                act.wait_ge(s["ssq"], C * n + C)
                if n >= 1:
                    act.wait_ge(s["rs"], n)
                nc.scalar.activation(rt[:, :], ssq[:, :], ACT.Sqrt, bias=eps[:, 0:1], scale=1.0 / GW).then_inc(s["rt"], 1)
                if more:
                    gate(n + 1)
            store(G - 1)

        @block.vector
        def _(dve):
            V = nc.vector
            dve.wait_ge(s["wdh"], 1)
            V.tensor_tensor(wdl[:, :, :], wdt, wdh[:, :, :].bitcast(F32), ALU.subtract).then_inc(s["wdl"], 1)
            dve.wait_ge(s["dtp"], 1)
            dve.wait_ge(s["row"], 48)
            V.tensor_tensor(dtz, banks[4][:, 0:C * H].rearrange("p (c h) -> p c h", c=C),
                            dtb[:, :].unsqueeze(1).to_broadcast([P, C, H]), ALU.add).then_inc(s["dt"], 1)
            dve.wait_ge(s["dt"], 1)
            V.tensor_scalar(dta, dtz, -1.0, None, ALU.mult).then_inc(s["dt"], 1)
            dve.wait_ge(s["dt"], 2)
            V.tensor_tensor(dta, dta, dtz, ALU.max).then_inc(s["dt"], 1)
            dve.wait_ge(s["e1"], 3)
            V.scalar_tensor_tensor(dt[:, :, :], dtz, 0.0, dta, ALU.max, ALU.add).then_inc(s["dt"], 1)
            dve.wait_ge(s["dt"], 4)
            V.scalar_tensor_tensor(adt[:, :, :], dt[:, :, :], -1.0, al[:, :].unsqueeze(1).to_broadcast([P, C, H]), ALU.mult,
                                   ALU.mult).then_inc(s["dt"], 1)
            dve.wait_ge(s["e2"], 1)
            V.tensor_copy(acs[:, :, :], banks[5][:, 0:C * H].rearrange("p (c h) -> p c h", c=C)).then_inc(s["acs"], 1)
            dve.wait_ge(s["acs"], 1)
            dve.wait_ge(s["pad"], 1)
            chain = [0]

            def normed(n):
                dve.wait_ge(s["rt"], n + 1)
                V.reciprocal(rs[:, :], rt[:, :]).then_inc(s["rs"], 1)
                dve.wait_ge(s["rs"], n + 1)
                V.tensor_tensor(y[:, :, :], y[:, :, :], rs[:, :].unsqueeze(2).to_broadcast([P, C, GW]), ALU.mult).then_inc(s["yn"], 1)

            taken = [0]

            def glu(n):
                dve.wait_ge(s["sg"], n + 1)
                vn = v[n % NV][:, DPAD:DPAD + T]
                V.scalar_tensor_tensor(vn, banks[0], col("glu_b", n), vn, ALU.add, ALU.mult).then_inc(s["v"], 1)

            def depthwise(n):
                for at in range(taken[0], min(taken[0] + n, KD * CONV_K)):
                    c, k = divmod(at, CONV_K)
                    if k == 0:
                        dve.wait_ge(s["v"], c + 1)
                    src = v[c % NV][:, k:k + T]
                    if k == 0:
                        ins = V.tensor_scalar(mixT[:, c, :], src, col("dw_w_a", c), col("dw_b", c), ALU.mult, ALU.add)
                    else:
                        ins = V.scalar_tensor_tensor(mixT[:, c, :], src, col("dw_w_a", k * KD + c), mixT[:, c, :], ALU.mult, ALU.add)
                    if k < CONV_K - 1:
                        ins.then_inc(s["tap"], 1)
                        dve.wait_ge(s["tap"], at - c + 1)
                    else:
                        ins.then_inc(s["cd"], 1)
                taken[0] += n

            def x_taps(n):
                for j in range(2):
                    dve.wait_ge(s["pc"], 4 * n + j + 1)
                    if n >= 1:
                        dve.wait_ge(s["tx"], 2 * n)
                    taps(dve, chain, n, j)

            W.make_lo(dve, 2)
            x_taps(0)
            W.make_lo(dve, 3)
            W.make_lo(dve, 4)
            glu(0)
            W.make_lo(dve, 5)
            glu(1)
            W.make_lo(dve, 6)
            for n in range(G):
                more = n + 1 < G
                dve.wait_ge(s["ar"], 16 * n + 16)
                if n >= 1:
                    dve.wait_ge(s["xde"], n)
                a_s = acs[:, :, n * R:n * R + R].rearrange("p c r -> p r c")
                V.tensor_tensor(dte[:, :, :].rearrange("p c r -> p r c"), A[:, :, P - 1:T:P], a_s, ALU.subtract).then_inc(s["dtd"], 1)
                dve.wait_ge(s["eal"], n + 1)
                dve.wait_ge(s["dtd"], n + 1)
                A4 = A[:, :, :].rearrange("p r (c l) -> p r c l", c=C)
                V.tensor_tensor(A4, A4, a_s.unsqueeze(3).to_broadcast([P, R, C, P]), ALU.subtract).then_inc(s["seg"], 1)
                dve.wait_ge(s["seg"], 2 * n + 1)
                V.tensor_scalar(A[:, :, :], A[:, :, :], 0.0, None, ALU.min).then_inc(s["seg"], 1)
                if n >= 1:
                    normed(n - 1)
                if more:
                    W.make_lo(dve, first(n) + 2)
                depthwise(7)
                dve.wait_ge(s["cb"], n + 1)
                if n >= 1:
                    dve.wait_ge(s["A"], n)
                V.tensor_tensor(cbm[:, :, :], banks[7].rearrange("p (c l) -> p c l", c=C),
                                tri[:, :].unsqueeze(1).to_broadcast([P, C, P]), ALU.mult).then_inc(s["cbm"], 1)
                dve.wait_ge(s["xn"], 2 * n + 2)
                if n >= 1:
                    dve.wait_ge(s["yd"], 2 * n)
                    dve.wait_ge(s["stp"], 2 * n)
                V.tensor_tensor(heads(xdt), heads(x_nat), by_head(dt, n), ALU.mult).then_inc(s["xdt"], 1)
                dve.wait_ge(s["xdt"], n + 1)
                dve.wait_ge(s["dte"], n + 1)
                V.tensor_tensor(heads(xde), heads(xdt), dte[:, :, :].unsqueeze(3).to_broadcast([P, C, R, SSM_HD]),
                                ALU.mult).then_inc(s["xde"], 1)
                dve.wait_ge(s["ex"], n + 1)
                dve.wait_ge(s["cbm"], n + 1)
                V.tensor_tensor(A[:, :, :], A[:, :, :], cbm[:, :, :].rearrange("p c l -> p (c l)").unsqueeze(1)
                                .to_broadcast([P, R, T]), ALU.mult).then_inc(s["A"], 1)
                depthwise(9)
                if n >= 1:
                    dve.wait_ge(s["yo"], 2 * n)
                for c in range(1, C):
                    dve.wait_ge(s["stp"], 2 * n + (1 if c < 3 else 2))
                    b = banks[6][:, (c - 1) * GW:c * GW] if c < 3 else banks[7][:, 0:GW]
                    if c == 1:
                        V.tensor_copy(st[:, 1, :], b).then_inc(s["stc"], 1)
                    else:
                        dve.wait_ge(s["stc"], 3 * n + c - 1)
                        for r in range(R):
                            q = slice(r * SSM_HD, r * SSM_HD + SSM_HD)
                            last = V.scalar_tensor_tensor(st[:, c, q], st[:, c - 1, q], eal[:, r, c - 1:c], b[:, q], ALU.mult, ALU.add)
                        last.then_inc(s["stc"], 1)
                if more:
                    x_taps(n + 1)
                depthwise(10)
                if more:
                    if n + 2 < KD:
                        glu(n + 2)
                for j in range(2):
                    dve.wait_ge(s["yd"], 2 * n + j + 1)
                    dve.wait_ge(s["xd"], n + 1)
                    yj = y[:, 2 * j:2 * j + 2, :]
                    V.tensor_tensor(yj, yj, banks[4 + j].rearrange("p (c d) -> p c d", c=2), ALU.add).then_inc(s["t0"], 1)
                depthwise(9)
                dve.wait_ge(s["yo"], 2 * n + 2)
                e4 = by_head(eacs, n)
                V.tensor_tensor(heads(yo)[:, 1, :, :], banks[2][:, GW:2 * GW].rearrange("p (r d) -> p r d", r=R), e4[:, 1, :, :],
                                ALU.mult).then_inc(s["t0"], 1)
                V.tensor_tensor(heads(yo)[:, 2:4, :, :], banks[3].rearrange("p (c r d) -> p c r d", c=2, r=R), e4[:, 2:4, :, :],
                                ALU.mult).then_inc(s["yr"], 1)
                dve.wait_ge(s["t0"], 4 * n + 3)
                dve.wait_ge(s["yr"], n + 1)
                V.tensor_tensor(y[:, 1:C, :], y[:, 1:C, :], yo[:, 1:C, :], ALU.add).then_inc(s["t0"], 1)
                dve.wait_ge(s["t0"], 4 * n + 4)
                dve.wait_ge(s["zs"], 2 * n + 2)
                V.tensor_tensor(y[:, :, :], y[:, :, :], zs[:, :, :], ALU.mult).then_inc(s["yt"], 1)
                if n + 2 < KD:
                    W.make_lo(dve, first(n) + 5)
            normed(G - 1)

        @block.tensor
        def _(pe):
            mm = nc.tensor.matmul

            def unit(kind, n):
                u = unit_at[kind, n]
                pe.wait_ge(*W.made(u))
                if kind != "z":
                    for half in range(2):
                        product(nc, pe, W, u, half, banks[(2 if kind == "bc" else 0) + half], hT)
                    return
                hi, lo = W.halves(u, KD)
                for i in range(C):
                    for k in range(KD):
                        t = slice(i * P, i * P + P)
                        last = split_mm(nc, banks[6 + i // 2][:, (i % 2) * GW:(i % 2 + 1) * GW], hT[0][:, k, t], hT[1][:, k, t], hi[:, k, :],
                                        lo[:, k, :], k == 0, k == KD - 1)
                    if i % 2:
                        last.then_inc(W.out, 1)

            def turn_out(n):
                pe.wait_ge(s["yn"], n + 1)
                if n < G - 1:
                    pe.wait_ge(s["zs"], 2 * n + 4)
                else:
                    pe.wait_ge(s["stc"], 3 * n + 3)
                for j in range(2):
                    for c in range(C):
                        last = nc.tensor.transpose(banks[6 + j][:, c * P:c * P + P], y[:, c, j * P:j * P + P], ident[:, :])
                    last.then_inc(s["ty"], 1)

            unit("x", 0)
            pe.wait_ge(s["wdl"], 1)
            for i in range(C):
                for k in range(KD):
                    t = slice(i * P, i * P + P)
                    last = split_mm(nc, banks[4][:, i * H:i * H + H], hT[0][:, k, t], hT[1][:, k, t], wdh[:, k, :], wdl[:, k, :],
                                    k == 0, k == KD - 1)
            last.then_inc(s["dtp"], 1)
            unit("bc", 0)
            pe.wait_ge(s["dt"], 5)
            for c in range(C):
                last = mm(banks[5][:, c * H:c * H + H], tri[:, :], adt[:, c, :], start=True, stop=True)
            for c in range(C):
                last = mm(banks[6][0:H, c * P:c * P + P], adt[:, c, :], tri[:, :], start=True, stop=True)
            last.then_inc(s["acp"], 1)
            pe.wait_ge(s["pc"], 2)
            unit("glu", 0)
            pe.wait_ge(s["acT"], 1)
            unit("z", 0)
            pe.wait_ge(s["v"], 1)
            unit("glu", 1)
            for n in range(G):
                more = n + 1 < G
                if more:
                    pe.wait_ge(s["v"], n + 2)
                    unit("x", n + 1)
                if n >= 1:
                    turn_out(n - 1)
                pe.wait_ge(s["sl"], 4 * n + 2)
                if n >= 1:
                    pe.wait_ge(s["yr"], n)
                else:
                    pe.wait_ge(s["acs"], 1)
                    pe.wait_ge(s["acT"], 1)
                for j in range(2):
                    for c in (2 * j, 2 * j + 1):
                        for d in range(2):
                            o = (c % 2) * GW + d * P
                            last = nc.tensor.transpose(banks[4 + j][:, o:o + P], xbc[:, d, c * P:c * P + P], ident[:, :])
                    last.then_inc(s["tx"], 1)
                pe.wait_ge(s["sl"], 4 * n + 4)
                if n >= 1:
                    pe.wait_ge(s["ye"], 2 * n)
                else:
                    pe.wait_ge(s["zs"], 2)
                for c in range(C):
                    last = nc.tensor.transpose(banks[6][:, c * P:c * P + P], xbc[:, 2, c * P:c * P + P], ident[:, :])
                last.then_inc(s["tb"], 1)
                for c in range(C):
                    t = slice(c * P, c * P + P)
                    last = mm(banks[7][:, t], xbc[:, 2, t], xbc[:, 3, t], start=True, stop=True)
                last.then_inc(s["cb"], 1)
                if more:
                    if n >= 1:
                        pe.wait_ge(s["yr"], n)
                    unit("bc", n + 1)
                pe.wait_ge(s["xde"], n + 1)
                pe.wait_ge(s["bn"], n + 1)
                pe.wait_ge(s["cbm"], n + 1)
                for c in range(3):
                    o = banks[6][:, c * GW:c * GW + GW] if c < 2 else banks[7][:, 0:GW]
                    last = mm(o, b_nat[:, c, :], xde[:, c, :], start=True, stop=True)
                    if c >= 1:
                        last.then_inc(s["stp"], 1)
                if n + 2 < KD:
                    pe.wait_ge(s["pc"], 4 * n + 6)
                    unit("glu", n + 2)
                pe.wait_ge(s["A"], n + 1)
                for c in range(C):
                    for r in range(R):
                        q = slice(r * SSM_HD, r * SSM_HD + SSM_HD)
                        o = (c % 2) * GW + r * SSM_HD
                        last = mm(banks[4 + c // 2][:, o:o + SSM_HD], A[:, r, c * P:c * P + P], xdt[:, c, q], start=True, stop=True)
                    if c % 2:
                        last.then_inc(s["yd"], 1)
                pe.wait_ge(s["stc"], 3 * n + 3)
                if more:
                    unit("z", n + 1)
                pe.wait_ge(s["pc"], 4 * (n + 1) + 4 if more else 4 * n + 4)
                for c in range(1, C):
                    o = (c % 2) * GW
                    last = mm(banks[2 + c // 2][:, o:o + GW], xbc[:, 3, c * P:c * P + P], st[:, c, :], start=True, stop=True)
                    if c % 2:
                        last.then_inc(s["yo"], 1)
            turn_out(G - 1)
    g["clear"](s)


def mix(nc, dram, g, sem, banks, W, hT, yT):
    h, eps, ident, ones = g["h"], g["eps"], g["ident"], g["ones"]
    mixT = g["mixed"][:, :, :].rearrange("p i d -> p (i d)").rearrange("p (c t) -> p c t", c=KD)
    mm_nat = g["mixed"]
    CG, PW, SG, SO, WO, NEXT = (g["unit"][n] for n in ("conv_gate", "pw", "ssm_gate", "ssm_out", "w_out", "gate_up"))
    s = {n: sem("m_" + n) for n in ("mean mu xc sqd vm rt rstd nrm act gate yh yl pwd gm mx mh ml cp gpo gpr ssq rt2 rs pn x xn "
                                    "tr hi lo").split()}

    def col(name, n):
        return g["cols"][:, VEC_AT[name] + n:VEC_AT[name] + n + 1]

    with ExitStack() as tmp:
        def sb(name, shape, dt=F32):
            return tmp.enter_context(nc.sbuf_tensor(name, shape, dt))

        gs = sb("gs", [P, KD, T])
        yh = [sb(f"yh{i}", [P, 2, T], F32R) for i in range(2)]
        yl = [sb(f"yl{i}", [P, 2, T], F32R) for i in range(2)]
        NP, NS = KD // 2, D_INNER // P // 2
        mu, rtv = sb("mu", [P, T]), sb("rtv", [P, T])
        gpo, gpr = sb("gpo", [P, D]), sb("gpr", [P, D])
        xn = [gs[:, 2 * i:2 * i + 2, :].rearrange("p c t -> p (c t)") for i in range(2)]
        sq = gs[:, 4:6, :].rearrange("p c t -> p (c t)")
        ssq, rt, rs = (sb(n, [P, 2 * NT]) for n in ("ssq_m", "rt_m", "rs_m"))
        NORMS = [0, 1, 2, 4, 3, 5, 6, 7]
        rms = {"ssq": s["ssq"], "rt": s["rt2"], "rs": s["rs"]}
        block = tmp.enter_context(nc.Block())

        def pair(r):
            return mixT[:, 2 * r:2 * r + 2, :] if r < NP else yT[:, 2 * (r - NP):2 * (r - NP) + 2, :]

        def unit_of(r):
            return PW + r if r < NP else SO + r - NP

        @block.sync
        def _(sp):
            for u in range(CG + 2, NEXT + 2):
                W.load(sp, u)

        @block.scalar
        def _(act):
            act.dma_start(gpo[:, :], dram["mix_post_g_2"][0].partition_broadcast(P)).then_inc(s["gpo"], 16)
            act.dma_start(gpr[:, :], dram["ffn_pre_g_2"][0].partition_broadcast(P)).then_inc(s["gpr"], 16)

            def y_hi(r):
                if r >= 2:
                    act.wait_ge(W.out, 2 * (unit_of(r - 2) + 1))
                nc.scalar.copy(yh[r % 2][:, :, :], pair(r)).then_inc(s["yh"], 1)

            def gates(first, u, name, n0):
                for j in range(2):
                    n = 2 * u + j
                    act.wait_ge(W.out, 2 * (first + u) + j + 1)
                    nc.scalar.activation(gs[:, n, :], banks[n % 6 if first == CG else n], ACT.Sigmoid,
                                         bias=col(name, n0 + n)).then_inc(s["gate"], 1)

            def square(c):
                act.wait_ge(s["xc"], c + 1)
                if c >= 4:
                    act.wait_ge(s["vm"], c - 3)
                nc.scalar.activation(gs[:, 4 + c % 4, :], mixT[:, c, :], ACT.Square).then_inc(s["sqd"], 1)

            def silu(c):
                act.wait_ge(s["nrm"], c + 1)
                nc.scalar.activation(mixT[:, c, :], mixT[:, c, :], ACT.Silu, bias=col("ln_b", c), scale=col("ln_g", c)).then_inc(s["act"], 1)
                act.wait_ge(s["act"], c + 1)

            for c in range(4):
                square(c)
            for u in range(2):
                gates(CG, u, "gate_b", 0)
                W.make_hi(act, CG + u + 2)
            for c in range(4, KD):
                square(c)
            act.wait_ge(s["vm"], KD)
            nc.scalar.activation(rtv[:, :], banks[7], ACT.Sqrt, bias=eps[:, 1:2], scale=1.0 / D).then_inc(s["rt"], 1)
            for r in range(2):
                silu(2 * r)
                silu(2 * r + 1)
                y_hi(r)
            for u in range(2, 4):
                gates(CG, u, "gate_b", 0)
                W.make_hi(act, CG + u + 2)
            for r in range(NP):
                if r + 2 < NP:
                    silu(2 * r + 4)
                    silu(2 * r + 5)
                W.make_hi(act, PW + r + 2)
                y_hi(r + 2)
            for u in range(4):
                act.wait_ge(s["pwd"], 2 * u + 2)
                gates(SG, u, "gate_b", KD)
                W.make_hi(act, SG + u + 2)
            for n in range(NS):
                W.make_hi(act, SO + n + 2)
                if n + 2 < NS:
                    y_hi(NP + n + 2)
            for n in range(KD):
                act.wait_ge(s["mx"], n + 1)
                nc.scalar.copy(hT[0][:, n, :], mixT[:, n, :]).then_inc(s["mh"], 1)
            for u in range(WO + 2, NEXT + 2):
                W.make_hi(act, u)
            for at, n in enumerate(NORMS):
                i = n % NT
                if n < NT:
                    act.wait_ge(s["cp"], NT + i + 1)
                else:
                    act.wait_ge(s["x"], i + 1)
                rms_root(nc, act, rms, at, mm_nat[:, i, :] if n < NT else h[:, i, :], sq, ssq[:, n:n + 1], rt[:, n:n + 1], eps)
            for i in range(NT):
                turned_hi(nc, act, s, i, banks, hT[0])

        @block.gpsimd
        def _(pool):
            for n in range(KD):
                pool.wait_ge(s["gm"], n + 1)
                nc.gpsimd.tensor_tensor(mixT[:, n, :], mixT[:, n, :], gs[:, n, :], ALU.add).then_inc(s["mx"], 1)
            for i in range(NT):
                pool.wait_ge(s["pn"], i + 1)
                nc.gpsimd.tensor_tensor(h[:, i, :], h[:, i, :], mm_nat[:, i, :], ALU.add).then_inc(s["x"], 1)

        @block.vector
        def _(dve):
            V = nc.vector

            def y_lo(r):
                dve.wait_ge(s["yh"], r + 1)
                V.tensor_tensor(yl[r % 2][:, :, :], pair(r), yh[r % 2][:, :, :].bitcast(F32), ALU.subtract).then_inc(s["yl"], 1)

            dve.wait_ge(s["mean"], 1)
            V.tensor_scalar(mu[:, :], banks[6], 1.0 / D, None, ALU.mult).then_inc(s["mu"], 1)
            dve.wait_ge(s["mu"], 1)
            for c in range(KD):
                V.tensor_tensor(mixT[:, c, :], mixT[:, c, :], mu[:, :], ALU.subtract).then_inc(s["xc"], 1)
            W.make_lo(dve, CG + 2)
            W.make_lo(dve, CG + 3)
            dve.wait_ge(s["rt"], 1)
            V.reciprocal(rtv[:, :], rtv[:, :]).then_inc(s["rstd"], 1)
            dve.wait_ge(s["rstd"], 1)
            dve.wait_ge(s["xc"], KD)
            for c in range(KD):
                V.tensor_tensor(mixT[:, c, :], mixT[:, c, :], rtv[:, :], ALU.mult).then_inc(s["nrm"], 1)
            y_lo(0)
            y_lo(1)
            W.make_lo(dve, CG + 4)
            W.make_lo(dve, CG + 5)
            for r in range(NP):
                W.make_lo(dve, PW + r + 2)
                y_lo(r + 2)
            for n in range(KD):
                dve.wait_ge(W.out, 2 * SG - 1 if n < KD // 2 else 2 * SG)
                V.scalar_tensor_tensor(mixT[:, n, :], banks[n], col("pw_b", n), gs[:, n, :], ALU.add, ALU.mult).then_inc(s["pwd"], 1)
            for u in range(4):
                W.make_lo(dve, SG + u + 2)
            for n in range(NS):
                W.make_lo(dve, SO + n + 2)
                if n + 2 < NS:
                    y_lo(NP + n + 2)
            for n in range(KD):
                dve.wait_ge(W.out, 2 * WO - 1 if n < KD // 2 else 2 * WO)
                V.tensor_tensor(gs[:, n, :], gs[:, n, :], banks[n], ALU.mult).then_inc(s["gm"], 1)
            for n in range(KD):
                dve.wait_ge(s["mh"], n + 1)
                V.tensor_tensor(hT[1][:, n, :], mixT[:, n, :], hT[0][:, n, :].bitcast(F32), ALU.subtract).then_inc(s["ml"], 1)
            for u in range(WO + 2, NEXT):
                W.make_lo(dve, u)
            dve.wait_ge(s["ml"], KD)
            for n in range(2):
                for i in range(NT):
                    dve.wait_ge(W.out, 2 * (WO + 2 * n + 1) + (1 if i < 2 else 2))
                    V.tensor_copy(mm_nat[:, i, 512 * n:512 * n + 512], banks[2 * i + n]).then_inc(s["cp"], 1)
                if n == 0:
                    W.make_lo(dve, NEXT)
            dve.wait_ge(s["gpo"], 16)
            dve.wait_ge(s["gpr"], 16)
            for at, n in enumerate(NORMS):
                i = n % NT
                rms_scale(nc, dve, rms, at, rt[:, n:n + 1], rs[:, n:n + 1])
                if n < NT:
                    V.scalar_tensor_tensor(mm_nat[:, i, :], mm_nat[:, i, :], rs[:, n:n + 1], gpo[:, :], ALU.mult,
                                           ALU.mult).then_inc(s["pn"], 1)
                    if at == 1:
                        W.make_lo(dve, NEXT + 1)
                else:
                    dve.wait_ge(s["x"], i + 1)
                    if i >= 2:
                        dve.wait_ge(s["tr"], 2 * (i - 1))
                    V.scalar_tensor_tensor(xn[i % 2], h[:, i, :], rs[:, n:n + 1], gpr[:, :], ALU.mult, ALU.mult).then_inc(s["xn"], 1)
                    if i >= 1:
                        turned_lo(nc, dve, s, i - 1, banks, *hT)
            turned_lo(nc, dve, s, NT - 1, banks, *hT)

        @block.tensor
        def _(pe):
            def gates(first, u):
                pe.wait_ge(*W.made(first + u))
                for j in range(2):
                    n = 2 * u + j
                    product(nc, pe, W, first + u, j, banks[n % 6 if first == CG else n], hT)

            def down(r, first, last_pair):
                u = unit_of(r)
                pe.wait_ge(*W.made(u))
                pe.wait_ge(s["yl"], r + 1)
                hi, lo = W.halves(u, 2)
                for c in range(KD):
                    for k in range(2):
                        last = split_mm(nc, banks[c], hi[:, k, c * P:c * P + P], lo[:, k, c * P:c * P + P], yh[r % 2][:, k, :],
                                        yl[r % 2][:, k, :], first and k == 0, last_pair and k == 1)
                    if c % 4 == 3:
                        last.then_inc(W.out, 1)

            for c in range(KD):
                last = nc.tensor.matmul(banks[6], ones[:, :], mixT[:, c, :], start=c == 0, stop=c == KD - 1)
            last.then_inc(s["mean"], 1)
            gates(CG, 0)
            gates(CG, 1)
            for c in range(KD):
                pe.wait_ge(s["sqd"], c + 1)
                nc.tensor.matmul(banks[7], ones[:, :], gs[:, 4 + c % 4, :], start=c == 0, stop=c == KD - 1).then_inc(s["vm"], 1)
            gates(CG, 2)
            pe.wait_ge(s["gate"], 2)
            gates(CG, 3)
            pe.wait_ge(s["gate"], KD)
            pe.wait_ge(s["rstd"], 1)
            for r in range(NP):
                down(r, r == 0, r == NP - 1)
            for u in range(4):
                pe.wait_ge(s["pwd"], 2 * u + 2)
                gates(SG, u)
            pe.wait_ge(s["gate"], 2 * KD)
            for n in range(NS):
                down(NP + n, n == 0, n == NS - 1)
            pe.wait_ge(s["gm"], KD)
            for n in range(2):
                for half in range(2):
                    pe.wait_ge(s["ml"], KD // 2 * (1 if n == half == 0 else 2))
                    u = WO + 2 * n + half
                    pe.wait_ge(*W.made(u))
                    hi, lo = W.halves(u, 4)
                    for i in range(NT):
                        t = slice(i * P, i * P + P)
                        for k in range(4):
                            kk = 4 * half + k
                            last = split_mm(nc, banks[2 * i + n], hT[0][:, kk, t], hT[1][:, kk, t], hi[:, k, :], lo[:, k, :],
                                            kk == 0, kk == KD - 1)
                        if i % 2:
                            last.then_inc(W.out, 1)
            pe.wait_ge(s["cp"], 2 * NT)
            for i in range(NT):
                turn_rows(nc, pe, s, i, xn[i % 2], banks, ident)
    g["clear"](s)


def ffn(nc, dram, g, sem, banks, W, hT, out):
    h, eps = g["h"], g["eps"]
    KH = HIDDEN // P
    GU, DN = g["unit"]["gate_up"], g["unit"]["down"]
    END = len(W.sources)
    out_t = out[0].rearrange("(i p) d -> p i d", p=P)
    s = {n: sem("g_" + n) for n in "gpo sg hd hi lo ssq sum rt rs pn x".split()}
    s_out = [sem(f"g_stored{i}") for i in range(2)]
    with ExitStack() as tmp:
        def sb(name, shape, dt=F32):
            return tmp.enter_context(nc.sbuf_tensor(name, shape, dt))

        hid = [sb(n, [P, KH, T], F32R) for n in ("hid_hi", "hid_lo")]
        sg, hd = g["mixed"][:, 0, 0:T], g["mixed"][:, 0, T:2 * T]
        gpo = g["mixed"][:, 1, :]
        fn = [g["mixed"][:, 2 + i, :] for i in range(2)]
        ssq = sb("ssq_g", [P, NT, 2])
        sums, rt, rs = (sb(n, [P, NT]) for n in ("sums_g", "rt_g", "rs_g"))
        block = tmp.enter_context(nc.Block())

        @block.sync
        def _(sp):
            for u in range(GU + 2, END):
                W.load(sp, u)
            for i in range(NT):
                sp.wait_ge(s["x"], i + 1)
                sp.dma_start(out_t[:, i, :], h[:, i, :]).then_inc(s_out[i % 2], 16)
            for x in s_out:
                sp.wait_ge(x, 16 * NT // 2)

        @block.scalar
        def _(act):
            act.dma_start(gpo, dram["ffn_post_g_2"][0].partition_broadcast(P)).then_inc(s["gpo"], 16)
            for c in range(KH):
                act.wait_ge(W.out, 2 * (GU + c) + 1)
                if c >= 1:
                    act.wait_ge(s["hd"], c)
                nc.scalar.activation(sg, banks[2 * c % 8], ACT.Silu).then_inc(s["sg"], 1)
                W.make_hi(act, GU + c + 2)
                act.wait_ge(s["hd"], c + 1)
                nc.scalar.copy(hid[0][:, c, :], hd).then_inc(s["hi"], 1)
            for u in range(DN + 2, END):
                W.make_hi(act, u)
            act.wait_ge(s["lo"], KH)
            for i in range(NT):
                act.wait_ge(W.out, 2 * END - 1 if i < 2 else 2 * END)
                for half in range(2):
                    if i or half:
                        act.wait_ge(s["ssq"], 2 * i + half)
                    nc.scalar.activation(hd, banks[2 * i + half], ACT.Square,
                                         accum_out=ssq[:, i, half:half + 1]).then_inc(s["ssq"], 1)
                act.wait_ge(s["sum"], i + 1)
                nc.scalar.activation(rt[:, i:i + 1], sums[:, i:i + 1], ACT.Sqrt, bias=eps[:, 0:1], scale=1.0 / D).then_inc(s["rt"], 1)

        @block.vector
        def _(dve):
            V = nc.vector
            for c in range(KH):
                dve.wait_ge(W.out, 2 * (GU + c) + 2)
                dve.wait_ge(s["sg"], c + 1)
                if c >= 1:
                    dve.wait_ge(s["lo"], c)
                V.tensor_tensor(hd, sg, banks[(2 * c + 1) % 8], ALU.mult).then_inc(s["hd"], 1)
                W.make_lo(dve, GU + c + 2)
                dve.wait_ge(s["hi"], c + 1)
                V.tensor_tensor(hid[1][:, c, :], hd, hid[0][:, c, :].bitcast(F32), ALU.subtract).then_inc(s["lo"], 1)
            for u in range(DN + 2, END):
                W.make_lo(dve, u)
            dve.wait_ge(s["gpo"], 16)
            for i in range(NT):
                dve.wait_ge(s["ssq"], 2 * i + 2)
                V.tensor_tensor(sums[:, i:i + 1], ssq[:, i, 0:1], ssq[:, i, 1:2], ALU.add).then_inc(s["sum"], 1)
                rms_scale(nc, dve, s, i, rt[:, i:i + 1], rs[:, i:i + 1])
                if i >= 2:
                    dve.wait_ge(s["x"], i - 1)
                for half in range(2):
                    c = slice(512 * half, 512 * half + 512)
                    V.scalar_tensor_tensor(fn[i % 2][:, c], banks[2 * i + half], rs[:, i:i + 1], gpo[:, c], ALU.mult,
                                           ALU.mult).then_inc(s["pn"], 1)
                dve.wait_ge(s["pn"], 2 * i + 2)
                V.tensor_tensor(h[:, i, :], h[:, i, :], fn[i % 2], ALU.add).then_inc(s["x"], 1)

        @block.tensor
        def _(pe):
            for c in range(KH):
                pe.wait_ge(*W.made(GU + c))
                if c >= 4:
                    pe.wait_ge(s["hd"], c - 3)
                for j in range(2):
                    product(nc, pe, W, GU + c, j, banks[(2 * c + j) % 8], hT)
            pe.wait_ge(s["lo"], KH)
            for n in range(KH // 2):
                u = DN + n
                pe.wait_ge(*W.made(u))
                hi, lo = W.halves(u, 2)
                for i in range(NT):
                    t = slice(i * P, i * P + P)
                    for half in range(2):
                        c = slice(512 * half, 512 * half + 512)
                        for k in range(2):
                            kk = 2 * n + k
                            last = split_mm(nc, banks[2 * i + half], hid[0][:, kk, t], hid[1][:, kk, t], hi[:, k, c], lo[:, k, c],
                                            kk == 0, kk == KH - 1)
                    if i % 2:
                        last.then_inc(W.out, 1)
    g["clear"](s, W.sems(), s_out)


def build(nc, dram, out):
    with ExitStack() as ctx:
        def sb(name, shape, dt=F32):
            return ctx.enter_context(nc.sbuf_tensor(name, shape, dt))

        def sem(name):
            return nc.alloc_semaphore(name)

        def clear(named, *lists):
            done = list(named.values()) + [x for group in lists for x in group]
            with nc.Block() as block:
                @block.gpsimd
                def _(pool):
                    for x in done:
                        pool.sem_clear(x)
            for x in done:
                if x not in g["gathers"]:
                    nc.release_semaphore(x)

        pall = ctx.enter_context(nc.psum_tensor("pall", [P, 8, BANK], F32))
        banks = [pall[:, b, :] for b in range(8)]
        g = {"h": sb("h", [P, NT, D]), "cols": sb("cols", [P, VEC_COLS]), "ident": sb("ident", [P, P]),
             "ones": sb("ones", [P, P]), "up": sb("up", [P, P]), "tri": sb("tri", [P, P]),
             "mixed": sb("mixed", [P, NT, D]), "eps": sb("eps", [P, 2]), "pall": pall}
        g["clear"] = clear
        g["gathers"] = []
        g["m_rows"] = nc.dram_tensor("m_rows", [T, D], F32, kind="Internal").ap()
        g["y_rows"] = nc.dram_tensor("y_rows", [2 * T, D], F32, kind="Internal").ap()
        g["acs_rows"] = nc.dram_tensor("acs_rows", [SSM_HEADS, T], F32, kind="Internal").ap()
        g["gate"] = [sb(f"gate{k}", [P, NT]) for k in range(2)]
        g["row_x"], g["row_y"] = sb("row_x", [P, NB], U32), sb("row_y", [P, NB], U32)
        g["over_e"] = sb("over_e", [P, OVER + 1], I32)
        stage_a(nc, dram, g, sem, banks)
        stage_b(nc, dram, g, sem, banks)
        stage_c(nc, dram, g, sem, banks, out)


_INS = ['x', 'meta_tokens', 'lb_logits', 'g_mix', 'w_in', 'sb_gain', 'hg_gain', 'w_out', 'g_ffn', 'w_router_group',
 'b_router_group', 'w_router_expert', 'b_router_expert', 'w_expert_gate', 'w_expert_up', 'w_expert_down', 'g_final',
 'mix_pre_g_2', 'w_in_2', 'gate_b_2', 'glu_b_2', 'conv_dw_w_2', 'conv_dw_b_2', 'conv_ln_g_2', 'conv_ln_b_2',
 'conv_pw_w_2', 'conv_pw_b_2', 'ssm_conv_w_2', 'ssm_conv_b_2', 'dt_bias_2', 'a_log_2', 'd_skip_2', 'ssm_norm_g_2',
 'ssm_out_w_2', 'w_out_2', 'mix_post_g_2', 'ffn_pre_g_2', 'w_gate_up_2', 'w_down_2', 'ffn_post_g_2']
_OUTS = [((1, 512, 1024), 'float32')]


def kernel(**inputs):
    import numpy as _np
    import concourse.bacc as _bacc
    from concourse import mybir as _mybir
    from concourse.bass_utils import run_bass_kernel_spmd as _run

    nc = _bacc.Bacc("TRN2", target_bir_lowering=False, num_devices=1)
    arrays, dram = {}, {}
    for name in _INS:
        a = _np.ascontiguousarray(inputs[name])
        arrays[f"in_{name}_dram"] = a
        dram[name] = nc.dram_tensor(f"in_{name}_dram", a.shape, _mybir.dt.from_np(a.dtype), kind="ExternalInput").ap()
    shape, dtype = _OUTS[0]
    out = nc.dram_tensor("out_0_dram", shape, _mybir.dt.from_np(_np.dtype(dtype)), kind="ExternalOutput").ap()
    build(nc, dram, out)
    r = _run(nc, [arrays], core_ids=[0])
    return r.results[0]["out_0_dram"]
```
